# Optimizing a Trainium2 kernel written in Bass

```python
import numpy as np
import jax
import jax.numpy as jnp
from jax import lax
import math

D_MODEL = 1024
BATCH = 1
SEQ = 256
DEPTH = 2

GRID_W = 64
CTX_LEN = 256
N_MIXERS = 2
N_HEADS = 16
HEAD_DIM = D_MODEL // N_HEADS
D_FF = 2816
CONV_WIDTH = 31
WIN_R = 8
WIN_C = 16
N_MOD = 9
N_CONV_LAYERS = (DEPTH + 1) // 2
N_NA_LAYERS = DEPTH // 2
RMS_EPS = 1e-6
LN_EPS = 1e-5
MASK_VALUE = -1e30


def _rmsnorm(x, g):
    xf = x.astype(jnp.float32)
    y = xf * lax.rsqrt(jnp.mean(xf * xf, axis=-1, keepdims=True) + RMS_EPS)
    return y.astype(x.dtype) * g

def _layernorm(x, g, b):
    xf = x.astype(jnp.float32)
    mu = jnp.mean(xf, axis=-1, keepdims=True)
    var = jnp.mean(jnp.square(xf - mu), axis=-1, keepdims=True)
    return ((xf - mu) * lax.rsqrt(var + LN_EPS)).astype(x.dtype) * g + b

def _modulate(h, shift, scale):
    return h * (1 + scale) + shift

def _swiglu(h, wg, wu, wd):
    return (jax.nn.silu(h @ wg) * (h @ wu)) @ wd

def _ffn_half(s, mod, g, wg, wu, wd):
    shift, scale, gate = mod
    h = _modulate(_rmsnorm(s, g), shift, scale)
    return s + 0.5 * gate * _swiglu(h, wg, wu, wd)

def _conv_module(h, w1, b1, wdw, bdw, lng, lnb, w2, b2):
    a, gt = jnp.split(h @ w1 + b1, 2, axis=-1)
    u = a * jax.nn.sigmoid(gt)
    u = lax.conv_general_dilated(
        u, wdw[:, None, :], window_strides=(1,),
        padding=[(CONV_WIDTH // 2, CONV_WIDTH // 2)],
        dimension_numbers=('NWC', 'WIO', 'NWC'),
        feature_group_count=u.shape[-1]) + bdw
    u = jax.nn.silu(_layernorm(u, lng, lnb))
    return u @ w2 + b2

def _col_window_tables():
    ncb = GRID_W // WIN_C
    span = 2 * WIN_C
    n = np.arange(ncb)
    blk_start = np.clip(n * WIN_C - WIN_C // 2, 0, GRID_W - span)
    key_cols = blk_start[:, None] + np.arange(span)[None, :]
    q_cols = n[:, None] * WIN_C + np.arange(WIN_C)[None, :]
    q_start = np.clip(q_cols - WIN_C // 2, 0, GRID_W - WIN_C)
    kc3 = key_cols[:, None, :]
    valid = (kc3 >= q_start[:, :, None]) & (kc3 < q_start[:, :, None] + WIN_C)
    rel = np.clip(kc3 - q_cols[:, :, None], -(WIN_C - 1), WIN_C - 1) + WIN_C - 1
    return key_cols.astype(np.int32), valid, rel.astype(np.int32)

def _neighbourhood_attention(q, k, v, kc, vc, rpb):
    B, T, H, Dh = q.shape
    rows = T // GRID_W
    wr = min(WIN_R, rows)
    key_cols, valid, rel_idx = _col_window_tables()
    ncb, span = key_cols.shape
    key_cols_j = jnp.asarray(key_cols)
    rel_idx_j = jnp.asarray(rel_idx)
    valid_j = jnp.asarray(valid)[None, None, :, :, None, :]
    rpb32 = rpb.astype(jnp.float32)
    qg = (q * (Dh ** -0.5)).reshape(B, rows, ncb, WIN_C, H, Dh).transpose(1, 0, 2, 3, 4, 5)
    kg = k.reshape(B, rows, GRID_W, H, Dh)
    vg = v.reshape(B, rows, GRID_W, H, Dh)

    def row_step(args):
        r, q_row = args
        r0 = jnp.clip(r - wr // 2, 0, rows - wr)
        k_band = lax.dynamic_slice_in_dim(kg, r0, wr, axis=1)
        v_band = lax.dynamic_slice_in_dim(vg, r0, wr, axis=1)
        k_blk = jnp.take(k_band, key_cols_j, axis=2)
        v_blk = jnp.take(v_band, key_cols_j, axis=2)
        s_lat = jnp.einsum('bnqhd,bjnmhd->bhnqjm', q_row, k_blk).astype(jnp.float32)
        rel_r = r0 + jnp.arange(wr) - r + WIN_R - 1
        bias = jnp.take(rpb32, rel_r, axis=1)
        bias = jnp.take(bias, rel_idx_j, axis=2).transpose(0, 2, 3, 1, 4)
        s_lat = jnp.where(valid_j, s_lat + bias, MASK_VALUE)
        s_ctx = jnp.einsum('bnqhd,bkhd->bhnqk', q_row, kc).astype(jnp.float32)
        s = jnp.concatenate([s_lat.reshape(B, H, ncb, WIN_C, wr * span), s_ctx], axis=-1)
        p = jax.nn.softmax(s, axis=-1).astype(v.dtype)
        p_lat = p[..., :wr * span].reshape(B, H, ncb, WIN_C, wr, span)
        p_ctx = p[..., wr * span:]
        return (jnp.einsum('bhnqjm,bjnmhd->bnqhd', p_lat, v_blk)
                + jnp.einsum('bhnqk,bkhd->bnqhd', p_ctx, vc))

    o = lax.map(row_step, (jnp.arange(rows), qg))
    return o.transpose(1, 0, 2, 3, 4, 5).reshape(B, T, H * Dh)

def _context_attention(qc, kc, vc):
    B, K, H, Dh = qc.shape
    s = jnp.einsum('bqhd,bkhd->bhqk', qc * (Dh ** -0.5), kc).astype(jnp.float32)
    p = jax.nn.softmax(s, axis=-1).astype(vc.dtype)
    return jnp.einsum('bhqk,bkhd->bqhd', p, vc).reshape(B, K, H * Dh)

def first_inputs(seed: int = 0) -> dict:
    key = jax.random.key(seed)
    ks = iter(jax.random.split(key, 32))

    def nrm(shape, scale):
        return jax.random.normal(next(ks), shape, jnp.float32) * scale

    D, F = D_MODEL, D_FF
    return {
        'x': nrm((BATCH, SEQ, D), 1.0),
        'c': nrm((BATCH, D), 1.0),
        'ctx': nrm((BATCH, CTX_LEN, D), 1.0),
        'c_ctx': nrm((D,), 1.0),
        'mod_w': nrm((DEPTH, D, N_MOD * D), 0.5 * D ** -0.5),
        'mod_b': nrm((DEPTH, N_MOD * D), 0.02),
        'norm_g': 1.0 + nrm((DEPTH, 3, D), 0.05),
        'ffn_w_gate': nrm((DEPTH, 2, D, F), D ** -0.5),
        'ffn_w_up': nrm((DEPTH, 2, D, F), D ** -0.5),
        'ffn_w_down': nrm((DEPTH, 2, F, D), F ** -0.5),
        'conv_w_pw1': nrm((N_CONV_LAYERS, D, 2 * D), D ** -0.5),
        'conv_b_pw1': nrm((N_CONV_LAYERS, 2 * D), 0.02),
        'conv_w_dw': nrm((N_CONV_LAYERS, CONV_WIDTH, D), CONV_WIDTH ** -0.5),
        'conv_b_dw': nrm((N_CONV_LAYERS, D), 0.02),
        'conv_ln_g': 1.0 + nrm((N_CONV_LAYERS, D), 0.05),
        'conv_ln_b': nrm((N_CONV_LAYERS, D), 0.02),
        'conv_w_pw2': nrm((N_CONV_LAYERS, D, D), D ** -0.5),
        'conv_b_pw2': nrm((N_CONV_LAYERS, D), 0.02),
        'na_w_qkv': nrm((N_NA_LAYERS, D, 3 * D), D ** -0.5),
        'na_b_qkv': nrm((N_NA_LAYERS, 3 * D), 0.02),
        'na_rpb': nrm((N_NA_LAYERS, N_HEADS, 2 * WIN_R - 1, 2 * WIN_C - 1), 0.1),
        'na_w_o': nrm((N_NA_LAYERS, D, D), D ** -0.5),
        'na_b_o': nrm((N_NA_LAYERS, D), 0.02),
        'final_g': 1.0 + nrm((D,), 0.05),
    }

def first_block(x, c, ctx, c_ctx, mod_w, mod_b, norm_g, ffn_w_gate, ffn_w_up, ffn_w_down,
              conv_w_pw1, conv_b_pw1, conv_w_dw, conv_b_dw, conv_ln_g, conv_ln_b, conv_w_pw2, conv_b_pw2,
              na_w_qkv, na_b_qkv, na_rpb, na_w_o, na_b_o, final_g):
    B, T, D = x.shape
    K = ctx.shape[1]
    xc = ctx
    for i in range(DEPTH):
        mixer = i % N_MIXERS
        j = i // N_MIXERS
        last = i == DEPTH - 1
        run_ctx = (not last) or mixer == 1
        ml = (jax.nn.silu(c) @ mod_w[i] + mod_b[i]).reshape(B, 1, N_MOD, D)
        mc = (jax.nn.silu(c_ctx) @ mod_w[i] + mod_b[i]).reshape(N_MOD, D)
        lat_m = [ml[:, :, n] for n in range(N_MOD)]
        ctx_m = [mc[n] for n in range(N_MOD)]

        x = _ffn_half(x, lat_m[0:3], norm_g[i, 0], ffn_w_gate[i, 0], ffn_w_up[i, 0], ffn_w_down[i, 0])
        if run_ctx:
            xc = _ffn_half(xc, ctx_m[0:3], norm_g[i, 0], ffn_w_gate[i, 0], ffn_w_up[i, 0], ffn_w_down[i, 0])

        h = _modulate(_rmsnorm(x, norm_g[i, 1]), lat_m[3], lat_m[4])
        if run_ctx:
            hc = _modulate(_rmsnorm(xc, norm_g[i, 1]), ctx_m[3], ctx_m[4])
        if mixer == 0:
            conv_p = (conv_w_pw1[j], conv_b_pw1[j], conv_w_dw[j], conv_b_dw[j],
                      conv_ln_g[j], conv_ln_b[j], conv_w_pw2[j], conv_b_pw2[j])
            y = _conv_module(h, *conv_p)
            if not last:
                yc = _conv_module(hc, *conv_p)
        else:
            qkv = (h @ na_w_qkv[j] + na_b_qkv[j]).reshape(B, T, 3, N_HEADS, HEAD_DIM)
            qkvc = (hc @ na_w_qkv[j] + na_b_qkv[j]).reshape(B, K, 3, N_HEADS, HEAD_DIM)
            kc, vc = qkvc[:, :, 1], qkvc[:, :, 2]
            o = _neighbourhood_attention(qkv[:, :, 0], qkv[:, :, 1], qkv[:, :, 2], kc, vc, na_rpb[j])
            y = o @ na_w_o[j] + na_b_o[j]
            if not last:
                yc = _context_attention(qkvc[:, :, 0], kc, vc) @ na_w_o[j] + na_b_o[j]
        x = x + lat_m[5] * y

        x = _ffn_half(x, lat_m[6:9], norm_g[i, 2], ffn_w_gate[i, 1], ffn_w_up[i, 1], ffn_w_down[i, 1])
        if not last:
            xc = xc + ctx_m[5] * yc
            xc = _ffn_half(xc, ctx_m[6:9], norm_g[i, 2], ffn_w_gate[i, 1], ffn_w_up[i, 1], ffn_w_down[i, 1])
    return _rmsnorm(x, final_g)


N_EVEN = (DEPTH + 1) // 2
N_ODD = DEPTH // 2
FFN_RES = 0.5
EPS = 1e-6
ROPE_BASE = 10000.0
Q_BLOCK = 128
NEG_INF = -1e30

MLA_HEADS = 8
MLA_Q_LORA = 256
MLA_KV_LORA = 128
MLA_NOPE = 64
MLA_ROPE = 32
MLA_V = 64
MLA_SCALE = (MLA_NOPE + MLA_ROPE) ** -0.5

SWA_HEADS = 8
SWA_KV_HEADS = 2
SWA_GROUP = SWA_HEADS // SWA_KV_HEADS
SWA_HEAD_DIM = 64
SWA_WINDOW = 128
SWA_SCALE = SWA_HEAD_DIM ** -0.5

ATTN_IN = MLA_Q_LORA + MLA_KV_LORA + MLA_ROPE + (SWA_HEADS + 2 * SWA_KV_HEADS) * SWA_HEAD_DIM
ATTN_OUT = MLA_HEADS * MLA_V + SWA_HEADS * SWA_HEAD_DIM

S5_WIDTH = D_MODEL
S5_GROUP = 16
S5_GROUPS = S5_WIDTH // S5_GROUP
S5_STATE = 64
S5_CHUNK = 128
S5_MAX_RE = -1e-4


def rmsnorm(x, g):
    xf = x.astype(jnp.float32)
    y = xf * lax.rsqrt(jnp.mean(xf * xf, axis=-1, keepdims=True) + EPS)
    return (y * g.astype(jnp.float32)).astype(x.dtype)

def modulate(h, g, shift, scale):
    return rmsnorm(h, g) * (1 + scale) + shift

def swiglu(h, w13, w2):
    gate, up = jnp.split(h @ w13, 2, axis=-1)
    return (jax.nn.silu(gate) * up) @ w2

def ffn_sublayer(h, m, j, g_pre, g_post, w13, w2):
    a = modulate(h, g_pre, m[3 * j], m[3 * j + 1])
    return h + FFN_RES * m[3 * j + 2] * rmsnorm(swiglu(a, w13, w2), g_post)

def axial_rope_table(rows, cols, d_rot):
    d_axis = d_rot // 2
    inv = ROPE_BASE ** (-jnp.arange(0, d_axis, 2, dtype=jnp.float32) / d_axis)
    ang = jnp.concatenate([rows.astype(jnp.float32)[:, None] * inv,
                           cols.astype(jnp.float32)[:, None] * inv], axis=-1)
    return jnp.cos(ang), jnp.sin(ang)

def apply_rope(x, table):
    cos, sin = table
    bshape = cos.shape[:1] + (1,) * (x.ndim - 3) + cos.shape[1:]
    cos = cos.reshape(bshape).astype(x.dtype)
    sin = sin.reshape(bshape).astype(x.dtype)
    x1, x2 = jnp.split(x, 2, axis=-1)
    return jnp.concatenate([x1 * cos - x2 * sin, x1 * sin + x2 * cos], axis=-1)

def to_blocks(t):
    b, s = t.shape[:2]
    return jnp.moveaxis(t.reshape((b, s // Q_BLOCK, Q_BLOCK) + t.shape[2:]), 1, 0)

def from_blocks(t):
    t = jnp.moveaxis(t, 0, 1)
    return t.reshape((t.shape[0], t.shape[1] * t.shape[2]) + t.shape[3:])

def softmax_attention(q, k, v, scale):
    s = jnp.einsum('bqhd,bkhd->bhqk', q, k, preferred_element_type=jnp.float32) * scale
    p = jax.nn.softmax(s, axis=-1).astype(v.dtype)
    return jnp.einsum('bhqk,bkhd->bqhd', p, v)

def sink_attention(q, k, v, sink, mask):
    s = jnp.einsum('bqkgd,bjkd->bkgqj', q, k, preferred_element_type=jnp.float32) * SWA_SCALE
    if mask is not None:
        s = jnp.where(mask, s, NEG_INF)
    sink_col = jnp.broadcast_to(sink.astype(jnp.float32)[None, :, :, None, None], s.shape[:-1] + (1,))
    p = jax.nn.softmax(jnp.concatenate([sink_col, s], axis=-1), axis=-1)[..., 1:]
    return jnp.einsum('bkgqj,bjkd->bqkgd', p.astype(v.dtype), v)

def attn_project(h, w_in, q_norm, w_uq, kv_norm, w_ukv, rope_a, rope_b):
    b, n = h.shape[:2]
    sizes = [MLA_Q_LORA, MLA_KV_LORA, MLA_ROPE, SWA_HEADS * SWA_HEAD_DIM, SWA_KV_HEADS * SWA_HEAD_DIM]
    cuts = [int(v) for v in np.cumsum(sizes)]
    cq, ckv, kpe, qs, ks, vs = jnp.split(h @ w_in, cuts, axis=-1)
    q = (rmsnorm(cq, q_norm) @ w_uq).reshape(b, n, MLA_HEADS, MLA_NOPE + MLA_ROPE)
    kv = (rmsnorm(ckv, kv_norm) @ w_ukv).reshape(b, n, MLA_HEADS, MLA_NOPE + MLA_V)
    q_nope, q_pe = q[..., :MLA_NOPE], q[..., MLA_NOPE:]
    k_nope, v_a = kv[..., :MLA_NOPE], kv[..., MLA_NOPE:]
    k_pe = kpe.reshape(b, n, 1, MLA_ROPE)
    q_s = qs.reshape(b, n, SWA_KV_HEADS, SWA_GROUP, SWA_HEAD_DIM)
    k_s = ks.reshape(b, n, SWA_KV_HEADS, SWA_HEAD_DIM)
    v_s = vs.reshape(b, n, SWA_KV_HEADS, SWA_HEAD_DIM)
    if rope_a is not None:
        q_pe = apply_rope(q_pe, rope_a)
        k_pe = apply_rope(k_pe, rope_a)
        q_s = apply_rope(q_s, rope_b)
        k_s = apply_rope(k_s, rope_b)
    q_a = jnp.concatenate([q_nope, q_pe], axis=-1)
    k_a = jnp.concatenate([k_nope, jnp.broadcast_to(k_pe, (b, n, MLA_HEADS, MLA_ROPE))], axis=-1)
    return q_a, k_a, v_a, q_s, k_s, v_s

def attn_mixer(h_ctx, h_lat, rope_a, rope_b, w_in, q_norm, w_uq, kv_norm, w_ukv, sink, w_out, ctx_out):
    qa_c, ka_c, va_c, qs_c, ks_c, vs_c = attn_project(h_ctx, w_in, q_norm, w_uq, kv_norm, w_ukv, None, None)
    qa_l, ka_l, va_l, qs_l, ks_l, vs_l = attn_project(h_lat, w_in, q_norm, w_uq, kv_norm, w_ukv, rope_a, rope_b)
    b, n = h_lat.shape[:2]
    n_ctx = h_ctx.shape[1]
    sink_kg = sink.reshape(SWA_KV_HEADS, SWA_GROUP)
    k_all = jnp.concatenate([ka_c, ka_l], axis=1)
    v_all = jnp.concatenate([va_c, va_l], axis=1)
    o_a = from_blocks(lax.map(lambda qb: softmax_attention(qb, k_all, v_all, MLA_SCALE), to_blocks(qa_l)))
    pad = ((0, 0), (SWA_WINDOW, SWA_WINDOW), (0, 0), (0, 0))
    k_pad = jnp.pad(ks_l, pad)
    v_pad = jnp.pad(vs_l, pad)
    span = Q_BLOCK + 2 * SWA_WINDOW

    def swa_block(args):
        i, qb = args
        start = i * Q_BLOCK
        k_loc = lax.dynamic_slice_in_dim(k_pad, start, span, axis=1)
        v_loc = lax.dynamic_slice_in_dim(v_pad, start, span, axis=1)
        q_pos = start + jnp.arange(Q_BLOCK)
        k_pos = start - SWA_WINDOW + jnp.arange(span)
        band = (jnp.abs(q_pos[:, None] - k_pos[None, :]) <= SWA_WINDOW) & (k_pos >= 0)[None, :] & (k_pos < n)[None, :]
        mask = jnp.concatenate([jnp.ones((Q_BLOCK, n_ctx), dtype=bool), band], axis=1)
        return sink_attention(qb, jnp.concatenate([ks_c, k_loc], axis=1),
                              jnp.concatenate([vs_c, v_loc], axis=1), sink_kg, mask)

    o_b = from_blocks(lax.map(swa_block, (jnp.arange(n // Q_BLOCK), to_blocks(qs_l))))
    y_lat = jnp.concatenate([o_a.reshape(b, n, -1), o_b.reshape(b, n, -1)], axis=-1) @ w_out
    y_ctx = None
    if ctx_out:
        o_a_c = softmax_attention(qa_c, ka_c, va_c, MLA_SCALE)
        o_b_c = sink_attention(qs_c, ks_c, vs_c, sink_kg, None)
        y_ctx = jnp.concatenate([o_a_c.reshape(b, n_ctx, -1), o_b_c.reshape(b, n_ctx, -1)], axis=-1) @ w_out
    return y_ctx, y_lat

def s5_discretise(lam_re, lam_im, b_re, b_im, log_step):
    lam_re = jnp.minimum(lam_re, S5_MAX_RE)
    dt = jnp.exp(log_step)[:, None]
    mag = jnp.exp(lam_re * dt)
    a_re = mag * jnp.cos(lam_im * dt)
    a_im = mag * jnp.sin(lam_im * dt)
    den = lam_re * lam_re + lam_im * lam_im
    f_re = ((a_re - 1.0) * lam_re + a_im * lam_im) / den
    f_im = (a_im * lam_re - (a_re - 1.0) * lam_im) / den
    bb_re = f_re[..., None] * b_re - f_im[..., None] * b_im
    bb_im = f_re[..., None] * b_im + f_im[..., None] * b_re
    return a_re, a_im, bb_re, bb_im

def complex_affine_combine(e1, e2):
    a1r, a1i, b1r, b1i = e1
    a2r, a2i, b2r, b2i = e2
    return (a2r * a1r - a2i * a1i, a2r * a1i + a2i * a1r,
            a2r * b1r - a2i * b1i + b2r, a2r * b1i + a2i * b1r + b2i)

def s5_scan(u, a_re, a_im, bb_re, bb_im, c_re, c_im, h_re, h_im, emit):
    b, n = u.shape[:2]
    chunks = jnp.moveaxis(u.reshape(b, n // S5_CHUNK, S5_CHUNK, S5_GROUPS, S5_GROUP), 1, 0)

    def step(carry, u_c):
        hr, hi = carry
        bu_re = jnp.einsum('blgh,gph->blgp', u_c, bb_re)
        bu_im = jnp.einsum('blgh,gph->blgp', u_c, bb_im)
        ar = jnp.broadcast_to(a_re, bu_re.shape)
        ai = jnp.broadcast_to(a_im, bu_re.shape)
        pa_re, pa_im, s_re, s_im = lax.associative_scan(complex_affine_combine, (ar, ai, bu_re, bu_im), axis=1)
        x_re = s_re + pa_re * hr[:, None] - pa_im * hi[:, None]
        x_im = s_im + pa_re * hi[:, None] + pa_im * hr[:, None]
        new = (x_re[:, -1], x_im[:, -1])
        if not emit:
            return new, None
        y = jnp.einsum('blgp,ghp->blgh', x_re, c_re) - jnp.einsum('blgp,ghp->blgh', x_im, c_im)
        return new, y

    h_end, ys = lax.scan(step, (h_re, h_im), chunks)
    y = jnp.moveaxis(ys, 0, 1).reshape(b, n, S5_WIDTH) if emit else None
    return y, h_end

def s5_mixer(h_ctx, h_lat, w_in, lam_re, lam_im, b_re, b_im, c_re, c_im, log_step, d_skip, w_glu, ctx_out):
    f32 = jnp.float32
    b = h_lat.shape[0]
    u_ctx = (h_ctx @ w_in).astype(f32)
    u_lat = (h_lat @ w_in).astype(f32)
    dsk = d_skip.astype(f32)
    y_lat = u_lat * dsk
    y_ctx = u_ctx * dsk if ctx_out else None
    for dr in range(2):
        a_re, a_im, bb_re, bb_im = s5_discretise(lam_re[dr].astype(f32), lam_im[dr].astype(f32),
                                                 b_re[dr].astype(f32), b_im[dr].astype(f32),
                                                 log_step[dr].astype(f32))
        cr = c_re[dr].astype(f32)
        ci = c_im[dr].astype(f32)
        uc = u_ctx.reshape(b, -1, S5_GROUPS, S5_GROUP)
        ul = u_lat.reshape(b, -1, S5_GROUPS, S5_GROUP)
        if dr == 1:
            uc, ul = uc[:, ::-1], ul[:, ::-1]
        zero = jnp.zeros((b, S5_GROUPS, S5_STATE), f32)
        yc, h_ctx_end = s5_scan(uc, a_re, a_im, bb_re, bb_im, cr, ci, zero, zero, ctx_out)
        yl, _ = s5_scan(ul, a_re, a_im, bb_re, bb_im, cr, ci, h_ctx_end[0], h_ctx_end[1], True)
        if dr == 1:
            yl = yl[:, ::-1]
            yc = yc[:, ::-1] if ctx_out else None
        y_lat = y_lat + yl
        if ctx_out:
            y_ctx = y_ctx + yc

    def glu_out(y):
        a, g = jnp.split(jax.nn.gelu(y).astype(h_lat.dtype) @ w_glu, 2, axis=-1)
        return a * jax.nn.sigmoid(g)

    return (glu_out(y_ctx) if ctx_out else None), glu_out(y_lat)

def second_inputs(seed: int = 0) -> dict:
    key = jax.random.key(seed)
    keys = iter(jax.random.split(key, 32))
    f32 = jnp.float32

    def nrm(shape, scale):
        return scale * jax.random.normal(next(keys), shape, f32)

    def gain(shape):
        return 1.0 + 0.01 * jax.random.normal(next(keys), shape, f32)

    G, P, H = S5_GROUPS, S5_STATE, S5_GROUP
    inp = {}
    inp['x'] = nrm((BATCH, SEQ, D_MODEL), 1.0)
    inp['c'] = nrm((BATCH, D_MODEL), 1.0)
    inp['ctx'] = nrm((BATCH, CTX_LEN, D_MODEL), 1.0)
    inp['c_ctx'] = nrm((D_MODEL,), 1.0)
    inp['mod_w'] = nrm((DEPTH, D_MODEL, N_MOD * D_MODEL), D_MODEL ** -0.5)
    inp['mod_b'] = nrm((DEPTH, N_MOD * D_MODEL), 0.01)
    inp['norm_pre'] = gain((DEPTH, 3, D_MODEL))
    inp['norm_post'] = gain((DEPTH, 3, D_MODEL))
    inp['ffn_w13'] = nrm((DEPTH, 2, D_MODEL, 2 * D_FF), D_MODEL ** -0.5)
    inp['ffn_w2'] = nrm((DEPTH, 2, D_FF, D_MODEL), D_FF ** -0.5)
    inp['attn_w_in'] = nrm((N_EVEN, D_MODEL, ATTN_IN), D_MODEL ** -0.5)
    inp['mla_q_norm'] = gain((N_EVEN, MLA_Q_LORA))
    inp['mla_w_uq'] = nrm((N_EVEN, MLA_Q_LORA, MLA_HEADS * (MLA_NOPE + MLA_ROPE)), MLA_Q_LORA ** -0.5)
    inp['mla_kv_norm'] = gain((N_EVEN, MLA_KV_LORA))
    inp['mla_w_ukv'] = nrm((N_EVEN, MLA_KV_LORA, MLA_HEADS * (MLA_NOPE + MLA_V)), MLA_KV_LORA ** -0.5)
    inp['swa_sink'] = nrm((N_EVEN, SWA_HEADS), 0.5)
    inp['attn_w_out'] = nrm((N_EVEN, ATTN_OUT, D_MODEL), ATTN_OUT ** -0.5)
    inp['s5_w_in'] = nrm((N_ODD, D_MODEL, S5_WIDTH), D_MODEL ** -0.5)
    inp['s5_lambda_re'] = -0.5 + nrm((N_ODD, 2, G, P), 0.01)
    inp['s5_lambda_im'] = np.pi * jnp.arange(P, dtype=f32) + nrm((N_ODD, 2, G, P), 0.01)
    inp['s5_b_re'] = nrm((N_ODD, 2, G, P, H), (2 * H) ** -0.5)
    inp['s5_b_im'] = nrm((N_ODD, 2, G, P, H), (2 * H) ** -0.5)
    inp['s5_c_re'] = nrm((N_ODD, 2, G, H, P), (2 * P) ** -0.5)
    inp['s5_c_im'] = nrm((N_ODD, 2, G, H, P), (2 * P) ** -0.5)
    inp['s5_log_step'] = jax.random.uniform(next(keys), (N_ODD, 2, G), f32, math.log(1e-3), math.log(1e-1))
    inp['s5_d'] = nrm((N_ODD, S5_WIDTH), 1.0)
    inp['s5_w_glu'] = nrm((N_ODD, S5_WIDTH, 2 * D_MODEL), S5_WIDTH ** -0.5)
    return inp

def second_block(x, c, ctx, c_ctx, mod_w, mod_b, norm_pre, norm_post, ffn_w13, ffn_w2,
              attn_w_in, mla_q_norm, mla_w_uq, mla_kv_norm, mla_w_ukv, swa_sink, attn_w_out,
              s5_w_in, s5_lambda_re, s5_lambda_im, s5_b_re, s5_b_im, s5_c_re, s5_c_im,
              s5_log_step, s5_d, s5_w_glu):
    b, n = x.shape[:2]
    ROWS = n // GRID_W
    rows = jnp.repeat(jnp.arange(ROWS), GRID_W)
    cols = jnp.tile(jnp.arange(GRID_W), ROWS)
    rope_a = axial_rope_table(rows, cols, MLA_ROPE)
    rope_b = axial_rope_table(rows, cols, SWA_HEAD_DIM)
    h_lat, h_ctx = x, ctx
    for l in range(DEPTH):
        last = l == DEPTH - 1
        m_lat = jnp.moveaxis((jax.nn.silu(c) @ mod_w[l] + mod_b[l]).reshape(b, N_MOD, 1, D_MODEL), 1, 0)
        m_ctx = (jax.nn.silu(c_ctx) @ mod_w[l] + mod_b[l]).reshape(N_MOD, 1, 1, D_MODEL)
        h_lat = ffn_sublayer(h_lat, m_lat, 0, norm_pre[l, 0], norm_post[l, 0], ffn_w13[l, 0], ffn_w2[l, 0])
        h_ctx = ffn_sublayer(h_ctx, m_ctx, 0, norm_pre[l, 0], norm_post[l, 0], ffn_w13[l, 0], ffn_w2[l, 0])
        a_lat = modulate(h_lat, norm_pre[l, 1], m_lat[3], m_lat[4])
        a_ctx = modulate(h_ctx, norm_pre[l, 1], m_ctx[3], m_ctx[4])
        if l % 2 == 0:
            e = l // 2
            y_ctx, y_lat = attn_mixer(a_ctx, a_lat, rope_a, rope_b, attn_w_in[e], mla_q_norm[e], mla_w_uq[e],
                                      mla_kv_norm[e], mla_w_ukv[e], swa_sink[e], attn_w_out[e], not last)
        else:
            o = l // 2
            y_ctx, y_lat = s5_mixer(a_ctx, a_lat, s5_w_in[o], s5_lambda_re[o], s5_lambda_im[o], s5_b_re[o],
                                    s5_b_im[o], s5_c_re[o], s5_c_im[o], s5_log_step[o], s5_d[o], s5_w_glu[o],
                                    not last)
        h_lat = h_lat + m_lat[5] * rmsnorm(y_lat, norm_post[l, 1])
        h_lat = ffn_sublayer(h_lat, m_lat, 2, norm_pre[l, 2], norm_post[l, 2], ffn_w13[l, 1], ffn_w2[l, 1])
        if not last:
            h_ctx = h_ctx + m_ctx[5] * rmsnorm(y_ctx, norm_post[l, 1])
            h_ctx = ffn_sublayer(h_ctx, m_ctx, 2, norm_pre[l, 2], norm_post[l, 2], ffn_w13[l, 1], ffn_w2[l, 1])
    return h_lat


def setup_inputs(seed=0):
    out = dict(first_inputs(seed))
    for name, value in second_inputs(seed + 1).items():
        if name != "x":
            out[name + "_2"] = value
    return out


def reference(
    x, c, ctx, c_ctx, mod_w, mod_b, norm_g, ffn_w_gate, ffn_w_up, ffn_w_down, conv_w_pw1,
    conv_b_pw1, conv_w_dw, conv_b_dw, conv_ln_g, conv_ln_b, conv_w_pw2, conv_b_pw2, na_w_qkv,
    na_b_qkv, na_rpb, na_w_o, na_b_o, final_g, c_2, ctx_2, c_ctx_2, mod_w_2, mod_b_2,
    norm_pre_2, norm_post_2, ffn_w13_2, ffn_w2_2, attn_w_in_2, mla_q_norm_2, mla_w_uq_2,
    mla_kv_norm_2, mla_w_ukv_2, swa_sink_2, attn_w_out_2, s5_w_in_2, s5_lambda_re_2,
    s5_lambda_im_2, s5_b_re_2, s5_b_im_2, s5_c_re_2, s5_c_im_2, s5_log_step_2, s5_d_2,
    s5_w_glu_2,
):
    x = first_block(
        x, c, ctx, c_ctx, mod_w, mod_b, norm_g, ffn_w_gate, ffn_w_up, ffn_w_down, conv_w_pw1,
        conv_b_pw1, conv_w_dw, conv_b_dw, conv_ln_g, conv_ln_b, conv_w_pw2, conv_b_pw2,
        na_w_qkv, na_b_qkv, na_rpb, na_w_o, na_b_o, final_g,
    )
    return second_block(
        x, c_2, ctx_2, c_ctx_2, mod_w_2, mod_b_2, norm_pre_2, norm_post_2, ffn_w13_2, ffn_w2_2,
        attn_w_in_2, mla_q_norm_2, mla_w_uq_2, mla_kv_norm_2, mla_w_ukv_2, swa_sink_2,
        attn_w_out_2, s5_w_in_2, s5_lambda_re_2, s5_lambda_im_2, s5_b_re_2, s5_b_im_2,
        s5_c_re_2, s5_c_im_2, s5_log_step_2, s5_d_2, s5_w_glu_2,
    )


_drawn_inputs = setup_inputs


def setup_inputs(seed=0):
    import zlib

    import numpy as np

    out = dict(_drawn_inputs(seed))
    spreads = {}
    factors = {'norm_g': 3.119,
     'conv_b_pw1': 8.0,
     'conv_b_dw': 7.161,
     'conv_ln_g': 5.093,
     'conv_ln_b': 8.0,
     'conv_b_pw2': 7.35,
     'na_b_qkv': 8.0,
     'na_rpb': 8.0,
     'na_b_o': 7.937,
     'mod_b_2': 2.831,
     'norm_pre_2': 6.587,
     'norm_post_2': 6.776,
     'mla_q_norm_2': 8.0,
     'mla_kv_norm_2': 8.0,
     'swa_sink_2': 8.0,
     's5_lambda_re_2': 64.0,
     's5_b_re_2': 2.888,
     's5_b_im_2': 2.897,
     's5_c_re_2': 2.915,
     's5_c_im_2': 2.864}
    for name, (base, spread) in spreads.items():
        noise = np.random.default_rng([zlib.crc32(name.encode()), seed]).standard_normal(out[name].shape)
        drawn = base * np.exp(spread * noise) if base else spread * noise
        out[name] = jnp.asarray(drawn.astype(out[name].dtype))
    for name, factor in factors.items():
        out[name] = (out[name] * factor).astype(out[name].dtype)
    return out
```

```python
from contextlib import ExitStack

import numpy as np

import concourse.bass as bass
from concourse import mybir

F32 = mybir.dt.float32
F32R = mybir.dt.float32r
ALU = mybir.AluOpType
ACT = mybir.ActivationFunctionType
AX = mybir.AxisListType

P = 128
D = 1024
DC = D // P
TOK = 256
T2 = 2 * TOK
F = 2816
FC = F // P
N_MOD = 9
MODC = N_MOD * DC
LAYERS = 4
TILE = DC * P
RAW = 4
SPLIT = 2
BANKS = 4
SUM_BANK, MOD_BANK, AUX0, AUX1 = 4, 5, 6, 7
DOWN_PARTS = (6, 6, 5, 5)
DOWN_AT = (0, 6, 12, 17)
MODS_AT_START = 28
RMS_EPS, LN_EPS = 1e-6, 1e-5
GROUPS, GROUP = 64, 16
SUB = 8
CHUNKS = T2 // SUB
COLS = GROUPS
TAPS = 31
PADW = TOK + TAPS - 1


def vector_columns():
    at, n = {}, 0

    def take(name, width):
        nonlocal n
        at[name] = (n, width)
        n += width

    take("mod_b", LAYERS * MODC * 2)
    for l in range(LAYERS):
        for s in range(3):
            take(f"g{l}{s}", DC * 2)
    for l in (2, 3):
        for s in range(3):
            take(f"gpost{l}{s}", DC * 2)
    take("c", 2 * DC * 2)
    take("b_pw1", 2 * DC)
    take("w_dw", DC * TAPS)
    for name in ("b_dw", "ln_g", "ln_b", "b_pw2"):
        take(name, DC)
    take("b_qkv", 3 * DC)
    take("b_o", DC)
    take("final_g", DC)
    take("q_norm", 2)
    take("kv_norm", 1)
    take("sink", 8)
    return at, n


VEC, NVEC = vector_columns()


class Tiles:

    def __init__(self, base, step=0):
        self.base, self.step = base, step

    def raw(self, b):
        return (self.base + b) % RAW

    def split(self, b):
        return (self.base + b) % SPLIT

    def loaded(self, b):
        return 16 * (self.step + (self.base + b) // RAW + 1)

    def count(self, b):
        return self.base + b + 4 * self.step


def build_plan(stop=None):
    counts = dict(tile=0, acc=0, sq=0, sums=0, rstd=0, scaled=0, affine=0, operand=0, silu=0, mods=0,
                  h=0, vecs=0, xnew=0, biased=0, unit=0)
    plan = []

    def add(kind, takes, **how):
        plan.append(dict(kind=kind, **how, **{f"{k}0": v for k, v in counts.items()}))
        for k, v in takes.items():
            counts[k] += v

    def norm(kind, n, fused=False, chunks=DC, **how):
        takes = dict(sq=chunks, sums=1, rstd=1, scaled=chunks)
        if kind in ("mod", "ln"):
            takes.update(affine=chunks, operand=chunks)
        if kind == "ln":
            takes["sums"] = 2
        if kind == "mod":
            takes["vecs"] = 1
        if kind in ("final", "post"):
            takes["xnew"] = chunks
        add("norm", takes, norm=kind, n=n, fused=fused, **how)

    def ffn(layer, half, n, mods, **how):
        add("pair", dict(tile=2 * FC, acc=2 * FC, silu=FC, mods=mods, h=FC), pair="ffn", n=n, pairs=FC,
            layer=layer, half=half, mods=mods)
        add("down", dict(tile=4 * DC, acc=DC), n=n, layer=layer, half=half, post=layer >= 2)
        if layer >= 2:
            norm("post", n, fused=True, layer=layer, site=2 * half)

    def finished(name):
        return stop is not None and name == stop

    def build():
        norm("mod", T2, layer=0, site=0)
        ffn(0, 0, T2, 44)
        if finished("ffn0"):
            return
        norm("mod", T2, fused=True, layer=0, site=1)
        add("pair", dict(tile=2 * DC, acc=2 * DC, silu=DC), pair="conv", n=T2, pairs=DC, mods=0)
        norm("ln", T2)
        add("dense", dict(tile=DC, acc=DC, biased=DC), dense="pw2", n=T2, outs=DC)
        if finished("conv"):
            return
        norm("mod", T2, fused=True, layer=0, site=2)
        ffn(0, 1, T2, 36)
        norm("mod", T2, fused=True, layer=1, site=0)
        ffn(1, 0, T2, 36)
        norm("mod", T2, fused=True, layer=1, site=1)
        add("dense", dict(tile=3 * DC, acc=3 * DC), dense="qkv", n=T2, outs=3 * DC)
        add("attention", dict(operand=DC, unit=32), which="na")
        add("dense", dict(tile=DC, acc=DC, biased=DC), dense="o", n=TOK, outs=DC)
        if finished("na"):
            return
        norm("mod", TOK, fused=True, layer=1, site=2)
        ffn(1, 1, TOK, 36)
        norm("final", TOK, fused=True)
        if finished("block1"):
            return
        norm("mod", T2, layer=2, site=0)
        ffn(2, 0, T2, 36)
        norm("mod", T2, layer=2, site=1)
        add("dense", dict(tile=10, acc=10), dense="win", n=T2, outs=10)
        add("attention", dict(operand=DC, unit=64), which="mix")
        add("dense", dict(tile=DC, acc=DC), dense="wout", n=T2, outs=DC)
        norm("post", T2, fused=True, layer=2, site=1)
        if finished("mix"):
            return
        norm("mod", T2, layer=2, site=2)
        ffn(2, 1, T2, 36)
        norm("mod", T2, layer=3, site=0)
        ffn(3, 0, T2, 36)
        norm("mod", T2, layer=3, site=1)
        if finished("pre5"):
            return
        add("dense", dict(tile=DC, acc=DC), dense="s5in", n=T2, outs=DC)
        add("s5", dict(operand=DC))
        add("pair", dict(tile=2 * DC, acc=2 * DC, silu=DC), pair="glu", n=TOK, pairs=DC, mods=0)
        norm("post", TOK, layer=3, site=1)
        if finished("s5mix"):
            return
        norm("mod", TOK, layer=3, site=2)
        ffn(3, 1, TOK, 0)

    build()
    return plan, counts


def build(nc, io, out, stop=None, dump=None):
    plan, totals = build_plan(stop)
    with ExitStack() as ctx:
        def sb(name, shape, dtype=F32, scope=ctx):
            return scope.enter_context(nc.sbuf_tensor(name, shape, dtype))

        def sem(name):
            return ctx.enter_context(nc.semaphore(name))

        X = sb("X", [P, DC, T2])
        y_scope = ExitStack()
        OVER = sb("OVER", [P, 2 * DC * T2], F32, y_scope)
        Y_ffn = OVER[:, 0:DC * T2].rearrange("p (c t) -> p c t", c=DC)
        y_scope.close()
        A_hi = sb("A_hi", [P, DC, T2], F32R)
        A_lo = sb("A_lo", [P, DC, T2], F32R)
        raw = sb("raw", [P, RAW, TILE])
        w_hi = sb("w_hi", [P, SPLIT, TILE], F32R)
        w_lo = sb("w_lo", [P, SPLIT, TILE], F32R)
        modw = sb("modw", [P, 2, TILE])
        V = sb("V", [P, NVEC])
        MOD = sb("MOD", [P, LAYERS * MODC * 2])
        silu_c = sb("silu_c", [P, 2, DC, 2])
        A_scale = sb("A_scale", [P, 2 * DC])
        GATE = sb("GATE", [P, 2 * DC])
        ones = sb("ones", [P, P])
        ident = sb("ident", [P, P])
        SQ = sb("SQ", [P, 2, T2])
        RST = sb("RST", [P, T2])
        SCL = sb("SCL", [P, 2, T2])
        AFF = sb("AFF", [P, 2, T2])

        ffn_scope = ExitStack()
        H_hi = sb("H_hi", [P, FC, T2], F32R, ffn_scope)
        H_lo = sb("H_lo", [P, FC, T2], F32R, ffn_scope)
        ffn_scope.close()
        conv_scope = ExitStack()
        U = sb("U", [P, DC, 2, PADW], F32, conv_scope)
        CO = sb("CO", [P, DC, T2], F32, conv_scope)
        MU = sb("MU", [P, T2], F32, conv_scope)
        conv_scope.close()
        na_scope = ExitStack()
        Q = sb("Q", [P, DC, TOK], F32, na_scope)
        K = sb("K", [P, DC, T2], F32, na_scope)
        VT = sb("VT", [P, DC, T2], F32, na_scope)
        VV = sb("VV", [P, 4, D], F32, na_scope)
        SS = sb("SS", [P, 2, T2 + 8], F32, na_scope)
        PX = sb("PX", [P, 2, T2 + 8], F32, na_scope)
        PT = sb("PT", [P, 2, T2], F32, na_scope)
        NB = sb("NB", [P, 2, TOK], F32, na_scope)
        ST = sb("ST", [P, 2, 4], F32, na_scope)
        na_scope.close()
        mix_scope = ExitStack()
        Q96 = sb("Q96", [96, 8, T2], F32, mix_scope)
        K96 = sb("K96", [96, 8, T2], F32, mix_scope)
        QS = sb("QS", [P, 4, T2], F32, mix_scope)
        KS = sb("KS", [P, T2], F32, mix_scope)
        VST = sb("VST", [P, T2], F32, mix_scope)
        VVa = sb("VVa", [P, 4, 512], F32, mix_scope)
        VVb = sb("VVb", [P, 4, P], F32, mix_scope)
        CQ = sb("CQ", [P, 2, T2], F32, mix_scope)
        CKV = sb("CKV", [P, T2], F32, mix_scope)
        KP = sb("KP", [P, T2], F32, mix_scope)
        WUQ = sb("WUQ", [P, 2, 768], F32, mix_scope)
        WUKV = sb("WUKV", [P, 1024], F32, mix_scope)
        ROT = sb("ROT", [P, 4, TOK], F32, mix_scope)
        TURN = sb("TURN", [P, 2, P], F32, mix_scope)
        BAND = sb("BAND", [P, 2, TOK], F32, mix_scope)
        SS2 = sb("SS2", [P, 2, T2 + 8], F32, mix_scope)
        PX2 = sb("PX2", [P, 2, T2 + 8], F32, mix_scope)
        PT2 = sb("PT2", [P, 2, T2], F32, mix_scope)
        ST2 = sb("ST2", [P, 2, 4], F32, mix_scope)
        mix_scope.close()
        s5_scope = ExitStack()
        UG = sb("UG", [P, GROUPS, CHUNKS], F32, s5_scope)
        SPAR = sb("SPAR", [P, 3, COLS], F32, s5_scope)
        BC = sb("BC", [P, 4, COLS, GROUP], F32, s5_scope)
        EP = sb("EP", [P, 4, COLS, SUB], F32, s5_scope)
        A8 = sb("A8", [P, 2, 2, COLS], F32, s5_scope)
        DSK = sb("DSK", [P, GROUPS], F32, s5_scope)
        MASK = sb("MASK", [P, 2, P], F32, s5_scope)
        WT = modw[:, :, 0:4 * P].rearrange("p j (x m) -> p j x m", x=4)
        DM = modw[:, 0, 4 * P:TILE].rearrange("p (g d m) -> p g d m", g=2, d=2)
        DD = modw[:, 1, 4 * P:TILE].rearrange("p (j g m) -> p j g m", j=2, g=2)
        SM = sb("SM", [P, 12, COLS], F32, s5_scope)
        early = ExitStack()
        UT = sb("UT", [P, DC, T2], F32, early)
        UTOK = sb("UTOK", [P, 4, D], F32, early)
        early.close()
        early2 = ExitStack()
        UGT = sb("UGT", [CHUNKS, GROUPS, SUB, GROUP], F32, early2)
        early2.close()
        late = ExitStack()
        YG = sb("YG", [P, GROUPS, CHUNKS // 2], F32, late)
        YS = sb("YS", [P, GROUPS, CHUNKS // 2], F32, late)
        late.close()
        S = sb("S", [P, CHUNKS, 2, COLS], F32, s5_scope)
        late2 = ExitStack()
        PW = sb("PW", [P, 4, SUB + 1, COLS], F32, late2)
        late2.close()
        late3 = ExitStack()
        YTOK = sb("YTOK", [P, 2, D], F32, late3)
        late3.close()
        TT = sb("TT", [P, CHUNKS // 2, 2, COLS], F32, s5_scope)
        s5_scope.close()
        EE = [OVER[:, i * 4096:(i + 1) * 4096].rearrange("p (d a g m) -> p d a g m", d=2, a=2, g=8) for i in range(2)]
        UCH = OVER[0:CHUNKS, :].rearrange("p (t d) -> p t d", t=SUB)
        YC = OVER[0:CHUNKS // 2, :].rearrange("p (t d) -> p t d", t=SUB)
        mixy_scope = ExitStack()
        Y_mix = sb("Y_mix", [P, DC, T2], F32, mixy_scope)
        mixy_scope.close()
        soft = {"na": (SS, PX, PT, ST), "mix": (SS2, PX2, PT2, ST2)}

        acc = ctx.enter_context(nc.psum_tensor("acc", [P, 8, T2], F32))

        raw_loaded = [sem(f"raw_loaded{i}") for i in range(RAW)]
        modw_loaded = [sem(f"modw_loaded{i}") for i in range(2)]
        x_loaded = sem("x_loaded")
        vec_loaded = sem("vec_loaded")
        ctx2_loaded = sem("ctx2_loaded")
        ones_set = sem("ones_set")
        silu_c_ready = sem("silu_c_ready")
        hi_ready = sem("hi_ready")
        lo_ready = sem("lo_ready")
        tile_done = sem("tile_done")
        evac = sem("evac")
        modw_used = sem("modw_used")
        vecs_ready = sem("vecs_ready")
        sq_ready = sem("sq_ready")
        sq_used = sem("sq_used")
        sum_ready = sem("sum_ready")
        recip_ready = sem("recip_ready")
        rstd_ready = sem("rstd_ready")
        centred = sem("centred")
        scaled = sem("scaled")
        affine = sem("affine")
        operand_ready = sem("operand_ready")
        xnew = sem("xnew")
        silu_ready = sem("silu_ready")
        h_ready = sem("h_ready")
        margins_set = sem("margins_set")
        dve_chain = sem("dve_chain")
        conv_done = sem("conv_done")
        biased = sem("biased")
        ident_loaded = sem("ident_loaded")
        s_scored = sem("s_scored")
        s_moved = sem("s_moved")
        nmax_ready = sem("nmax_ready")
        exp_ready = sem("exp_ready")
        p_ready = sem("p_ready")
        pt_ready = sem("pt_ready")
        pt_copied = sem("pt_copied")
        o_ready = sem("o_ready")
        vt_ready = sem("vt_ready")
        v_copied = sem("v_copied")
        bias_loaded = [sem(f"bias_loaded{i}") for i in range(2)]
        mix_loaded = sem("mix_loaded")
        lora_squared = sem("lora_squared")
        lora_summed = sem("lora_summed")
        lora_recip = sem("lora_recip")
        lora_rstd = sem("lora_rstd")
        lora_ready = sem("lora_ready")
        proj_ready = sem("proj_ready")
        proj_moved = sem("proj_moved")
        rot_ready = sem("rot_ready")
        rot_done = sem("rot_done")
        kpe_spread = sem("kpe_spread")
        stored = sem("stored")
        s5_loaded = sem("s5_loaded")
        dt_ready = sem("dt_ready")
        rates_ready = sem("rates_ready")
        mags_ready = sem("mags_ready")
        angles_ready = sem("angles_ready")
        sines_ready = sem("sines_ready")
        u_turned = sem("u_turned")
        u_copied = sem("u_copied")
        u_stored = sem("u_stored")
        uch_loaded = sem("uch_loaded")
        ug_turned = sem("ug_turned")
        ug_copied = sem("ug_copied")
        e_ready = sem("e_ready")
        w_turned = sem("w_turned")
        w_copied = sem("w_copied")
        s_summed = sem("s_summed")
        s_stored = sem("s_stored")
        scan_step = sem("scan_step")
        f_ready = sem("f_ready")
        d_summed = sem("d_summed")
        d_ready = sem("d_ready")
        y_taken = sem("y_taken")
        g_inner = sem("g_inner")
        g_tanh = sem("g_tanh")
        g_done = sem("g_done")
        yc_turned = sem("yc_turned")
        uch_sorted = sem("uch_sorted")
        y_pair_done = sem("y_pair_done")
        yc_copied = sem("yc_copied")
        y_stored = sem("y_stored")
        ytok_loaded = sem("ytok_loaded")
        y_turned = sem("y_turned")

        def vec(name, c=0, width=1):
            return V[:, bass.ds(VEC[name][0] + c, width)]

        tiled = [s for s in plan if s["tile0"] < totals["tile"] and s["kind"] in ("pair", "down", "dense")]

        def steps(eng, s, first, last, body):
            end = last - 1 if s is tiled[-1] else last
            if first < end:
                with eng.Fori(first, end) as i:
                    body(i)
            if end < last:
                body(last - 1)

        def source(s):
            if s["norm"] == "post":
                return Y_mix if s["site"] == 1 else Y_ffn
            return CO if s["norm"] == "ln" else X

        def attention_units(which):
            for h in range(16):
                pair, po = h // 2, 64 * (h % 2)
                for qt in range(2 if which == "na" else 4):
                    at = slice(qt * P, (qt + 1) * P)
                    k0 = TOK if qt >= 2 else 0
                    u = dict(h=h, qt=qt, pair=pair, po=po, k0=k0, bias=None, sink=None)
                    if which == "na":
                        u.update(q=Q[po:po + 64, pair, at], k=K[po:po + 64, pair, k0:T2], scale=64 ** -0.5,
                                 v=lambda k, h=h: VV[:, k, h * 64:(h + 1) * 64], bias="loaded")
                    elif h < 8:
                        u.update(q=Q96[0:96, h, at], k=K96[0:96, h, k0:T2], scale=96 ** -0.5,
                                 v=lambda k, h=h: VVa[:, k, h * 64:(h + 1) * 64])
                    else:
                        kv = (h - 8) // 4
                        rows = slice(64 * kv, 64 * kv + 64)
                        u.update(q=QS[rows, (h - 8) % 4, at], k=KS[rows, k0:T2], scale=64 ** -0.5,
                                 v=lambda k, kv=kv: VVb[:, k, kv * 64:(kv + 1) * 64],
                                 bias=None if qt >= 2 else BAND[:, qt, :], sink=h - 8)
                    yield u

        units = {w: list(attention_units(w)) for w in ("na", "mix")}

        def mix_moves():
            yield VVb[:], acc[:, 0, :].rearrange("p (k d) -> p k d", k=4)
            for h in range(8):
                yield Q96[:, h, :], acc[0:96, (1 + h) % 4, :]
            for h in range(8):
                yield K96[0:64, h, :], acc[0:64, (9 + h) % 4, :]
            for k in range(4):
                yield VVa[:, k, :], acc[:, (17 + k) % 4, :]

        def rotations():
            todo = [(KP[0:96, 0:TOK], 0, 96)] + [(Q96[:, h, 0:TOK], 0, 96) for h in range(8)]
            todo += [(QS[:, c, 0:TOK], 1, P) for c in range(4)] + [(KS[:, 0:TOK], 1, P)]
            for j, (x, which, rows) in enumerate(todo):
                yield x, which, j % 2, rows

        u_scratch = nc.dram_tensor("u_scratch", (T2, D), F32).ap()
        y_scratch = nc.dram_tensor("y_scratch", (TOK, D), F32).ap()

        block = ctx.enter_context(nc.Block())

        @block.sync
        def _(sp):
            sp.dma_start(V[:], io["vecs"]).then_inc(vec_loaded, 16)
            sp.dma_start(X[:], io["x"]).then_inc(x_loaded, 16)
            for j in range(MODS_AT_START):
                if j >= 2:
                    sp.wait_ge(modw_used, j + 1)
                sp.dma_start(modw[:, j % 2], io["mod_w"][j]).then_inc(modw_loaded[j % 2], 16)

            def load_tile(t, b, src, width=TILE):
                sp.wait_ge(lo_ready, t.count(b) + 1)
                sp.dma_start(raw[:, t.raw(b), 0:width], src).then_inc(raw_loaded[t.raw(b)], 16)

            def load_mod(j, slot):
                sp.wait_ge(modw_used, j + 1)
                sp.dma_start(modw[:, slot], io["mod_w"][j]).then_inc(modw_loaded[slot], 16)

            def pairs(s, first, second, i, mods):
                t = Tiles(s["tile0"], i)
                for b in range(4):
                    load_tile(t, b, (second if b % 2 else first)[2 * i + b // 2])
                    if mods:
                        load_mod(MODS_AT_START + s["mods0"] + 4 * i + b, b % 2)

            for s in plan:
                if s["kind"] == "pair":
                    if s["pair"] == "ffn":
                        first = io["ffn_gate"][s["layer"]][s["half"]]
                        second = io["ffn_up"][s["layer"]][s["half"]]
                    elif s["pair"] == "conv":
                        first, second = io["pw1_gate"], io["pw1_a"]
                    else:
                        first, second = io["glu_gate"], io["glu_a"]
                    with_mods = s["mods"] // 4
                    if with_mods:
                        with sp.Fori(0, with_mods) as i:
                            pairs(s, first, second, i, True)
                    if with_mods < s["pairs"] // 2:
                        with sp.Fori(with_mods, s["pairs"] // 2) as i:
                            pairs(s, first, second, i, False)
                if s["kind"] == "down":
                    w = io["ffn_down"][s["layer"]][s["half"]]
                    with sp.Fori(0, DC) as i:
                        for b in range(4):
                            at, width = DOWN_AT[b] * P, DOWN_PARTS[b] * P
                            load_tile(Tiles(s["tile0"], i), b, w[i, :, at:at + width], width)
                if s["kind"] == "dense":
                    w = io[s["dense"]]
                    with sp.Fori(0, s["outs"] // 4) as i:
                        for b in range(4):
                            load_tile(Tiles(s["tile0"], i), b, w[4 * i + b])
                    for o in range(s["outs"] // 4 * 4, s["outs"]):
                        load_tile(Tiles(s["tile0"]), o, w[o])

        @block.scalar
        def _(act):
            act.wait_ge(vec_loaded, 16)
            act.activation(silu_c[:], vec("c", 0, 4 * DC).rearrange("p (b c s) -> p b c s", b=2, c=DC),
                           ACT.Silu).then_inc(silu_c_ready, 1)

            def split_hi(t, b, width=TILE):
                if isinstance(t.step, int) and t.count(b) >= totals["tile"]:
                    return
                act.wait_ge(raw_loaded[t.raw(b)], t.loaded(b))
                act.wait_ge(tile_done, t.count(b) + 1)
                act.activation(w_hi[:, t.split(b), 0:width], raw[:, t.raw(b), 0:width], ACT.Copy).then_inc(hi_ready, 1)

            split_hi(Tiles(0), 0)

            def square(s, src, c, k, value):
                if value is not None:
                    act.wait_ge(evac, value)
                act.wait_ge(sq_used, k + 1)
                n = s["n"]
                act.activation(SQ[:, s["sqslot"], 0:n], src[:, c, 0:n], ACT.Square).then_inc(sq_ready, 1)

            def pair_body(s, i):
                t = Tiles(s["tile0"], i)
                for b in range(4):
                    split_hi(t, b + 1)
                    if b % 2 == 0:
                        f = s["silu0"] + 2 * i + b // 2
                        act.wait_ge(tile_done, t.count(b) + 1 + SPLIT)
                        gate = acc[:, (s["acc0"] + b) % BANKS, 0:s["n"]]
                        dst = SCL[:, b // 2, 0:s["n"]]
                        if s["pair"] == "ffn":
                            act.activation(dst, gate, ACT.Silu).then_inc(silu_ready, 1)
                        elif s["pair"] == "conv":
                            act.activation(dst, gate, ACT.Sigmoid, bias=vec("b_pw1", DC + 2 * i + b // 2)).then_inc(silu_ready, 1)
                        else:
                            act.activation(dst, gate, ACT.Sigmoid).then_inc(silu_ready, 1)

            def down_body(s, i):
                for o in range(2):
                    for b in range(4):
                        t = Tiles(s["tile0"] + 4 * o, 2 * i)
                        split_hi(t, b + 1, TILE if b == 3 else DOWN_PARTS[b + 1] * P)
                    square({**s, "sqslot": (s["sq0"] + o) % 2}, Y_ffn if s["post"] else X, 2 * i + o,
                           s["sq0"] + 2 * i + o, s["acc0"] + 2 * i + o + 1 + BANKS)

            def norm_stage(s):
                n = s["n"]
                src = source(s)
                if not s["fused"]:
                    if s["sq0"] == 0:
                        act.wait_ge(x_loaded, 16)
                    else:
                        s_wait(s)
                    for c in range(DC):
                        if s["norm"] == "ln":
                            act.wait_ge(centred, c + 1)
                        square({**s, "sqslot": (s["sq0"] + c) % 2}, src, c, s["sq0"] + c, None)
                act.wait_ge(recip_ready, s["rstd0"] + 1)
                act.activation(RST[:, 0:n], RST[:, 0:n], ACT.Sqrt).then_inc(rstd_ready, 1)
                if s["norm"] in ("mod", "ln"):
                    if s["norm"] == "mod":
                        act.wait_ge(vecs_ready, s["vecs0"] + 1)
                    for c in range(DC):
                        act.wait_ge(scaled, s["scaled0"] + c + 1)
                        if c >= 2:
                            act.wait_ge(operand_ready, s["operand0"] + c - 1)
                        if s["norm"] == "ln":
                            act.activation(AFF[:, c % 2, :], SCL[:, c % 2, :], ACT.Silu, scale=vec("ln_g", c),
                                           bias=vec("ln_b", c)).then_inc(affine, 1)
                            continue
                        shift = s["layer"] * MODC * 2 + (3 * s["site"]) * 2 * DC
                        for half in range(n // TOK):
                            at = slice(half * TOK, half * TOK + TOK)
                            mm = act.activation(AFF[:, c % 2, at], SCL[:, c % 2, at], ACT.Identity,
                                                scale=A_scale[:, 2 * c + half:2 * c + half + 1],
                                                bias=MOD[:, shift + 2 * c + half:shift + 2 * c + half + 1])
                        mm.then_inc(affine, 1)

            def s_wait(s):
                if s["norm"] == "ln":
                    pass
                elif s["norm"] == "post":
                    act.wait_ge(evac, s["acc0"] + BANKS)
                else:
                    act.wait_ge(xnew, s["xnew0"])
                    if s.get("layer") == 2 and s.get("site") == 0:
                        act.wait_ge(ctx2_loaded, 16)

            def dense_body(s, i, outs):
                t = Tiles(s["tile0"], i)
                for b in outs:
                    split_hi(t, b + 1)
                    if s["dense"] in ("pw2", "o", "wout"):
                        square({**s, "sqslot": (s["sq0"] + b) % 2}, Y_mix if s["dense"] == "wout" else X, 4 * i + b,
                               s["sq0"] + 4 * i + b, s["acc0"] + 4 * i + b + 1 + BANKS)

            def na_values():
                for c in range(DC):
                    act.wait_ge(vt_ready, c + 1)
                    act.activation(VV[:, :, c * P:(c + 1) * P],
                                   acc[:, AUX0 + c % 2, :].rearrange("p (k d) -> p k d", k=4), ACT.Copy).then_inc(v_copied, 1)

            def mix_projections(s):
                act.wait_ge(evac, s["acc0"] + BANKS)
                for dst, src in ((SCL[:, 0, :], CQ[:, 0, :]), (SCL[:, 1, :], CQ[:, 1, :]), (AFF[:, 0, :], CKV[:])):
                    act.activation(dst, src, ACT.Square).then_inc(lora_squared, 1)
                for i, r in enumerate((RST[:], AFF[:, 1, :])):
                    act.wait_ge(lora_recip, i + 1)
                    act.activation(r, r, ACT.Sqrt).then_inc(lora_rstd, 1)
                for j, (dst, src) in enumerate(mix_moves()):
                    act.wait_ge(proj_ready, j + 1)
                    act.activation(dst, src, ACT.Copy).then_inc(proj_moved, 1)
                act.wait_ge(rot_done, 1)
                for h in range(8):
                    act.activation(K96[64:96, h, :], KP[64:96, :], ACT.Copy).then_inc(kpe_spread, 1)

            def softmax_stage(s):
                SS, PX, PT, ST = soft[s["which"]]
                todo, u0 = units[s["which"]], s["unit0"]
                for u in range(len(todo) + 1):
                    if u < len(todo):
                        w, r = todo[u], u % 2
                        m = T2 - w["k0"] + (w["sink"] is not None)
                        act.wait_ge(nmax_ready, u0 + u + 1)
                        act.activation(PX[:, r, 0:m], SS[:, r, 0:m], ACT.Exp, bias=ST[:, r, 1:2],
                                       accum_out=ST[:, r, 2:3]).then_inc(exp_ready, 1)
                    if u >= 1:
                        m, r = T2 - todo[u - 1]["k0"], (u - 1) % 2
                        act.wait_ge(pt_ready, u0 + u)
                        if u >= 3:
                            act.wait_ge(o_ready, u0 + u - 2)
                        act.activation(PT[:, r, 0:m], acc[:, 2 + r, 0:m], ACT.Copy).then_inc(pt_copied, 1)

            def s5_stage(s):
                act.wait_ge(s5_loaded, 16 * 5)
                act.activation(SM[:, 0, :], SPAR[:, 2, :], ACT.Exp).then_inc(dt_ready, 1)
                act.wait_ge(rates_ready, 1)
                act.activation(SM[:, 3, :], SM[:, 2, :], ACT.Exp)
                act.activation(SM[:, 4, :], SM[:, 2, :], ACT.Exp, scale=-1.0).then_inc(mags_ready, 1)
                act.wait_ge(angles_ready, 1)
                act.activation(SM[:, 8:10, :], SM[:, 6:8, :], ACT.Sin).then_inc(sines_ready, 1)
                for c in range(DC):
                    act.wait_ge(u_turned, c + 1)
                    act.activation(UTOK[:, :, c * P:(c + 1) * P],
                                   acc[:, AUX0 + c % 2, :].rearrange("p (k d) -> p k d", k=4), ACT.Copy).then_inc(u_copied, 1)
                act.wait_ge(uch_loaded, 32)
                for b in range(8):
                    act.activation(UGT[:, 8 * b:8 * b + 8], UCH.rearrange("p t (g c) -> p g t c", c=GROUP)[:, 8 * b:8 * b + 8],
                                   ACT.Copy).then_inc(uch_sorted, 1)
                for b in range(8):
                    act.wait_ge(ug_turned, b + 1)
                    act.activation(UG[:, 8 * b:8 * b + 8, :],
                                   acc[:, AUX0 + b % 2, :].rearrange("p (g c) -> p g c", g=8), ACT.Copy).then_inc(ug_copied, 1)

                def store_states(j):
                    act.wait_ge(s_summed, j + 1)
                    half = CHUNKS // 2
                    src = acc[:, 2 + j % 2, 0:4 * CHUNKS].rearrange("p (d a c) -> p d a c", d=2, a=2)
                    for d, to, frm in ((0, slice(0, CHUNKS), slice(0, CHUNKS)),
                                       (1, slice(0, half), slice(half - 1, None, -1)),
                                       (1, slice(half, CHUNKS), slice(CHUNKS - 1, half - 1, -1))):
                        op = act.activation(S[:, to, :, 32 * d + j].rearrange("p c a -> p a c"), src[:, d, :, frm], ACT.Copy)
                    op.then_inc(s_stored, 1)

                for j in range(33):
                    if j < 32:
                        act.wait_ge(w_turned, j + 1)
                        if j >= 2:
                            act.wait_ge(s_summed, j - 1)
                        act.activation(WT[:, j % 2, :, :], acc[:, j % 2, :].rearrange("p (x m) -> p x m", x=4),
                                       ACT.Copy).then_inc(w_copied, 1)
                    if j >= 1:
                        store_states(j - 1)
                act.wait_ge(g_inner, 1)
                act.activation(YS[:], YS[:], ACT.Tanh, scale=float(np.sqrt(2 / np.pi))).then_inc(g_tanh, 1)
                for b in range(16):
                    act.wait_ge(yc_turned, b + 1)
                    act.activation(YC.rearrange("p t (g c) -> p g t c", c=GROUP)[:, 4 * b:4 * b + 4],
                                   acc[0:32, AUX0 + b % 2, :].rearrange("p (g t c) -> p g t c", g=4, t=SUB),
                                   ACT.Copy).then_inc(yc_copied, 1)

            for s in plan:
                if s["kind"] == "s5":
                    s5_stage(s)
                if s["kind"] == "norm":
                    norm_stage(s)
                elif s["kind"] == "pair":
                    steps(act, s, 0, s["pairs"] // 2, lambda i: pair_body(s, i))
                elif s["kind"] == "down":
                    steps(act, s, 0, DC // 2, lambda i: down_body(s, i))
                elif s["kind"] == "dense":
                    steps(act, s, 0, s["outs"] // 4, lambda i: dense_body(s, i, range(4)))
                    if s["outs"] % 4:
                        dense_body(s, s["outs"] // 4, range(s["outs"] % 4))
                elif s["kind"] == "attention":
                    if s["which"] == "na":
                        na_values()
                    else:
                        mix_projections(s)
                    softmax_stage(s)

        @block.gpsimd
        def _(pool):
            pool.memset(ones[:], 1.0).then_inc(ones_set, 1)
            pool.dma_start(ident[:], io["ident"]).then_inc(ident_loaded, 16)
            for s in plan:
                if s["kind"] == "norm":
                    n = s["n"]
                    src = source(s)
                    pool.wait_ge(rstd_ready, s["rstd0"] + 1)
                    for c in range(DC):
                        if c >= 2:
                            if s["norm"] in ("mod", "ln"):
                                pool.wait_ge(affine, s["affine0"] + c - 1)
                            else:
                                pool.wait_ge(xnew, s["xnew0"] + c - 1)
                        pool.tensor_tensor(SCL[:, c % 2, 0:n], src[:, c, 0:n], RST[:, 0:n], ALU.mult).then_inc(scaled, 1)
                    if s["norm"] == "mod" and s["layer"] == 0 and s["site"] == 1:
                        pool.memset(U[:, :, :, 0:TAPS // 2], 0.0)
                        pool.memset(U[:, :, :, PADW - TAPS // 2:PADW], 0.0).then_inc(margins_set, 1)
                if s["kind"] == "norm" and s["norm"] == "mod" and s["layer"] == 3 and s["site"] == 1:
                    for dst, name in ((SPAR, "s5_par"), (BC, "s5_bc"), (DSK, "s5_skip"), (MASK, "s5_mask"), (SM, "s5_zero")):
                        pool.dma_start(dst[:], io[name]).then_inc(s5_loaded, 16)
                if s["kind"] == "s5":
                    pool.wait_ge(u_copied, DC)
                    pool.dma_start(u_scratch.rearrange("(k p) d -> p k d", p=P), UTOK[:]).then_inc(u_stored, 16)
                    pool.wait_ge(u_stored, 16)
                    half = CHUNKS // 2
                    for rows, at in ((slice(0, half), slice(TOK, T2)), (slice(half, CHUNKS), slice(0, TOK))):
                        pool.dma_start(UCH[rows], u_scratch[at].rearrange("(c t) d -> c t d", t=SUB)).then_inc(uch_loaded, 16)
                    pool.wait_ge(yc_copied, 16)
                    pool.dma_start(y_scratch.rearrange("(c t) d -> c t d", t=SUB), YC[:]).then_inc(y_stored, 16)
                    pool.wait_ge(y_stored, 16)
                    pool.dma_start(YTOK[:], y_scratch.rearrange("(k p) d -> p k d", p=P)).then_inc(ytok_loaded, 16)
                if s["kind"] == "norm" and s["norm"] == "mod" and s["layer"] == 2 and s["site"] == 1:
                    for dst, name in ((WUQ, "w_uq"), (WUKV, "w_ukv"), (ROT, "rot"), (TURN, "turn"), (BAND, "band")):
                        pool.dma_start(dst[:], io[name]).then_inc(mix_loaded, 16)
                if s["kind"] == "attention" and s["which"] == "na":
                    for u, unit in enumerate(units["na"]):
                        if u < 2:
                            pool.wait_ge(evac, s["acc0"] + BANKS)
                        else:
                            pool.wait_ge(s_moved, u - 1)
                        pool.dma_start(NB[:, u % 2, :], io["na_bias"][unit["h"], unit["qt"]]).then_inc(bias_loaded[u % 2], 16)
                if s["kind"] == "norm" and s["norm"] == "mod" and s["layer"] == 1 and s["site"] == 1 and totals["tile"] > s["tile0"] + 160:
                    pool.wait_ge(affine, s["affine0"] + DC)
                    pool.dma_start(X[:, :, TOK:T2], io["ctx_2"]).then_inc(ctx2_loaded, 16)
            pool.wait_ge(evac, totals["acc"] + BANKS)
            if totals["xnew"]:
                pool.wait_ge(xnew, totals["xnew"])
            pool.dma_start(out, X[:, :, 0:TOK]).then_inc(stored, 16)
            pool.wait_ge(stored, 16)

        @block.vector
        def _(dve):
            chain = [0]

            def link(ins):
                chain[0] += 1
                ins.then_inc(dve_chain, 1)
                dve.wait_ge(dve_chain, chain[0])

            dve.sem_inc(lo_ready, RAW)
            dve.sem_inc(evac, BANKS)

            def split_lo(t, b, width=TILE):
                if isinstance(t.step, int) and t.count(b) >= totals["tile"]:
                    return
                dve.wait_ge(hi_ready, t.count(b) + 1)
                dve.tensor_tensor(w_lo[:, t.split(b), 0:width], raw[:, t.raw(b), 0:width],
                                  w_hi[:, t.split(b), 0:width].bitcast(F32), ALU.subtract).then_inc(lo_ready, 1)

            split_lo(Tiles(0), 0)
            dve.wait_ge(vec_loaded, 16)

            def take_mods(j0, n):
                dve.wait_ge(modw_used, 2 + j0 + n)
                link(dve.tensor_tensor(MOD[:, 2 * j0:2 * (j0 + n)], acc[:, MOD_BANK, 0:2 * n],
                                       V[:, VEC["mod_b"][0] + 2 * j0:VEC["mod_b"][0] + 2 * (j0 + n)], ALU.add))

            take_mods(0, MODS_AT_START)

            def pair_body(s, i):
                n = s["n"]
                t = Tiles(s["tile0"], i)
                for b in range(4):
                    split_lo(t, b + 1)
                    if b % 2 == 0:
                        continue
                    f = 2 * i + b // 2
                    dve.wait_ge(silu_ready, s["silu0"] + f + 1)
                    dve.wait_ge(tile_done, t.count(b) + 1 + SPLIT)
                    up = acc[:, (s["acc0"] + b) % BANKS, 0:n]
                    part = SCL[:, b // 2, 0:n]
                    if s["pair"] == "ffn":
                        dve.tensor_tensor(AFF[:, b // 2, 0:n], part, up, ALU.mult).then_inc(evac, 2)
                        dve.wait_ge(evac, s["acc0"] + 2 * f + 2 + BANKS)
                        dve.tensor_copy(H_hi[:, f, 0:n], AFF[:, b // 2, 0:n]).then_inc(h_ready, 1)
                        dve.wait_ge(h_ready, 2 * (s["h0"] + f) + 1)
                        dve.tensor_tensor(H_lo[:, f, 0:n], AFF[:, b // 2, 0:n], H_hi[:, f, 0:n].bitcast(F32),
                                          ALU.subtract).then_inc(h_ready, 1)
                    elif s["pair"] == "conv":
                        dve.scalar_tensor_tensor(
                            out=U[:, f, :, TAPS // 2:TAPS // 2 + TOK], in0=up.rearrange("p (s t) -> p s t", s=2),
                            scalar=vec("b_pw1", f), in1=part.rearrange("p (s t) -> p s t", s=2),
                            op0=ALU.add, op1=ALU.mult).then_inc(evac, 2)
                        dve.wait_ge(evac, s["acc0"] + 2 * f + 2 + BANKS)
                        dst = CO[:, f, :].rearrange("p (s t) -> p s t", s=2)
                        for tap in range(TAPS):
                            src = U[:, f, :, tap:tap + TOK]
                            w = vec("w_dw", f * TAPS + tap)
                            if tap == 0:
                                op = dve.tensor_scalar(dst, src, w, vec("b_dw", f), ALU.mult, ALU.add)
                            else:
                                op = dve.scalar_tensor_tensor(out=dst, in0=src, scalar=w, in1=dst,
                                                              op0=ALU.mult, op1=ALU.add)
                            if tap < TAPS - 1:
                                link(op)
                            else:
                                op.then_inc(conv_done, 1)
                    else:
                        dve.tensor_tensor(Y_mix[:, f, 0:n], up, part, ALU.mult).then_inc(evac, 2)

            def add_gated(dst_c, bank, n):
                for half in range(n // TOK):
                    at = slice(half * TOK, half * TOK + TOK)
                    yield dve.scalar_tensor_tensor(out=X[:, dst_c, at], in0=acc[:, bank, at],
                                                   scalar=GATE_col(dst_c, half), in1=X[:, dst_c, at],
                                                   op0=ALU.mult, op1=ALU.add)

            def GATE_col(c, half):
                return GATE[:, bass.ds(2 * c + half, 1)]

            def down_body(s, i):
                n = s["n"]
                for o in range(2):
                    t = Tiles(s["tile0"] + 4 * o, 2 * i)
                    for b in range(4):
                        split_lo(t, b + 1, TILE if b == 3 else DOWN_PARTS[b + 1] * P)
                    c = 2 * i + o
                    dve.wait_ge(tile_done, t.count(3) + 1 + SPLIT)
                    bank = (s["acc0"] + o) % 2
                    if s["post"]:
                        dve.tensor_copy(Y_ffn[:, c, 0:n], acc[:, bank, 0:n]).then_inc(evac, 1)
                    else:
                        *_, last = list(add_gated(c, bank, n))
                        last.then_inc(evac, 1)

            def norm_stage(s):
                n = s["n"]
                dve.wait_ge(evac, s["acc0"] + BANKS)
                if s["xnew0"]:
                    dve.wait_ge(xnew, s["xnew0"])
                if s["norm"] == "mod":
                    base = s["layer"] * MODC * 2 + 3 * s["site"] * 2 * DC
                    g = vec(f"g{s['layer']}{s['site']}", 0, 2 * DC)
                    dve.scalar_tensor_tensor(out=A_scale[:], in0=MOD[:, base + 2 * DC:base + 4 * DC], scalar=1.0,
                                             in1=g, op0=ALU.add, op1=ALU.mult).then_inc(vecs_ready, 1)
                    gate = MOD[:, base + 4 * DC:base + 6 * DC]
                    half = 1.0 if s["site"] == 1 else 0.5
                    if s["layer"] < 2:
                        link(dve.tensor_scalar(GATE[:], gate, half, None, ALU.mult))
                    else:
                        link(dve.scalar_tensor_tensor(out=GATE[:], in0=gate, scalar=half,
                                                      in1=vec(f"gpost{s['layer']}{s['site']}", 0, 2 * DC),
                                                      op0=ALU.mult, op1=ALU.mult))
                if s["norm"] == "ln":
                    dve.wait_ge(sum_ready, s["sums0"] + 1)
                    link(dve.tensor_scalar(MU[:, 0:n], acc[:, SUM_BANK, 0:n], 1.0 / D, None, ALU.mult))
                    for c in range(DC):
                        dve.tensor_tensor(CO[:, c, :], CO[:, c, :], MU[:], ALU.subtract).then_inc(centred, 1)
                dve.wait_ge(sum_ready, s["sums0"] + (2 if s["norm"] == "ln" else 1))
                eps = LN_EPS if s["norm"] == "ln" else RMS_EPS
                link(dve.tensor_scalar(RST[:, 0:n], acc[:, SUM_BANK, 0:n], 1.0 / D, eps, ALU.mult, ALU.add))
                dve.reciprocal(RST[:, 0:n], RST[:, 0:n]).then_inc(recip_ready, 1)
                for c in range(DC):
                    if s["norm"] in ("mod", "ln"):
                        dve.wait_ge(affine, s["affine0"] + c + 1)
                        link(dve.tensor_copy(A_hi[:, c, 0:n], AFF[:, c % 2, 0:n]))
                        dve.tensor_tensor(A_lo[:, c, 0:n], AFF[:, c % 2, 0:n], A_hi[:, c, 0:n].bitcast(F32),
                                          ALU.subtract).then_inc(operand_ready, 1)
                    elif s["norm"] == "final":
                        dve.wait_ge(scaled, s["scaled0"] + c + 1)
                        dve.tensor_scalar(X[:, c, 0:n], SCL[:, c % 2, 0:n], vec("final_g", c), None,
                                          ALU.mult).then_inc(xnew, 1)
                    else:
                        dve.wait_ge(scaled, s["scaled0"] + c + 1)
                        for half in range(n // TOK):
                            at = slice(half * TOK, half * TOK + TOK)
                            op = dve.scalar_tensor_tensor(out=X[:, c, at], in0=SCL[:, c % 2, at],
                                                          scalar=GATE[:, 2 * c + half:2 * c + half + 1],
                                                          in1=X[:, c, at], op0=ALU.mult, op1=ALU.add)
                        op.then_inc(xnew, 1)

            def dense_body(s, i, outs):
                n = s["n"]
                t = Tiles(s["tile0"], i)
                for b in outs:
                    split_lo(t, b + 1)
                    c = 4 * i + b
                    dve.wait_ge(tile_done, t.count(b) + 1 + SPLIT)
                    bank = (s["acc0"] + b) % BANKS
                    what = s["dense"]
                    if what in ("pw2", "o"):
                        bias = "b_pw2" if what == "pw2" else "b_o"
                        for half in range(n // TOK):
                            at = slice(half * TOK, half * TOK + TOK)
                            op = dve.tensor_scalar(AFF[:, b % 2, at], acc[:, bank, at], vec(bias, c), GATE_col(c, half),
                                                   ALU.add, ALU.mult)
                        op.then_inc(biased, 1)
                        dve.wait_ge(biased, s["biased0"] + 4 * i + b + 1)
                        dve.tensor_tensor(X[:, c, 0:n], X[:, c, 0:n], AFF[:, b % 2, 0:n], ALU.add).then_inc(evac, 1)
                    elif what == "qkv":
                        dst = (Q, K, VT)[i // 2]
                        m = TOK if i // 2 == 0 else T2
                        dve.tensor_scalar(dst[:, c % DC, 0:m], acc[:, bank, 0:m], vec("b_qkv", c), None,
                                          ALU.add).then_inc(evac, 1)
                    elif what == "s5in":
                        dve.tensor_copy(UT[:, c, :], acc[:, bank, :]).then_inc(evac, 1)
                    elif what == "win":
                        dst = (CQ[:, 0, :], CQ[:, 1, :], CKV[:], KP[:], QS[:, 0, :], QS[:, 1, :], QS[:, 2, :],
                               QS[:, 3, :], KS[:], VST[:])[c]
                        dve.tensor_copy(dst, acc[:, bank, :]).then_inc(evac, 1)
                    elif what == "wout":
                        dve.tensor_copy(Y_mix[:, c, 0:n], acc[:, bank, 0:n]).then_inc(evac, 1)

            def mix_norms(s):
                dve.wait_ge(evac, s["acc0"] + BANKS)
                for i, (r, bank, width) in enumerate(((RST[:], SUM_BANK, 2 * P), (AFF[:, 1, :], AUX0, P))):
                    dve.wait_ge(lora_summed, i + 1)
                    link(dve.tensor_scalar(r, acc[:, bank, :], 1.0 / width, RMS_EPS, ALU.mult, ALU.add))
                    dve.reciprocal(r, r).then_inc(lora_recip, 1)
                for i, (dst, g, r) in enumerate(((CQ[:, 0, :], vec("q_norm", 0), RST[:]), (CQ[:, 1, :], vec("q_norm", 1), RST[:]),
                                                 (CKV[:], vec("kv_norm"), AFF[:, 1, :]))):
                    dve.wait_ge(lora_rstd, 1 + i // 2)
                    dve.scalar_tensor_tensor(out=dst, in0=dst, scalar=g, in1=r, op0=ALU.mult, op1=ALU.mult).then_inc(lora_ready, 1)

            def mix_rotations():
                dve.wait_ge(mix_loaded, 16 * 5)
                for j, (x, which, bank, rows) in enumerate(rotations()):
                    dve.wait_ge(rot_ready, j + 1)
                    link(dve.tensor_tensor(AFF[0:rows, 0, 0:TOK], acc[0:rows, bank, 0:TOK], ROT[0:rows, 2 * which + 1, :], ALU.mult))
                    link(dve.tensor_tensor(x, x, ROT[0:rows, 2 * which, :], ALU.mult))
                    dve.tensor_tensor(x, x, AFF[0:rows, 0, 0:TOK], ALU.add).then_inc(rot_done, 1)
                    dve.wait_ge(rot_done, j + 1)

            def product(out_re, out_im, a, b, t1, t2, sign=1.0):
                link(dve.tensor_tensor(t1, a[0], b[0], ALU.mult))
                link(dve.tensor_tensor(t2, a[1], b[1], ALU.mult))
                link(dve.tensor_tensor(out_re, t1, t2, ALU.subtract))
                link(dve.tensor_tensor(t1, a[0], b[1], ALU.mult))
                link(dve.tensor_tensor(t2, a[1], b[0], ALU.mult))
                if sign > 0:
                    link(dve.tensor_tensor(out_im, t1, t2, ALU.add))
                else:
                    link(dve.scalar_tensor_tensor(out=out_im, in0=t1, scalar=-1.0, in1=t2, op0=ALU.mult, op1=ALU.subtract))

            def s5_discretise():
                dve.wait_ge(s5_loaded, 16 * 5)
                dt, lr, x, mag, inv, li, angle, lean, sine, cosine, den, spare = (SM[:, i, :] for i in range(12))
                link(dve.tensor_scalar(lr, SPAR[:, 0, :], -1e-4, None, ALU.min))
                dve.wait_ge(dt_ready, 1)
                dve.tensor_tensor(x, lr, dt, ALU.mult).then_inc(rates_ready, 1)
                li = SPAR[:, 1, :]
                link(dve.tensor_tensor(SM[:, 5, :], li, dt, ALU.mult))

                def reduce(dst, src, shift):
                    if shift:
                        link(dve.tensor_scalar(dst, src, shift, None, ALU.add))
                        src = dst
                    link(dve.tensor_scalar(spare, src, 1 / (2 * np.pi), 1.5 * 2.0 ** 23, ALU.mult, ALU.add))
                    link(dve.tensor_scalar(spare, spare, 1.5 * 2.0 ** 23, None, ALU.subtract))
                    for part in (6.28125, 0.0019350051879882812, 3.0199159819567e-07):
                        link(dve.scalar_tensor_tensor(out=dst, in0=spare, scalar=-part, in1=src, op0=ALU.mult, op1=ALU.add))
                        src = dst

                reduce(angle, SM[:, 5, :], 0.0)
                reduce(lean, angle, float(np.pi / 2))
                dve.tensor_scalar(SM[:, 6:8, :], SM[:, 6:8, :], 3.1415925, -3.1415925, ALU.min, ALU.max).then_inc(angles_ready, 1)
                dve.wait_ge(sines_ready, 1)
                dve.wait_ge(mags_ready, 1)
                link(dve.memset(PW[:, 0:4:2, 0, :], 1.0))
                link(dve.memset(PW[:, 1:4:2, 0, :], 0.0))
                link(dve.tensor_tensor(PW[:, 0, 1, :], mag, cosine, ALU.mult))
                link(dve.tensor_tensor(PW[:, 1, 1, :], mag, sine, ALU.mult))
                link(dve.tensor_tensor(PW[:, 2, 1, :], inv, cosine, ALU.mult))
                link(dve.scalar_tensor_tensor(out=PW[:, 3, 1, :], in0=inv, scalar=-1.0, in1=sine, op0=ALU.mult, op1=ALU.mult))
                t1, t2 = AFF[:].rearrange("p a b -> p (a b)"), SCL[:].rearrange("p a b -> p (a b)")
                for part in (0, 2):
                    for k, n in ((1, 1), (2, 2), (4, 4)):
                        at = slice(k + 1, k + n + 1)
                        one = [PW[:, part + i, 1:n + 1, :] for i in range(2)]
                        two = [PW[:, part + i, k:k + 1, :].broadcast_to([P, n, COLS]) for i in range(2)]
                        v1, v2 = (t[:, 0:n * COLS].rearrange("p (n c) -> p n c", n=n) for t in (t1, t2))
                        product(PW[:, part, at, :], PW[:, part + 1, at, :], one, two, v1, v2)
                link(dve.tensor_copy(A8[:, 0, 0, :], PW[:, 0, 8, :]))
                link(dve.tensor_copy(A8[:, 0, 1, :], PW[:, 0, 8, :]))
                link(dve.tensor_scalar(A8[:, 1, 0, :], PW[:, 1, 8, :], -1.0, None, ALU.mult))
                link(dve.tensor_copy(A8[:, 1, 1, :], PW[:, 1, 8, :]))
                for i in range(4):
                    link(dve.tensor_copy(EP[:, i, 0:32, :], PW[:, i, 7::-1, 0:32].rearrange("p t c -> p c t")))
                    link(dve.tensor_copy(EP[:, i, 32:64, :], PW[:, i, 0:8, 32:64].rearrange("p t c -> p c t")))
                a_re, a_im = PW[:, 0, 1, :], PW[:, 1, 1, :]
                f_re, f_im = SM[:, 6, :], SM[:, 7, :]
                nr, u1, u2 = SM[:, 8, :], SM[:, 9, :], SM[:, 11, :]
                link(dve.tensor_tensor(u1, lr, lr, ALU.mult))
                link(dve.tensor_tensor(u2, li, li, ALU.mult))
                link(dve.tensor_tensor(den, u1, u2, ALU.add))
                link(dve.reciprocal(den, den))
                link(dve.tensor_scalar(nr, a_re, -1.0, None, ALU.add))
                link(dve.tensor_tensor(u1, nr, lr, ALU.mult))
                link(dve.tensor_tensor(u2, a_im, li, ALU.mult))
                link(dve.tensor_tensor(f_re, u1, u2, ALU.add))
                link(dve.tensor_tensor(f_re, f_re, den, ALU.mult))
                link(dve.tensor_tensor(u1, a_im, lr, ALU.mult))
                link(dve.tensor_tensor(u2, nr, li, ALU.mult))
                link(dve.tensor_tensor(f_im, u1, u2, ALU.subtract))
                link(dve.tensor_tensor(f_im, f_im, den, ALU.mult))
                fs = [f.rearrange("p (c o) -> p c o", o=1).broadcast_to([P, COLS, GROUP]) for f in (f_re, f_im)]
                v1, v2 = (t.rearrange("p (c h) -> p c h", c=COLS) for t in (t1, t2))
                v3 = PW[:].rearrange("p a b c -> p (a b c)")[:, 0:COLS * GROUP].rearrange("p (c h) -> p c h", c=COLS)
                b_re, b_im = BC[:, 0], BC[:, 1]
                link(dve.tensor_tensor(v1, b_re, fs[0], ALU.mult))
                link(dve.tensor_tensor(v2, b_im, fs[1], ALU.mult))
                link(dve.tensor_tensor(v3, b_re, fs[1], ALU.mult))
                link(dve.tensor_tensor(b_re, v1, v2, ALU.subtract))
                link(dve.tensor_tensor(v2, b_im, fs[0], ALU.mult))
                link(dve.tensor_tensor(b_im, v3, v2, ALU.add))

            def s5_spread(dst, q, powers, what, sign, done):
                t1, t2 = (t[:].rearrange("p a b -> p (a b)").rearrange("p (g t c) -> p g t c", g=8, t=SUB) for t in (AFF, SCL))
                for d in range(2):
                    cols = slice(32 * d + 8 * q, 32 * d + 8 * q + 8)
                    a = [EP[:, powers + i, cols, :].rearrange("p g (t o) -> p g t o", o=1).broadcast_to([P, 8, SUB, GROUP]) for i in range(2)]
                    b = [BC[:, what + i, cols, :].rearrange("p g (o c) -> p g o c", o=1).broadcast_to([P, 8, SUB, GROUP]) for i in range(2)]
                    o = [dst[:, d, i].rearrange("p g (t c) -> p g t c", t=SUB) for i in range(2)]
                    link(dve.tensor_tensor(t1, a[0], b[0], ALU.mult))
                    link(dve.tensor_tensor(t2, a[1], b[1], ALU.mult))
                    link(dve.tensor_tensor(o[0], t1, t2, ALU.subtract))
                    link(dve.tensor_tensor(t1, a[0], b[1], ALU.mult))
                    link(dve.tensor_tensor(t2, a[1], b[0], ALU.mult))
                    link(dve.tensor_tensor(o[1], t1, t2, ALU.add))
                    if sign < 0:
                        link(dve.tensor_scalar(o[1], o[1], -1.0, None, ALU.mult))
                dve.sem_inc(done, 1)

            def s5_stage(s):
                dve.wait_ge(evac, s["acc0"] + BANKS)
                s5_discretise()
                dve.wait_ge(ug_copied, 8)
                for q in range(4):
                    if q >= 2:
                        dve.wait_ge(w_turned, 8 * (q - 1))
                    s5_spread(EE[q % 2], q, 0, 0, 1, e_ready)
                dve.wait_ge(s_stored, 32)
                M1, M2 = (SM[:, 2 * i:2 * i + 2, :] for i in range(2))

                def scan_body(k, at):
                    dve.tensor_tensor(M1, S[:, k - 1], A8[:, 0], ALU.mult).then_inc(scan_step, 1)
                    dve.tensor_tensor(M2[:, 0], S[:, k - 1, 1], A8[:, 1, 0], ALU.mult).then_inc(scan_step, 1)
                    dve.tensor_tensor(M2[:, 1], S[:, k - 1, 0], A8[:, 1, 1], ALU.mult).then_inc(scan_step, 1)
                    dve.wait_ge(scan_step, 5 * k - 2)
                    dve.tensor_tensor(TT[:, at], M1, M2, ALU.add).then_inc(scan_step, 1)
                    dve.wait_ge(scan_step, 5 * k - 1)
                    dve.tensor_tensor(S[:, k], S[:, k], TT[:, at], ALU.add).then_inc(scan_step, 1)
                    dve.wait_ge(scan_step, 5 * k)

                half = CHUNKS // 2
                with dve.Fori(1, half) as k:
                    scan_body(k, 0)
                with dve.Fori(half, CHUNKS) as k:
                    scan_body(k, k - half)
                for q in range(4):
                    if q >= 1:
                        dve.wait_ge(y_pair_done, 8 * q)
                    s5_spread(EE[0], q, 0, 0, 1, f_ready)
                    s5_spread(EE[1], q, 2, 2, -1, f_ready)
                    for i in range(8):
                        j = 8 * q + i
                        dve.wait_ge(d_summed, j + 1)
                        if j:
                            dve.wait_ge(d_ready, j)
                        link(dve.tensor_tensor(DM.rearrange("p g d m -> p g (d m)"),
                                               acc[:, (0, AUX0)[j % 2]:(0, AUX0)[j % 2] + 2, 0:2 * P],
                                               MASK[:].rearrange("p (o d) m -> p o (d m)", o=1).broadcast_to([P, 2, 2 * P]), ALU.mult))
                        if j >= 2:
                            dve.wait_ge(y_pair_done, j - 1)
                        dve.tensor_tensor(DD[:, j % 2], DM[:, :, 0, :], DM[:, :, 1, :], ALU.add).then_inc(d_ready, 1)
                    dve.wait_ge(y_pair_done, 8 * q + 8)
                    at = slice(16 * q, 16 * q + 16)
                    skip = DSK[:, at].rearrange("p (g o) -> p g o", o=1).broadcast_to([P, 16, half])
                    link(dve.tensor_tensor(YS[:, at], UG[:, at, half:CHUNKS], skip, ALU.mult))
                    for g2 in range(2):
                        at = slice(16 * q + g2, 16 * q + 16, 2)
                        dve.tensor_tensor(YG[:, at], acc[:, 2 + 2 * (q % 2) + g2, 0:TOK].rearrange("p (g c) -> p g c", g=8),
                                          YS[:, at], ALU.add).then_inc(y_taken, 1)
                dve.wait_ge(y_taken, 8)
                link(dve.tensor_tensor(YS[:], YG[:], YG[:], ALU.mult))
                link(dve.tensor_scalar(YS[:], YS[:], 0.044715, 1.0, ALU.mult, ALU.add))
                dve.tensor_tensor(YS[:], YS[:], YG[:], ALU.mult).then_inc(g_inner, 1)
                dve.wait_ge(g_tanh, 1)
                link(dve.tensor_scalar(YS[:], YS[:], 1.0, 0.5, ALU.add, ALU.mult))
                dve.tensor_tensor(YG[:], YG[:], YS[:], ALU.mult).then_inc(g_done, 1)
                for c in range(DC):
                    dve.wait_ge(y_turned, c + 1)
                    src = acc[:, c % 2, 0:TOK]
                    link(dve.tensor_copy(A_hi[:, c, 0:TOK], src))
                    dve.tensor_tensor(A_lo[:, c, 0:TOK], src, A_hi[:, c, 0:TOK].bitcast(F32),
                                      ALU.subtract).then_inc(operand_ready, 1)

            def softmax_stage(s):
                SS, PX, PT, ST = soft[s["which"]]
                todo, u0 = units[s["which"]], s["unit0"]
                per = len(todo) // DC
                for u in range(len(todo) + 1):
                    if u < len(todo):
                        w, r = todo[u], u % 2
                        m = T2 - w["k0"]
                        dve.wait_ge(s_scored, u0 + u + 1)
                        if u >= 2:
                            dve.wait_ge(exp_ready, u0 + u - 1)
                        if w["bias"] is None:
                            op = dve.tensor_scalar(SS[:, r, 0:m], acc[:, r, 0:m], w["scale"], None, ALU.mult)
                        else:
                            if w["bias"] == "loaded":
                                dve.wait_ge(bias_loaded[r], 16 * (u // 2 + 1))
                                bias = NB[:, r, :]
                            else:
                                bias = w["bias"]
                            dve.scalar_tensor_tensor(out=SS[:, r, 0:TOK], in0=acc[:, r, 0:TOK], scalar=w["scale"],
                                                     in1=bias, op0=ALU.mult, op1=ALU.add)
                            op = dve.tensor_scalar(SS[:, r, TOK:T2], acc[:, r, TOK:T2], w["scale"], None, ALU.mult)
                        op.then_inc(s_moved, 1)
                        if w["sink"] is not None:
                            link(dve.tensor_copy(SS[:, r, m:m + 1], vec("sink", w["sink"])))
                            m += 1
                        dve.wait_ge(s_moved, u0 + u + 1)
                        link(dve.tensor_reduce(ST[:, r, 0:1], SS[:, r, 0:m], AX.X, ALU.max))
                        dve.tensor_scalar(ST[:, r, 1:2], ST[:, r, 0:1], -1.0, None, ALU.mult).then_inc(nmax_ready, 1)
                    if u >= 1:
                        v, r = u - 1, (u - 1) % 2
                        m = T2 - todo[v]["k0"]
                        dve.wait_ge(exp_ready, u0 + v + 1)
                        link(dve.reciprocal(ST[:, r, 3:4], ST[:, r, 2:3]))
                        dve.tensor_scalar(PX[:, r, 0:m], PX[:, r, 0:m], ST[:, r, 3:4], None, ALU.mult).then_inc(p_ready, 1)
                        dve.wait_ge(p_ready, u0 + v + 1)
                    if u >= per + 2 and (u - 2) % per == 0 or u == len(todo):
                        pair = (u - per - 2) // per if u < len(todo) else DC - 1
                        n = per // 2 * P
                        dve.wait_ge(o_ready, u0 + per * (pair + 1))
                        src = acc[:, AUX0 + pair % 2, 0:n]
                        link(dve.tensor_copy(A_hi[:, pair, 0:n], src))
                        dve.tensor_tensor(A_lo[:, pair, 0:n], src, A_hi[:, pair, 0:n].bitcast(F32),
                                          ALU.subtract).then_inc(operand_ready, 1)

            for s in plan:
                if s["kind"] == "s5":
                    s5_stage(s)
                if s["kind"] == "norm":
                    norm_stage(s)
                elif s["kind"] == "pair":
                    if s["pair"] == "conv":
                        dve.wait_ge(margins_set, 1)
                        for i in range(s["pairs"] // 2):
                            pair_body(s, i)
                    else:
                        steps(dve, s, 0, s["pairs"] // 2, lambda i: pair_body(s, i))
                    if s["mods"]:
                        take_mods(MODS_AT_START + s["mods0"], s["mods"])
                elif s["kind"] == "down":
                    steps(dve, s, 0, DC // 2, lambda i: down_body(s, i))
                elif s["kind"] == "dense":
                    if s["dense"] in ("pw2", "o", "wout"):
                        steps(dve, s, 0, s["outs"] // 4, lambda i: dense_body(s, i, range(4)))
                    else:
                        for i in range(s["outs"] // 4):
                            dense_body(s, i, range(4))
                        if s["outs"] % 4:
                            dense_body(s, s["outs"] // 4, range(s["outs"] % 4))
                elif s["kind"] == "attention":
                    if s["which"] == "mix":
                        mix_norms(s)
                        mix_rotations()
                    softmax_stage(s)

        @block.tensor
        def _(pe):
            pe.sem_inc(tile_done, SPLIT)
            pe.sem_inc(sq_used, 2)
            pe.sem_inc(modw_used, 2)

            def mod_chunk(j, col, slot, value, blk):
                pe.wait_ge(modw_loaded[slot], value)
                for k in range(DC):
                    mm = pe.matmul(acc[:, MOD_BANK, bass.ds(col, 2)], modw[:, slot, k * P:(k + 1) * P],
                                   silu_c[:, blk, k, :], start=(k == 0), stop=(k == DC - 1))
                mm.then_inc(modw_used, 1)
                return mm

            pe.wait_ge(silu_c_ready, 1)
            for j in range(MODS_AT_START):
                mod_chunk(j, 2 * j, j % 2, 16 * (j // 2 + 1), 0)

            def products(t, b, hi, lo, n, blocks, bank, first, last, waits=None):
                pe.wait_ge(lo_ready, t.count(b) + 1 + RAW)
                slot = t.split(b)
                for x, k in enumerate(blocks):
                    if waits is not None and waits(k) is not None:
                        pe.wait_ge(*waits(k))
                    wh, wl = (w[:, slot, x * P:(x + 1) * P] for w in (w_hi, w_lo))
                    dst = acc[:, bank, 0:n]
                    pe.matmul(dst, wh, hi[:, k, 0:n], start=(first and x == 0), stop=False)
                    pe.matmul(dst, wh, lo[:, k, 0:n], start=False, stop=False)
                    mm = pe.matmul(dst, wl, hi[:, k, 0:n], start=False, stop=(last and x == len(blocks) - 1))
                mm.then_inc(tile_done, 1)

            def operand_wait(s):
                return lambda k: (operand_ready, s["operand0"] + k + 1 - DC)

            def pair_body(s, i, mods):
                t = Tiles(s["tile0"], i)
                for b in range(4):
                    pe.wait_ge(evac, s["acc0"] + 4 * i + b + 1)
                    products(t, b, A_hi, A_lo, s["n"], range(DC), (s["acc0"] + b) % BANKS, True, True,
                             operand_wait(s) if b == 0 else None)
                    if mods:
                        j0 = MODS_AT_START + s["mods0"]
                        mod_chunk(None, 8 * i + 2 * b, b % 2, 16 * (2 * i + b // 2 + j0 // 2 + 1), s["mod_block"])

            def add_square(s, k, slot, first, last):
                pe.wait_ge(sq_ready, k + 1)
                n = s["n"]
                mm = pe.matmul(acc[:, SUM_BANK, 0:n], ones[:], SQ[:, slot, 0:n], start=first, stop=last)
                if last:
                    mm.then_inc(sum_ready, 1)
                else:
                    mm.then_inc(sq_used, 1)

            def down_body(s, i, first):
                for o in range(2):
                    t = Tiles(s["tile0"] + 4 * o, 2 * i)
                    bank = (s["acc0"] + o) % 2
                    pe.wait_ge(evac, s["acc0"] + 2 * i + o + 1 + 2)
                    for b in range(4):
                        h = 2 * s["h0"]

                        def waits(k):
                            return (h_ready, h - 2 * FC + 2 * (k + 1)) if k >= FC - 2 and o == 0 else (
                                (h_ready, h - 4) if k == 0 and o == 0 else None)
                        products(t, b, H_hi, H_lo, s["n"], range(DOWN_AT[b], DOWN_AT[b] + DOWN_PARTS[b]), bank,
                                 b == 0, b == 3, waits)
                        if b == 1 and not (first and o == 0):
                            add_square(s, s["sq0"] + 2 * i + o - 1, (s["sq0"] + o - 1) % 2, first and o == 1, False)

            def dense_body(s, i, outs, first=False):
                t = Tiles(s["tile0"], i)
                for b in outs:
                    pe.wait_ge(evac, s["acc0"] + 4 * i + b + 1)
                    m = s["n"]
                    if s["dense"] == "qkv" and i in (0, 1):
                        m = TOK
                    products(t, b, A_hi, A_lo, m, range(DC), (s["acc0"] + b) % BANKS, True, True,
                             operand_wait(s) if b == 0 else None)
                    if s["dense"] in ("pw2", "o", "wout") and not (first and b == 0):
                        add_square(s, s["sq0"] + 4 * i + b - 1, (s["sq0"] + b - 1) % 2, first and b == 1, False)

            def norm_stage(s):
                src = source(s)
                n = s["n"]
                if s["norm"] == "ln":
                    pe.wait_ge(conv_done, DC)
                    for c in range(DC):
                        mm = pe.matmul(acc[:, SUM_BANK, 0:n], ones[:], src[:, c, 0:n], start=(c == 0), stop=(c == DC - 1))
                    mm.then_inc(sum_ready, 1)
                if s["fused"]:
                    add_square(s, s["sq0"] + DC - 1, (s["sq0"] + DC - 1) % 2, False, True)
                    pe.sem_inc(sq_used, 1)
                else:
                    for c in range(DC):
                        add_square(s, s["sq0"] + c, (s["sq0"] + c) % 2, c == 0, c == DC - 1)
                    pe.sem_inc(sq_used, 1)

            def na_values(s):
                pe.wait_ge(evac, s["acc0"] + BANKS)
                pe.wait_ge(ident_loaded, 16)
                for c in range(DC):
                    if c >= 2:
                        pe.wait_ge(v_copied, c - 1)
                    for k in range(4):
                        mm = pe.transpose(acc[:, AUX0 + c % 2, k * P:(k + 1) * P], VT[:, c, k * P:(k + 1) * P], ident[:])
                    mm.then_inc(vt_ready, 1)
                pe.wait_ge(v_copied, DC)

            def mix_projections(s):
                pe.wait_ge(mix_loaded, 16 * 5)
                for i, (src, bank, first, last) in enumerate(((SCL[:, 0, :], SUM_BANK, True, False),
                                                              (SCL[:, 1, :], SUM_BANK, False, True),
                                                              (AFF[:, 0, :], AUX0, True, True))):
                    pe.wait_ge(lora_squared, i + 1)
                    mm = pe.matmul(acc[:, bank, :], ones[:], src, start=first, stop=last)
                    if last:
                        mm.then_inc(lora_summed, 1)
                for k in range(4):
                    mm = pe.transpose(acc[:, 0, k * P:(k + 1) * P], VST[:, k * P:(k + 1) * P], ident[:])
                mm.then_inc(proj_ready, 1)
                pe.wait_ge(lora_ready, 2)
                for h in range(8):
                    j = 1 + h
                    if j >= 4:
                        pe.wait_ge(proj_moved, j - 3)
                    for k in range(2):
                        mm = pe.matmul(acc[0:96, j % 4, :], WUQ[:, k, h * 96:(h + 1) * 96], CQ[:, k, :],
                                       start=(k == 0), stop=(k == 1))
                    mm.then_inc(proj_ready, 1)
                pe.wait_ge(lora_ready, 3)
                for h in range(8):
                    j = 9 + h
                    pe.wait_ge(proj_moved, j - 3)
                    pe.matmul(acc[0:64, j % 4, :], WUKV[:, h * 64:(h + 1) * 64], CKV[:], start=True,
                              stop=True).then_inc(proj_ready, 1)
                for k in range(4):
                    j = 17 + k
                    pe.wait_ge(proj_moved, j - 3)
                    pe.matmul(acc[:, j % 4, :], CKV[:, k * P:(k + 1) * P], WUKV[:, 512:1024], start=True,
                              stop=True).then_inc(proj_ready, 1)
                pe.wait_ge(proj_moved, 21)
                for j, (x, which, bank, rows) in enumerate(rotations()):
                    if j >= 2:
                        pe.wait_ge(rot_done, j - 1)
                    pe.matmul(acc[0:rows, bank, 0:TOK], TURN[0:rows, which, 0:rows], x, start=True,
                              stop=True).then_inc(rot_ready, 1)
                pe.wait_ge(rot_done, 14)
                pe.wait_ge(kpe_spread, 8)

            def softmax_stage(s):
                SS, PX, PT, ST = soft[s["which"]]
                todo, u0 = units[s["which"]], s["unit0"]
                per = len(todo) // DC
                for u in range(len(todo) + 2):
                    if u < len(todo):
                        w = todo[u]
                        if u >= 2:
                            pe.wait_ge(s_moved, u0 + u - 1)
                        pe.matmul(acc[:, u % 2, 0:T2 - w["k0"]], w["q"], w["k"], start=True, stop=True).then_inc(s_scored, 1)
                    if 1 <= u <= len(todo):
                        v, r = u - 1, (u - 1) % 2
                        pe.wait_ge(p_ready, u0 + v + 1)
                        if v >= 2:
                            pe.wait_ge(pt_copied, u0 + v - 1)
                        for k in range((T2 - todo[v]["k0"]) // P):
                            mm = pe.transpose(acc[:, 2 + r, k * P:(k + 1) * P], PX[:, r, k * P:(k + 1) * P], ident[:])
                        mm.then_inc(pt_ready, 1)
                    if u >= 2:
                        v, w = u - 2, todo[u - 2]
                        pe.wait_ge(pt_copied, u0 + v + 1)
                        if v % per == 0 and v >= 2 * per:
                            pe.wait_ge(operand_ready, s["operand0"] + w["pair"] - 1)
                        nk = (T2 - w["k0"]) // P
                        for k in range(nk):
                            mm = pe.matmul(acc[w["po"]:w["po"] + 64, AUX0 + w["pair"] % 2, w["qt"] * P:(w["qt"] + 1) * P],
                                           w["v"](w["k0"] // P + k), PT[:, v % 2, k * P:(k + 1) * P],
                                           start=(k == 0), stop=(k == nk - 1))
                        mm.then_inc(o_ready, 1)

            def s5_stage(s):
                pe.wait_ge(evac, s["acc0"] + BANKS)
                half = CHUNKS // 2
                for c in range(DC):
                    if c >= 2:
                        pe.wait_ge(u_copied, c - 1)
                    for k in range(4):
                        mm = pe.transpose(acc[:, AUX0 + c % 2, k * P:(k + 1) * P], UT[:, c, k * P:(k + 1) * P], ident[:])
                    mm.then_inc(u_turned, 1)
                for b in range(8):
                    pe.wait_ge(uch_sorted, b + 1)
                    pe.wait_ge(u_copied, DC)
                    if b >= 2:
                        pe.wait_ge(ug_copied, b - 1)
                    for i in range(8):
                        g = 8 * b + i
                        mm = pe.transpose(acc[:, AUX0 + b % 2, i * CHUNKS:(i + 1) * CHUNKS],
                                          UGT[:, g].rearrange("p t c -> p (t c)"), ident[0:CHUNKS, 0:CHUNKS])
                    mm.then_inc(ug_turned, 1)
                pe.wait_ge(ug_copied, 8)

                def own_states(j):
                    pe.wait_ge(w_copied, j + 1)
                    if j >= 2:
                        pe.wait_ge(s_stored, j - 1)
                    for g2 in range(2):
                        for x in range(4):
                            mm = pe.matmul(acc[64 * g2:64 * g2 + 64, 2 + j % 2, x * CHUNKS:(x + 1) * CHUNKS],
                                           WT[:, j % 2, x, 64 * g2:64 * g2 + 64], UG[:, 2 * j + g2, :],
                                           start=True, stop=True)
                    mm.then_inc(s_summed, 1)

                for j in range(33):
                    if j < 32:
                        q = j // 8
                        pe.wait_ge(e_ready, q + 1)
                        if j >= 2:
                            pe.wait_ge(w_copied, j - 1)
                        for d in range(2):
                            for part in range(2):
                                x = 2 * d + part
                                mm = pe.transpose(acc[:, j % 2, x * P:(x + 1) * P], EE[q % 2][:, d, part, j % 8, :], ident[:])
                        mm.then_inc(w_turned, 1)
                    if j >= 1:
                        own_states(j - 1)

                def outputs(j):
                    q = j // 8
                    pe.wait_ge(d_ready, j + 1)
                    for g2 in range(2):
                        rows = slice(64 * g2, 64 * g2 + 64)
                        at = j % 8 * half
                        dst = acc[:, 2 + 2 * (q % 2) + g2, at:at + half]
                        pe.matmul(dst, DD[:, j % 2, g2, :], UG[:, 2 * j + g2, half:CHUNKS], start=True, stop=False)
                        for d in range(2):
                            order = slice(None, None, -1) if d else slice(None)
                            for part in range(2):
                                mm = pe.matmul(dst, EE[1][rows, d, part, j % 8, :], TT[rows, order, part, 32 * d + j],
                                               start=False, stop=(d == 1 and part == 1))
                    mm.then_inc(y_pair_done, 1)

                pe.wait_ge(scan_step, 5 * (CHUNKS - 1))
                for q in range(4):
                    pe.wait_ge(f_ready, 2 * q + 2)
                    for i in range(9):
                        if i < 8:
                            j = 8 * q + i
                            if j >= 2:
                                pe.wait_ge(d_ready, j - 1)
                            for g2 in range(2):
                                rows = slice(64 * g2, 64 * g2 + 64)
                                for d in range(2):
                                    for part in range(2):
                                        mm = pe.matmul(acc[:, (0, AUX0)[j % 2] + g2, d * P:(d + 1) * P],
                                                       EE[0][rows, d, part, i, :], EE[1][rows, d, part, i, :],
                                                       start=(part == 0), stop=(part == 1))
                            mm.then_inc(d_summed, 1)
                        if i >= 1:
                            outputs(8 * q + i - 1)
                pe.wait_ge(g_done, 1)
                for b in range(16):
                    if b >= 2:
                        pe.wait_ge(yc_copied, b - 1)
                    for i in range(4):
                        mm = pe.transpose(acc[0:half, AUX0 + b % 2, i * P:(i + 1) * P], YG[:, 4 * b + i, :], ident[:])
                    mm.then_inc(yc_turned, 1)
                pe.wait_ge(ytok_loaded, 16)
                for c in range(DC):
                    if c >= 2:
                        pe.wait_ge(operand_ready, s["operand0"] + c - 1)
                    for k in range(2):
                        mm = pe.transpose(acc[:, c % 2, k * P:(k + 1) * P], YTOK[:, k, c * P:(c + 1) * P], ident[:])
                    mm.then_inc(y_turned, 1)

            pe.wait_ge(ones_set, 1)
            for s in plan:
                if s["kind"] == "s5":
                    s5_stage(s)
                if s["kind"] == "norm":
                    norm_stage(s)
                elif s["kind"] == "pair":
                    s["mod_block"] = 0 if MODS_AT_START + s["mods0"] < 2 * MODC else 1
                    with_mods = s["mods"] // 4
                    if with_mods:
                        with pe.Fori(0, with_mods) as i:
                            pair_body(s, i, True)
                    if with_mods < s["pairs"] // 2:
                        with pe.Fori(with_mods, s["pairs"] // 2) as i:
                            pair_body(s, i, False)
                elif s["kind"] == "down":
                    down_body(s, 0, True)
                    with pe.Fori(1, DC // 2) as i:
                        down_body(s, i, False)
                elif s["kind"] == "dense":
                    if s["dense"] in ("pw2", "o", "wout"):
                        dense_body(s, 0, range(4), True)
                        dense_body(s, 1, range(4))
                    else:
                        for i in range(s["outs"] // 4):
                            dense_body(s, i, range(4))
                        if s["outs"] % 4:
                            dense_body(s, s["outs"] // 4, range(s["outs"] % 4))
                elif s["kind"] == "attention":
                    if s["which"] == "na":
                        na_values(s)
                    else:
                        mix_projections(s)
                    softmax_stage(s)
STOP = None



def _tiles(w):
    k, m = w.shape
    return np.ascontiguousarray(
        w.reshape(k // P, P, m // P, P).transpose(2, 1, 0, 3).reshape(m // P, P, k))


def _columns(v):
    return v.reshape(-1, P).T


def _twice(v):
    return np.repeat(_columns(v), 2, axis=1)


def _features(x):
    return x.T.reshape(DC, P, -1).transpose(1, 0, 2)


def _rotation_tables():
    f = np.float32
    pos = np.arange(TOK)
    rot, turn = np.zeros((P, 4, TOK), f), np.zeros((P, 2, P), f)
    rot[:, 0] = 1
    for which, (width, starts) in enumerate(((32, (64,)), (64, (0, 64)))):
        axis = width // 2
        inv = f(10000.0) ** (-np.arange(0, axis, 2, dtype=f) / f(axis))
        angle = np.concatenate([(pos // 64).astype(f)[:, None] * inv, (pos % 64).astype(f)[:, None] * inv], axis=1)
        for at in starts:
            for half in range(2):
                rows = slice(at + half * axis, at + (half + 1) * axis)
                rot[rows, 2 * which], rot[rows, 2 * which + 1] = np.cos(angle).T, np.sin(angle).T
            for i in range(axis):
                turn[at + axis + i, which, at + i] = -1
                turn[at + i, which, at + axis + i] = 1
    band = np.where(np.abs(pos[:, None] - pos[None]) <= 128, f(0), f(-1e30)).reshape(2, P, TOK).transpose(1, 0, 2)
    return rot, turn, band


def _arrays(a):
    a = {k: np.asarray(v) for k, v in a.items()}
    out = {}
    out["x"] = np.concatenate([_features(a["x"][0]), _features(a["ctx"][0])], axis=2)
    out["ctx_2"] = _features(a["ctx_2"][0])
    out["ident"] = np.eye(P, dtype=np.float32)

    vecs = np.zeros((P, NVEC), np.float32)

    def put(name, cols):
        at, width = VEC[name]
        vecs[:, at:at + width] = cols

    put("mod_b", np.concatenate([_twice(a[n][l]) for n in ("mod_b", "mod_b_2") for l in range(2)], axis=1))
    for l in range(LAYERS):
        for s in range(3):
            put(f"g{l}{s}", _twice((a["norm_g"] if l < 2 else a["norm_pre_2"])[l % 2, s]))
            if l >= 2:
                put(f"gpost{l}{s}", _twice(a["norm_post_2"][l % 2, s]))
    put("c", np.stack([np.stack([_columns(a["c"][0]), _columns(a["c_ctx"])], axis=2),
                       np.stack([_columns(a["c_2"][0]), _columns(a["c_ctx_2"])], axis=2)], axis=1).reshape(P, -1))
    put("b_pw1", _columns(a["conv_b_pw1"][0]))
    put("w_dw", a["conv_w_dw"][0].reshape(TAPS, DC, P).transpose(2, 1, 0).reshape(P, -1))
    put("b_dw", _columns(a["conv_b_dw"][0]))
    put("ln_g", _columns(a["conv_ln_g"][0]))
    put("ln_b", _columns(a["conv_ln_b"][0]))
    put("b_pw2", _columns(a["conv_b_pw2"][0]))
    put("b_qkv", _columns(a["na_b_qkv"][0]))
    put("b_o", _columns(a["na_b_o"][0]))
    put("final_g", _columns(a["final_g"]))
    put("q_norm", _columns(a["mla_q_norm_2"][0]))
    put("kv_norm", _columns(a["mla_kv_norm_2"][0]))
    put("sink", np.broadcast_to(a["swa_sink_2"][0], (P, 8)))
    out["vecs"] = vecs

    out["mod_w"] = np.concatenate([_tiles(a[n][l]) for n in ("mod_w", "mod_w_2") for l in range(2)])
    for l in range(LAYERS):
        for h in range(2):
            if l < 2:
                gate, up, down = (a[n][l, h] for n in ("ffn_w_gate", "ffn_w_up", "ffn_w_down"))
            else:
                gate, up = a["ffn_w13_2"][l - 2, h, :, :F], a["ffn_w13_2"][l - 2, h, :, F:]
                down = a["ffn_w2_2"][l - 2, h]
            out[f"ffn_gate_{l}{h}"] = _tiles(gate)
            out[f"ffn_up_{l}{h}"] = _tiles(up)
            out[f"ffn_down_{l}{h}"] = _tiles(down)
    pw1 = a["conv_w_pw1"][0]
    out["pw1_a"], out["pw1_gate"] = _tiles(pw1[:, :D]), _tiles(pw1[:, D:])
    out["pw2"] = _tiles(a["conv_w_pw2"][0])
    out["qkv"] = _tiles(a["na_w_qkv"][0])
    out["o"] = _tiles(a["na_w_o"][0])

    w = a["attn_w_in_2"][0]
    at = np.cumsum([0, 256, 128, 32, 512, 128, 128])
    cq, ckv, kpe, qs, ks, vs = (w[:, at[i]:at[i + 1]] for i in range(6))
    pad = np.zeros((D, 64), np.float32)
    qs = qs.reshape(D, 2, 4, 64).transpose(0, 2, 1, 3).reshape(D, 512)
    out["win"] = _tiles(np.concatenate([cq, ckv, pad, kpe, pad[:, :32], qs, ks, vs], axis=1))
    out["wout"] = _tiles(a["attn_w_out_2"][0])
    out["w_uq"] = a["mla_w_uq_2"][0].reshape(2, P, 768).transpose(1, 0, 2)
    out["w_ukv"] = a["mla_w_ukv_2"][0].reshape(P, 8, 2, 64).transpose(0, 2, 1, 3).reshape(P, 1024)
    out["rot"], out["turn"], out["band"] = _rotation_tables()

    out["s5in"] = _tiles(a["s5_w_in_2"][0])
    glu = a["s5_w_glu_2"][0]
    out["glu_a"], out["glu_gate"] = _tiles(glu[:, :D]), _tiles(glu[:, D:])

    def states(v):
        v = v.reshape((2, GROUPS // 2, 2, 64) + v.shape[3:])
        return np.moveaxis(v, (2, 3), (0, 1)).reshape((P, COLS) + v.shape[4:])

    step = np.broadcast_to(a["s5_log_step_2"][0][:, :, None], (2, GROUPS, 64))
    out["s5_par"] = np.stack([states(a["s5_lambda_re_2"][0]), states(a["s5_lambda_im_2"][0]), states(step)], axis=1)
    out["s5_bc"] = np.stack([states(a["s5_b_re_2"][0]), states(a["s5_b_im_2"][0]),
                             states(a["s5_c_re_2"][0].transpose(0, 1, 3, 2)),
                             states(a["s5_c_im_2"][0].transpose(0, 1, 3, 2))], axis=1)
    out["s5_skip"] = np.tile(a["s5_d_2"][0].reshape(GROUPS, GROUP).T, (SUB, 1))
    token = np.arange(P) // GROUP
    out["s5_mask"] = np.stack([token[:, None] <= token[None], token[:, None] >= token[None]], axis=1).astype(np.float32)
    out["s5_zero"] = np.zeros((P, 12, COLS), np.float32)

    rows, cols, win = TOK // 64, 64, 16
    q, k = np.arange(TOK), np.arange(TOK)
    qr, qc, kr, kc = q[:, None] // cols, q[:, None] % cols, k[None] // cols, k[None] % cols
    start = np.clip(qc - win // 2, 0, cols - win)
    inside = (kc >= start) & (kc < start + win)
    rel = np.clip(kc - qc, -(win - 1), win - 1) + win - 1
    bias = a["na_rpb"][0][:, kr - qr + 7, rel]
    out["na_bias"] = np.where(inside[None], bias, np.float32(-1e30)).astype(np.float32).reshape(16, 2, P, TOK)
    return {k: np.ascontiguousarray(v) for k, v in out.items()}


def kernel(**inputs):
    import concourse.bacc as _bacc
    from concourse.bass_utils import run_bass_kernel_spmd as _run

    nc = _bacc.Bacc("TRN2", target_bir_lowering=False, num_devices=1)
    arrays = _arrays(inputs)
    io = {}
    for name, a in arrays.items():
        io[name] = nc.dram_tensor(f"in_{name}", a.shape, F32, kind="ExternalInput").ap()
    for kind in ("gate", "up", "down"):
        io[f"ffn_{kind}"] = [[io[f"ffn_{kind}_{l}{h}"] for h in range(2)] for l in range(LAYERS)]
    out = nc.dram_tensor("out_x", (P, DC, TOK), F32, kind="ExternalOutput").ap()
    build(nc, io, out, STOP)
    r = _run(nc, [{f"in_{k}": v for k, v in arrays.items()}], core_ids=[0])
    got = r.results[0]["out_x"]
    return np.ascontiguousarray(got.transpose(1, 0, 2).reshape(D, TOK).T)[None]
```

```python
from contextlib import ExitStack

import numpy as np

import concourse.bass as bass
from concourse import mybir

F32 = mybir.dt.float32
F32R = mybir.dt.float32r
ALU = mybir.AluOpType
ACT = mybir.ActivationFunctionType
AX = mybir.AxisListType

P = 128
D = 1024
DC = D // P
TOK = 256
T2 = 2 * TOK
F = 2816
FC = F // P
N_MOD = 9
MODC = N_MOD * DC
LAYERS = 4
TILE = DC * P
RAW = 4
SPLIT = 2
BANKS = 4
SUM_BANK, MOD_BANK, AUX0 = 4, 5, 6
DOWN_PARTS = (6, 6, 5, 5)
DOWN_AT = (0, 6, 12, 17)
MODS_AT_START = 28
RMS_EPS, LN_EPS = 1e-6, 1e-5
GROUPS, GROUP = 64, 16
SUB = 8
CHUNKS = T2 // SUB
COLS = GROUPS
TAPS = 31
SIDE_TAPS = 11
PADW = TOK + TAPS - 1


def vector_columns():
    at, n = {}, 0

    def take(name, width):
        nonlocal n
        at[name] = (n, width)
        n += width

    take("mod_b", LAYERS * MODC * 2)
    for l in range(LAYERS):
        for s in range(3):
            take(f"g{l}{s}", DC * 2)
    for l in (2, 3):
        for s in range(3):
            take(f"gpost{l}{s}", DC * 2)
    take("c", 2 * DC * 2)
    take("b_pw1", 2 * DC)
    take("w_dw", DC * TAPS)
    for name in ("b_dw", "ln_g", "ln_b", "b_pw2"):
        take(name, DC)
    take("b_qkv", 3 * DC)
    take("b_o", DC)
    take("final_g", DC)
    take("q_norm", 2)
    take("kv_norm", 1)
    take("sink", 8)
    return at, n


VEC, NVEC = vector_columns()


class Tiles:

    def __init__(self, base, step=0):
        self.base, self.step = base, step

    def raw(self, b):
        return (self.base + b) % RAW

    def split(self, b):
        return (self.base + b) % SPLIT

    def loaded(self, b):
        return 16 * (self.step + (self.base + b) // RAW + 1)

    def count(self, b):
        return self.base + b + 4 * self.step


def build_plan():
    counts = dict(tile=0, acc=0, sq=0, sums=0, rstd=0, scaled=0, affine=0, operand=0, silu=0, mods=0,
                  h=0, vecs=0, xnew=0, biased=0, unit=0)
    plan = []

    def add(kind, takes, **how):
        plan.append(dict(kind=kind, **how, **{f"{k}0": v for k, v in counts.items()}))
        for k, v in takes.items():
            counts[k] += v

    def norm(kind, n, fused=False, chunks=DC, **how):
        takes = dict(sq=chunks, sums=1, rstd=1, scaled=chunks)
        if kind in ("mod", "ln"):
            takes.update(affine=chunks, operand=chunks)
        if kind == "ln":
            takes["sums"] = 2
        if kind == "mod":
            takes["vecs"] = 1
        if kind in ("final", "post"):
            takes["xnew"] = chunks
        add("norm", takes, norm=kind, n=n, fused=fused, **how)

    def ffn(layer, half, n, mods, **how):
        add("pair", dict(tile=2 * FC, acc=2 * FC, silu=FC, mods=mods, h=FC), pair="ffn", n=n, pairs=FC,
            layer=layer, half=half, mods=mods)
        add("down", dict(tile=4 * DC, acc=DC), n=n, layer=layer, half=half, post=layer >= 2)
        if layer >= 2:
            norm("post", n, fused=True, layer=layer, site=2 * half)

    def build():
        norm("mod", T2, layer=0, site=0)
        ffn(0, 0, T2, 44)
        norm("mod", T2, fused=True, layer=0, site=1)
        add("pair", dict(tile=2 * DC, acc=2 * DC, silu=DC), pair="conv", n=T2, pairs=DC, mods=0)
        norm("ln", T2)
        add("dense", dict(tile=DC, acc=DC, biased=DC), dense="pw2", n=T2, outs=DC)
        norm("mod", T2, fused=True, layer=0, site=2)
        ffn(0, 1, T2, 44)
        norm("mod", T2, fused=True, layer=1, site=0)
        ffn(1, 0, T2, 44)
        norm("mod", T2, fused=True, layer=1, site=1)
        add("dense", dict(tile=3 * DC, acc=3 * DC), dense="qkv", n=T2, outs=3 * DC)
        add("attention", dict(operand=DC, unit=32), which="na")
        add("dense", dict(tile=DC, acc=DC, biased=DC), dense="o", n=TOK, outs=DC)
        norm("mod", TOK, fused=True, layer=1, site=2)
        ffn(1, 1, TOK, 12)
        norm("final", TOK, fused=True)
        norm("mod", T2, layer=2, site=0)
        ffn(2, 0, T2, 44)
        norm("mod", T2, layer=2, site=1)
        add("dense", dict(tile=10, acc=10), dense="win", n=T2, outs=10)
        add("attention", dict(operand=DC, unit=64), which="mix")
        add("dense", dict(tile=DC, acc=DC), dense="wout", n=T2, outs=DC)
        norm("post", T2, fused=True, layer=2, site=1)
        norm("mod", T2, layer=2, site=2)
        ffn(2, 1, T2, 44)
        norm("mod", T2, layer=3, site=0)
        ffn(3, 0, T2, 28)
        norm("mod", T2, layer=3, site=1)
        add("dense", dict(tile=DC, acc=DC), dense="s5in", n=T2, outs=DC)
        add("s5", dict(operand=DC))
        add("pair", dict(tile=2 * DC, acc=2 * DC, silu=DC), pair="glu", n=TOK, pairs=DC, mods=0)
        norm("post", TOK, layer=3, site=1)
        norm("mod", TOK, layer=3, site=2)
        ffn(3, 1, TOK, 0)

    build()
    return plan, counts


def build(nc, io, out):
    plan, totals = build_plan()
    with ExitStack() as ctx:
        def sb(name, shape, dtype=F32, scope=ctx):
            return scope.enter_context(nc.sbuf_tensor(name, shape, dtype))

        def sem(name):
            return ctx.enter_context(nc.semaphore(name))

        X = sb("X", [P, DC, T2])
        y_scope = ExitStack()
        OVER = sb("OVER", [P, 2 * DC * T2], F32, y_scope)
        Y_ffn = OVER[:, 0:DC * T2].rearrange("p (c t) -> p c t", c=DC)
        y_scope.close()
        A_hi = sb("A_hi", [P, DC, T2], F32R)
        A_lo = sb("A_lo", [P, DC, T2], F32R)
        raw = sb("raw", [P, RAW, TILE])
        w_hi = sb("w_hi", [P, SPLIT, TILE], F32R)
        w_lo = sb("w_lo", [P, SPLIT, TILE], F32R)
        modw = sb("modw", [P, 2, TILE])
        V = sb("V", [P, NVEC])
        MOD = sb("MOD", [P, LAYERS * MODC * 2])
        silu_c = sb("silu_c", [P, 2, DC, 2])
        A_scale = sb("A_scale", [P, 2 * DC])
        GATE = sb("GATE", [P, 2 * DC])
        ones = sb("ones", [P, P])
        ident = sb("ident", [P, P])
        WARM = sb("WARM", [P, 1])
        SQ = sb("SQ", [P, 2, T2])
        RST = sb("RST", [P, T2])
        SCL = sb("SCL", [P, 2, T2])
        AFF = sb("AFF", [P, 2, T2])

        ffn_scope = ExitStack()
        H_hi = sb("H_hi", [P, FC, T2], F32R, ffn_scope)
        H_lo = sb("H_lo", [P, FC, T2], F32R, ffn_scope)
        MT = sb("MT", [P, 2, 2, T2], F32, ffn_scope)
        ffn_scope.close()
        conv_scope = ExitStack()
        U = sb("U", [P, DC, 2, PADW], F32, conv_scope)
        CO = sb("CO", [P, DC, T2], F32, conv_scope)
        MU = sb("MU", [P, T2], F32, conv_scope)
        CM = sb("CM", [P, 4, T2], F32, conv_scope)
        CP = sb("CP", [P, 2, T2], F32, conv_scope)
        conv_scope.close()
        na_scope = ExitStack()
        Q = sb("Q", [P, DC, TOK], F32, na_scope)
        K = sb("K", [P, DC, T2], F32, na_scope)
        VT = sb("VT", [P, DC, T2], F32, na_scope)
        VV = sb("VV", [P, 4, D], F32, na_scope)
        SS = sb("SS", [P, 2, T2 + 8], F32, na_scope)
        PX = sb("PX", [P, 2, T2 + 8], F32, na_scope)
        PT = sb("PT", [P, 2, T2], F32, na_scope)
        NB = sb("NB", [P, 2, TOK], F32, na_scope)
        ST = sb("ST", [P, 2, 4], F32, na_scope)
        na_scope.close()
        mix_scope = ExitStack()
        Q96 = sb("Q96", [96, 8, T2], F32, mix_scope)
        K96 = sb("K96", [96, 8, T2], F32, mix_scope)
        QS = sb("QS", [P, 4, T2], F32, mix_scope)
        KS = sb("KS", [P, T2], F32, mix_scope)
        VST = sb("VST", [P, T2], F32, mix_scope)
        VVa = sb("VVa", [P, 4, 512], F32, mix_scope)
        VVb = sb("VVb", [P, 4, P], F32, mix_scope)
        CQ = sb("CQ", [P, 2, T2], F32, mix_scope)
        CKV = sb("CKV", [P, T2], F32, mix_scope)
        KP = sb("KP", [P, T2], F32, mix_scope)
        WUQ = sb("WUQ", [P, 2, 768], F32, mix_scope)
        WUKV = sb("WUKV", [P, 1024], F32, mix_scope)
        ROT = sb("ROT", [P, 4, TOK], F32, mix_scope)
        TURN = sb("TURN", [P, 2, P], F32, mix_scope)
        BAND = sb("BAND", [P, 2, TOK], F32, mix_scope)
        SS2 = sb("SS2", [P, 2, T2 + 8], F32, mix_scope)
        PX2 = sb("PX2", [P, 2, T2 + 8], F32, mix_scope)
        PT2 = sb("PT2", [P, 2, T2], F32, mix_scope)
        ST2 = sb("ST2", [P, 2, 4], F32, mix_scope)
        mix_scope.close()
        s5_scope = ExitStack()
        UG = sb("UG", [P, GROUPS, CHUNKS], F32, s5_scope)
        SPAR = sb("SPAR", [P, 3, COLS], F32, s5_scope)
        BC = sb("BC", [P, 4, COLS, GROUP], F32, s5_scope)
        EP = sb("EP", [P, 4, COLS, SUB], F32, s5_scope)
        A8 = sb("A8", [P, 2, 2, COLS], F32, s5_scope)
        DSK = sb("DSK", [P, GROUPS], F32, s5_scope)
        MASK = sb("MASK", [P, 2, P], F32, s5_scope)
        WT = modw[:, :, 0:4 * P].rearrange("p j (x m) -> p j x m", x=4)
        DM = modw[:, 0, 4 * P:TILE].rearrange("p (g d m) -> p g d m", g=2, d=2)
        DD = modw[:, 1, 4 * P:TILE].rearrange("p (j g m) -> p j g m", j=2, g=2)
        SM = sb("SM", [P, 12, COLS], F32, s5_scope)
        early = ExitStack()
        UT = sb("UT", [P, DC, T2], F32, early)
        UTOK = sb("UTOK", [P, 4, D], F32, early)
        early.close()
        early2 = ExitStack()
        UGT = sb("UGT", [CHUNKS, GROUPS, SUB, GROUP], F32, early2)
        early2.close()
        late = ExitStack()
        YG = sb("YG", [P, GROUPS, CHUNKS // 2], F32, late)
        YS = sb("YS", [P, GROUPS, CHUNKS // 2], F32, late)
        late.close()
        S = sb("S", [P, CHUNKS, 2, COLS], F32, s5_scope)
        late2 = ExitStack()
        PW = sb("PW", [P, 4, SUB + 1, COLS], F32, late2)
        late2.close()
        late3 = ExitStack()
        YTOK = sb("YTOK", [P, 2, D], F32, late3)
        late3.close()
        TT = sb("TT", [P, CHUNKS // 2, 2, COLS], F32, s5_scope)
        s5_scope.close()
        EE = [OVER[:, i * 4096:(i + 1) * 4096].rearrange("p (d a g m) -> p d a g m", d=2, a=2, g=8) for i in range(2)]
        UCH = OVER[0:CHUNKS, :].rearrange("p (t d) -> p t d", t=SUB)
        YC = OVER[0:CHUNKS // 2, :].rearrange("p (t d) -> p t d", t=SUB)
        mixy_scope = ExitStack()
        Y_mix = sb("Y_mix", [P, DC, T2], F32, mixy_scope)
        mixy_scope.close()
        soft = {"na": (SS, PX, PT, ST), "mix": (SS2, PX2, PT2, ST2)}

        acc = ctx.enter_context(nc.psum_tensor("acc", [P, 8, T2], F32))

        raw_loaded = [sem(f"raw_loaded{i}") for i in range(RAW)]
        modw_loaded = [sem(f"modw_loaded{i}") for i in range(2)]
        x_loaded = sem("x_loaded")
        vec_loaded = sem("vec_loaded")
        ctx2_loaded = sem("ctx2_loaded")
        ones_set = sem("ones_set")
        silu_c_ready = sem("silu_c_ready")
        hi_ready = sem("hi_ready")
        lo_ready = sem("lo_ready")
        tile_done = sem("tile_done")
        evac = sem("evac")
        mod_terms = [sem("mod_terms_latent"), sem("mod_terms_context")]
        mod_products = sem("mod_products")
        mods_summed = sem("mods_summed")
        vecs_ready = sem("vecs_ready")
        sq_ready = sem("sq_ready")
        sq_used = sem("sq_used")
        sum_ready = sem("sum_ready")
        recip_ready = sem("recip_ready")
        rstd_ready = sem("rstd_ready")
        centred = sem("centred")
        scaled = sem("scaled")
        affine = sem("affine")
        operand_ready = sem("operand_ready")
        xnew = sem("xnew")
        silu_ready = sem("silu_ready")
        h_ready = sem("h_ready")
        margins_set = sem("margins_set")
        dve_chain = sem("dve_chain")
        pool_chain = sem("pool_chain")
        conv_done = sem("conv_done")
        tap_products = sem("tap_products")
        taps_added = sem("taps_added")
        biased = sem("biased")
        ident_loaded = sem("ident_loaded")
        s_scored = sem("s_scored")
        s_moved = sem("s_moved")
        nmax_ready = sem("nmax_ready")
        exp_ready = sem("exp_ready")
        p_ready = sem("p_ready")
        pt_ready = sem("pt_ready")
        pt_copied = sem("pt_copied")
        o_ready = sem("o_ready")
        vt_ready = sem("vt_ready")
        v_copied = sem("v_copied")
        bias_loaded = [sem(f"bias_loaded{i}") for i in range(2)]
        mix_loaded = sem("mix_loaded")
        lora_squared = sem("lora_squared")
        lora_summed = sem("lora_summed")
        lora_recip = sem("lora_recip")
        lora_rstd = sem("lora_rstd")
        lora_ready = sem("lora_ready")
        proj_ready = sem("proj_ready")
        proj_moved = sem("proj_moved")
        rot_ready = sem("rot_ready")
        rot_done = sem("rot_done")
        kpe_spread = sem("kpe_spread")
        stored = sem("stored")
        s5_loaded = sem("s5_loaded")
        dt_ready = sem("dt_ready")
        rates_ready = sem("rates_ready")
        mags_ready = sem("mags_ready")
        angles_ready = sem("angles_ready")
        sines_ready = sem("sines_ready")
        u_turned = sem("u_turned")
        u_copied = sem("u_copied")
        u_stored = sem("u_stored")
        uch_loaded = sem("uch_loaded")
        ug_turned = sem("ug_turned")
        ug_copied = sem("ug_copied")
        e_ready = sem("e_ready")
        w_turned = sem("w_turned")
        w_copied = sem("w_copied")
        s_summed = sem("s_summed")
        s_stored = sem("s_stored")
        scan_step = sem("scan_step")
        f_ready = sem("f_ready")
        d_summed = sem("d_summed")
        d_ready = sem("d_ready")
        y_taken = sem("y_taken")
        g_inner = sem("g_inner")
        g_tanh = sem("g_tanh")
        g_done = sem("g_done")
        yc_turned = sem("yc_turned")
        uch_sorted = sem("uch_sorted")
        y_pair_done = sem("y_pair_done")
        yc_copied = sem("yc_copied")
        y_stored = sem("y_stored")
        ytok_loaded = sem("ytok_loaded")
        y_turned = sem("y_turned")

        def vec(name, c=0, width=1):
            return V[:, bass.ds(VEC[name][0] + c, width)]

        tiled = [s for s in plan if s["tile0"] < totals["tile"] and s["kind"] in ("pair", "down", "dense")]

        def steps(eng, s, first, last, body):
            end = last - 1 if s is tiled[-1] else last
            if first < end:
                with eng.Fori(first, end) as i:
                    body(i)
            if end < last:
                body(last - 1)

        def s5_spread(eng, link, dst, pairs, at, d, powers, done):
            n = len(pairs)
            t1, t2 = (t[:].rearrange("p a b -> p (a b)")[:, 0:n * P].rearrange("p (g t c) -> p g t c", g=n, t=SUB)
                      for t in (AFF, SCL))
            cols = slice(32 * d + pairs[0], 32 * d + pairs[0] + n)
            a = [EP[:, powers + i, cols, :].rearrange("p g (t o) -> p g t o", o=1).broadcast_to([P, n, SUB, GROUP]) for i in range(2)]
            b = [BC[:, powers + i, cols, :].rearrange("p g (o c) -> p g o c", o=1).broadcast_to([P, n, SUB, GROUP]) for i in range(2)]
            o = [dst[:, d, i, at:at + n].rearrange("p g (t c) -> p g t c", t=SUB) for i in range(2)]
            link(eng.tensor_tensor(t1, a[0], b[0], ALU.mult))
            link(eng.tensor_tensor(t2, a[1], b[1], ALU.mult))
            link(eng.tensor_tensor(o[0], t1, t2, ALU.subtract))
            link(eng.tensor_tensor(t1, a[0], b[1], ALU.mult))
            link(eng.tensor_tensor(t2, a[1], b[0], ALU.mult))
            link(eng.tensor_tensor(o[1], t1, t2, ALU.add))
            if powers:
                link(eng.tensor_scalar(o[1], o[1], -1.0, None, ALU.mult))
            eng.sem_inc(done, 1)

        def taps_of(f, half):
            cut = (SIDE_TAPS + 1) // 2
            for x in (range(cut), range(cut, SIDE_TAPS))[half]:
                yield f * SIDE_TAPS + x, TAPS - SIDE_TAPS + x

        def mod_sums(block, stream):
            if block is None:
                return SQ[:, stream, :]
            return raw[:, RAW - 1, stream * T2:(stream + 1) * T2] if block % 2 else AFF[:, stream, :]

        def pair_runs(s):
            n, done = s["mods"] // 4, MODS_AT_START + s["mods0"]
            cut = min(max((2 * MODC - done) // 4, 0), n)
            runs = [(0, cut, True, 0), (cut, n, True, 1), (n, s["pairs"] // 2, False, 0)]
            return [r for r in runs if r[0] < r[1]]

        def mod_factor(blk, stream, k):
            return silu_c[:, blk, k, stream:stream + 1]

        def sums_free(eng, base, i, block):
            if block is None:
                eng.wait_ge(mods_summed, base // 4 + i)
            elif block >= 2:
                eng.wait_ge(mods_summed, block - 1)

        def source(s):
            if s["norm"] == "post":
                return Y_mix if s["site"] == 1 else Y_ffn
            return CO if s["norm"] == "ln" else X

        def attention_units(which):
            for h in range(16):
                pair, po = h // 2, 64 * (h % 2)
                for qt in range(2 if which == "na" else 4):
                    at = slice(qt * P, (qt + 1) * P)
                    k0 = TOK if qt >= 2 else 0
                    u = dict(h=h, qt=qt, pair=pair, po=po, k0=k0, bias=None, sink=None)
                    if which == "na":
                        u.update(q=Q[po:po + 64, pair, at], k=K[po:po + 64, pair, k0:T2], scale=64 ** -0.5,
                                 v=lambda k, h=h: VV[:, k, h * 64:(h + 1) * 64], bias="loaded")
                    elif h < 8:
                        u.update(q=Q96[0:96, h, at], k=K96[0:96, h, k0:T2], scale=96 ** -0.5,
                                 v=lambda k, h=h: VVa[:, k, h * 64:(h + 1) * 64])
                    else:
                        kv = (h - 8) // 4
                        rows = slice(64 * kv, 64 * kv + 64)
                        u.update(q=QS[rows, (h - 8) % 4, at], k=KS[rows, k0:T2], scale=64 ** -0.5,
                                 v=lambda k, kv=kv: VVb[:, k, kv * 64:(kv + 1) * 64],
                                 bias=None if qt >= 2 else BAND[:, qt, :], sink=h - 8)
                    yield u

        units = {w: list(attention_units(w)) for w in ("na", "mix")}

        def mix_moves():
            yield VVb[:], acc[:, 0, :].rearrange("p (k d) -> p k d", k=4)
            for h in range(8):
                yield Q96[:, h, :], acc[0:96, (1 + h) % 4, :]
            for h in range(8):
                yield K96[0:64, h, :], acc[0:64, (9 + h) % 4, :]
            for k in range(4):
                yield VVa[:, k, :], acc[:, (17 + k) % 4, :]

        def rotations():
            todo = [(KP[0:96, 0:TOK], 0, 96)] + [(Q96[:, h, 0:TOK], 0, 96) for h in range(8)]
            todo += [(QS[:, c, 0:TOK], 1, P) for c in range(4)] + [(KS[:, 0:TOK], 1, P)]
            for j, (x, which, rows) in enumerate(todo):
                yield x, which, j % 2, rows

        u_scratch = nc.dram_tensor("u_scratch", (T2, D), F32).ap()
        y_scratch = nc.dram_tensor("y_scratch", (TOK, D), F32).ap()

        block = ctx.enter_context(nc.Block())

        @block.sync
        def _(sp):
            sp.dma_start(V[:], io["vecs"]).then_inc(vec_loaded, 16)
            for j in range(MODS_AT_START):
                if j == 2:
                    sp.dma_start(X[:], io["x"]).then_inc(x_loaded, 16)
                if j >= 2:
                    for terms in (mod_terms[0], mod_products):
                        sp.wait_ge(terms, 2 * j - 2)
                sp.dma_start(modw[:, j % 2], io["mod_w"][j]).then_inc(modw_loaded[j % 2], 16)

            sp.wait_ge(mods_summed, MODS_AT_START // 4 - 1)

            def load_tile(t, b, src, width=TILE):
                sp.wait_ge(lo_ready, t.count(b) + 1)
                sp.dma_start(raw[:, t.raw(b), 0:width], src).then_inc(raw_loaded[t.raw(b)], 16)

            def load_mod(j, slot):
                for terms in (mod_terms[0], mod_products):
                    sp.wait_ge(terms, 2 * j - 2)
                sp.dma_start(modw[:, slot], io["mod_w"][j]).then_inc(modw_loaded[slot], 16)

            def pairs(s, first, second, i, mods):
                t = Tiles(s["tile0"], i)
                for b in range(4):
                    load_tile(t, b, (second if b % 2 else first)[2 * i + b // 2])
                    if mods:
                        load_mod(MODS_AT_START + s["mods0"] + 4 * i + b, b % 2)

            for s in plan:
                if s["kind"] == "pair":
                    if s["pair"] == "ffn":
                        first = io["ffn_gate"][s["layer"]][s["half"]]
                        second = io["ffn_up"][s["layer"]][s["half"]]
                    elif s["pair"] == "conv":
                        first, second = io["pw1_gate"], io["pw1_a"]
                    else:
                        first, second = io["glu_gate"], io["glu_a"]
                    for i0, i1, mods, _blk in pair_runs(s):
                        with sp.Fori(i0, i1) as i:
                            pairs(s, first, second, i, mods)
                if s["kind"] == "down":
                    w = io["ffn_down"][s["layer"]][s["half"]]
                    with sp.Fori(0, DC) as i:
                        for b in range(4):
                            at, width = DOWN_AT[b] * P, DOWN_PARTS[b] * P
                            load_tile(Tiles(s["tile0"], i), b, w[i, :, at:at + width], width)
                if s["kind"] == "dense":
                    w = io[s["dense"]]
                    with sp.Fori(0, s["outs"] // 4) as i:
                        for b in range(4):
                            load_tile(Tiles(s["tile0"], i), b, w[4 * i + b])
                    for o in range(s["outs"] // 4 * 4, s["outs"]):
                        load_tile(Tiles(s["tile0"]), o, w[o])

        @block.scalar
        def _(act):
            act.wait_ge(vec_loaded, 16)
            act.activation(silu_c[:], vec("c", 0, 4 * DC).rearrange("p (b c s) -> p b c s", b=2, c=DC),
                           ACT.Silu).then_inc(silu_c_ready, 1)
            act.wait_ge(silu_c_ready, 1)
            act.wait_ge(ones_set, 1)

            def split_hi(t, b, width=TILE):
                if isinstance(t.step, int) and t.count(b) >= totals["tile"]:
                    return
                act.wait_ge(raw_loaded[t.raw(b)], t.loaded(b))
                act.wait_ge(tile_done, t.count(b) + 1)
                act.activation(w_hi[:, t.split(b), 0:width], raw[:, t.raw(b), 0:width], ACT.Copy).then_inc(hi_ready, 1)

            def multiply_mod_tile(base, i, b, blk, start=False):
                j = base + 4 * i + b
                act.wait_ge(modw_loaded[b % 2], 16 * (base // 2 + 2 * i + b // 2 + 1))
                if not (start and j < 2):
                    act.wait_ge(mod_terms[1], 2 * j - 2)
                for h in range(2):
                    act.activation(MT[:, b % 2, h, :], modw[:, b % 2, h * T2:(h + 1) * T2], ACT.Copy,
                                   scale=mod_factor(blk, 1, 2 * b + h)).then_inc(mod_products, 1)

            def square(s, src, c, k, value):
                if value is not None:
                    act.wait_ge(evac, value)
                act.wait_ge(sq_used, k + 1)
                n = s["n"]
                act.activation(SQ[:, s["sqslot"], 0:n], src[:, c, 0:n], ACT.Square).then_inc(sq_ready, 1)

            def multiply_taps(s, f, half):
                act.wait_ge(margins_set, 1)
                act.wait_ge(evac, s["acc0"] + 2 * f + 2 + BANKS)
                for n, tap in taps_of(f, half):
                    if n >= 4:
                        act.wait_ge(taps_added, n - 3)
                    act.activation(CM[:, n % 4, :].rearrange("p (s t) -> p s t", s=2), U[:, f, :, tap:tap + TOK],
                                   ACT.Copy, scale=vec("w_dw", f * TAPS + tap)).then_inc(tap_products, 1)

            def pair_body(s, i, mods, blk):
                t = Tiles(s["tile0"], i)
                for b in range(4):
                    split_hi(t, b + 1)
                    if b % 2:
                        f = 2 * i + b // 2
                        act.wait_ge(tile_done, t.count(b - 1) + 1 + SPLIT)
                        gate = acc[:, (s["acc0"] + b - 1) % BANKS, 0:s["n"]]
                        dst = SCL[:, b // 2, 0:s["n"]]
                        if s["pair"] == "ffn":
                            act.activation(dst, gate, ACT.Silu).then_inc(silu_ready, 1)
                        elif s["pair"] == "conv":
                            act.activation(dst, gate, ACT.Sigmoid, bias=vec("b_pw1", DC + f)).then_inc(silu_ready, 1)
                            multiply_taps(s, f, 0)
                        else:
                            act.activation(dst, gate, ACT.Sigmoid).then_inc(silu_ready, 1)
                    elif s["pair"] == "conv" and 2 * i + b:
                        multiply_taps(s, 2 * i + b // 2 - 1, 1)
                    if mods:
                        multiply_mod_tile(MODS_AT_START + s["mods0"], i, b, blk)

            def down_body(s, i):
                for o in range(2):
                    for b in range(4):
                        t = Tiles(s["tile0"] + 4 * o, 2 * i)
                        split_hi(t, b + 1, TILE if b == 3 else DOWN_PARTS[b + 1] * P)
                    square({**s, "sqslot": (s["sq0"] + o) % 2}, Y_ffn if s["post"] else X, 2 * i + o,
                           s["sq0"] + 2 * i + o, s["acc0"] + 2 * i + o + 1 + BANKS)

            def norm_stage(s):
                n = s["n"]
                src = source(s)
                if s is plan[0]:
                    for block in range(MODS_AT_START // 4):
                        if block == 1:
                            act.wait_ge(x_loaded, 16)
                            for c in range(DC):
                                square({**s, "sqslot": c % 2}, src, c, c, None)
                        for b in range(4):
                            multiply_mod_tile(4 * block, 0, b, 0, True)
                    split_hi(Tiles(0), 0)
                elif not s["fused"]:
                    for c in range(DC):
                        if s["norm"] == "ln":
                            act.wait_ge(centred, c + 1)
                        elif s["norm"] == "post":
                            act.wait_ge(evac, s["acc0"] + BANKS + 2 * (c + 1 - DC))
                        else:
                            act.wait_ge(xnew, s["xnew0"] + c + 1 - DC)
                            if s["layer"] == 2 and s["site"] == 0:
                                act.wait_ge(ctx2_loaded, 16)
                        square({**s, "sqslot": (s["sq0"] + c) % 2}, src, c, s["sq0"] + c, None)
                act.activation(WARM[:], ones[:, 0:1], ACT.Sqrt)
                act.wait_ge(recip_ready, s["rstd0"] + 1)
                act.activation(RST[:, 0:n], RST[:, 0:n], ACT.Sqrt).then_inc(rstd_ready, 1)
                if s["norm"] in ("mod", "ln"):
                    if s["norm"] == "mod":
                        act.wait_ge(vecs_ready, s["vecs0"] + 1)
                    for c in range(DC):
                        act.wait_ge(scaled, s["scaled0"] + c + 1)
                        if c >= 2:
                            act.wait_ge(operand_ready, s["operand0"] + c - 1)
                        if s["norm"] == "ln":
                            act.activation(AFF[:, c % 2, :], SCL[:, c % 2, :], ACT.Silu, scale=vec("ln_g", c),
                                           bias=vec("ln_b", c)).then_inc(affine, 1)
                            continue
                        shift = s["layer"] * MODC * 2 + (3 * s["site"]) * 2 * DC
                        for half in range(n // TOK):
                            at = slice(half * TOK, half * TOK + TOK)
                            mm = act.activation(AFF[:, c % 2, at], SCL[:, c % 2, at], ACT.Identity,
                                                scale=A_scale[:, 2 * c + half:2 * c + half + 1],
                                                bias=MOD[:, shift + 2 * c + half:shift + 2 * c + half + 1])
                        mm.then_inc(affine, 1)

            def dense_body(s, i, outs):
                t = Tiles(s["tile0"], i)
                for b in outs:
                    split_hi(t, b + 1)
                    if s["dense"] in ("pw2", "o", "wout"):
                        square({**s, "sqslot": (s["sq0"] + b) % 2}, Y_mix if s["dense"] == "wout" else X, 4 * i + b,
                               s["sq0"] + 4 * i + b, s["acc0"] + 4 * i + b + 1 + BANKS)

            def na_values():
                for c in range(DC):
                    act.wait_ge(vt_ready, c + 1)
                    act.activation(VV[:, :, c * P:(c + 1) * P],
                                   acc[:, AUX0 + c % 2, :].rearrange("p (k d) -> p k d", k=4), ACT.Copy).then_inc(v_copied, 1)

            def mix_projections(s):
                act.wait_ge(evac, s["acc0"] + BANKS)
                for dst, src in ((SCL[:, 0, :], CQ[:, 0, :]), (SCL[:, 1, :], CQ[:, 1, :]), (AFF[:, 0, :], CKV[:])):
                    act.activation(dst, src, ACT.Square).then_inc(lora_squared, 1)
                for i, r in enumerate((RST[:], AFF[:, 1, :])):
                    act.wait_ge(lora_recip, i + 1)
                    act.activation(r, r, ACT.Sqrt).then_inc(lora_rstd, 1)
                for j, (dst, src) in enumerate(mix_moves()):
                    act.wait_ge(proj_ready, j + 1)
                    act.activation(dst, src, ACT.Copy).then_inc(proj_moved, 1)
                act.wait_ge(rot_done, 1)
                for h in range(8):
                    act.activation(K96[64:96, h, :], KP[64:96, :], ACT.Copy).then_inc(kpe_spread, 1)

            def softmax_stage(s):
                SS, PX, PT, ST = soft[s["which"]]
                todo, u0 = units[s["which"]], s["unit0"]
                for u in range(len(todo) + 1):
                    if u < len(todo):
                        w, r = todo[u], u % 2
                        m = T2 - w["k0"] + (w["sink"] is not None)
                        act.wait_ge(nmax_ready, u0 + u + 1)
                        act.activation(PX[:, r, 0:m], SS[:, r, 0:m], ACT.Exp, bias=ST[:, r, 1:2],
                                       accum_out=ST[:, r, 2:3]).then_inc(exp_ready, 1)
                    if u >= 1:
                        m, r = T2 - todo[u - 1]["k0"], (u - 1) % 2
                        act.wait_ge(pt_ready, u0 + u)
                        if u >= 3:
                            act.wait_ge(o_ready, u0 + u - 2)
                        act.activation(PT[:, r, 0:m], acc[:, 2 + r, 0:m], ACT.Copy).then_inc(pt_copied, 1)

            def s5_stage(s):
                act.wait_ge(s5_loaded, 16 * 5)
                act.activation(SM[:, 0, :], SPAR[:, 2, :], ACT.Exp).then_inc(dt_ready, 1)
                act.wait_ge(rates_ready, 1)
                act.activation(SM[:, 3, :], SM[:, 2, :], ACT.Exp)
                act.activation(SM[:, 4, :], SM[:, 2, :], ACT.Exp, scale=-1.0).then_inc(mags_ready, 1)
                act.wait_ge(angles_ready, 1)
                act.activation(SM[:, 8:10, :], SM[:, 6:8, :], ACT.Sin).then_inc(sines_ready, 1)
                for c in range(DC):
                    act.wait_ge(u_turned, c + 1)
                    act.activation(UTOK[:, :, c * P:(c + 1) * P],
                                   acc[:, AUX0 + c % 2, :].rearrange("p (k d) -> p k d", k=4), ACT.Copy).then_inc(u_copied, 1)
                act.wait_ge(uch_loaded, 32)
                for b in range(8):
                    act.activation(UGT[:, 8 * b:8 * b + 8], UCH.rearrange("p t (g c) -> p g t c", c=GROUP)[:, 8 * b:8 * b + 8],
                                   ACT.Copy).then_inc(uch_sorted, 1)
                for b in range(8):
                    act.wait_ge(ug_turned, b + 1)
                    act.activation(UG[:, 8 * b:8 * b + 8, :],
                                   acc[:, AUX0 + b % 2, :].rearrange("p (g c) -> p g c", g=8), ACT.Copy).then_inc(ug_copied, 1)

                def store_states(j):
                    act.wait_ge(s_summed, j + 1)
                    half = CHUNKS // 2
                    src = acc[:, 2 + j % 2, 0:4 * CHUNKS].rearrange("p (d a c) -> p d a c", d=2, a=2)
                    for d, to, frm in ((0, slice(0, CHUNKS), slice(0, CHUNKS)),
                                       (1, slice(0, half), slice(half - 1, None, -1)),
                                       (1, slice(half, CHUNKS), slice(CHUNKS - 1, half - 1, -1))):
                        op = act.activation(S[:, to, :, 32 * d + j].rearrange("p c a -> p a c"), src[:, d, :, frm], ACT.Copy)
                    op.then_inc(s_stored, 1)

                for j in range(33):
                    if j < 32:
                        act.wait_ge(w_turned, j + 1)
                        if j >= 2:
                            act.wait_ge(s_summed, j - 1)
                        act.activation(WT[:, j % 2, :, :], acc[:, j % 2, :].rearrange("p (x m) -> p x m", x=4),
                                       ACT.Copy).then_inc(w_copied, 1)
                    if j >= 1:
                        store_states(j - 1)
                act.wait_ge(g_inner, 1)
                act.activation(YS[:], YS[:], ACT.Tanh, scale=float(np.sqrt(2 / np.pi))).then_inc(g_tanh, 1)
                for b in range(16):
                    act.wait_ge(yc_turned, b + 1)
                    act.activation(YC.rearrange("p t (g c) -> p g t c", c=GROUP)[:, 4 * b:4 * b + 4],
                                   acc[0:32, AUX0 + b % 2, :].rearrange("p (g t c) -> p g t c", g=4, t=SUB),
                                   ACT.Copy).then_inc(yc_copied, 1)

            for s in plan:
                if s["kind"] == "s5":
                    s5_stage(s)
                if s["kind"] == "norm":
                    norm_stage(s)
                elif s["kind"] == "pair":
                    if s["pair"] == "conv":
                        for i in range(s["pairs"] // 2):
                            pair_body(s, i, False, 0)
                        multiply_taps(s, DC - 1, 1)
                    else:
                        for i0, i1, mods, blk in pair_runs(s):
                            steps(act, s, i0, i1, lambda i: pair_body(s, i, mods, blk))
                elif s["kind"] == "down":
                    steps(act, s, 0, DC // 2, lambda i: down_body(s, i))
                elif s["kind"] == "dense":
                    steps(act, s, 0, s["outs"] // 4, lambda i: dense_body(s, i, range(4)))
                    if s["outs"] % 4:
                        dense_body(s, s["outs"] // 4, range(s["outs"] % 4))
                elif s["kind"] == "attention":
                    if s["which"] == "na":
                        na_values()
                    else:
                        mix_projections(s)
                    softmax_stage(s)

        @block.gpsimd
        def _(pool):
            pool.memset(ones[:], 1.0).then_inc(ones_set, 1)
            pool.dma_start(ident[:], io["ident"]).then_inc(ident_loaded, 16)

            def add_mod_terms(base, i, block=None):
                sums = mod_sums(block, 1)
                for b in range(4):
                    for h in range(2):
                        if b == 0 and h == 0:
                            continue
                        pool.wait_ge(mod_products, 2 * (base + 4 * i + b) + h + 1)
                        if b == 0:
                            sums_free(pool, base, i, block)
                            pool.tensor_tensor(sums, MT[:, 0, 0, :], MT[:, 0, 1, :], ALU.add).then_inc(mod_terms[1], 2)
                        else:
                            pool.wait_ge(mod_terms[1], 2 * (base + 4 * i + b) + h)
                            pool.tensor_tensor(sums, sums, MT[:, b % 2, h, :], ALU.add).then_inc(mod_terms[1], 1)

            for block in range(MODS_AT_START // 4):
                add_mod_terms(4 * block, 0, block)
            for s in plan:
                if s["kind"] == "pair" and s["pair"] == "conv":
                    for f in range(DC):
                        dst = CP[:, f % 2, :]
                        for n, _tap in [*taps_of(f, 0), *taps_of(f, 1)][1:]:
                            pool.wait_ge(tap_products, n + 1)
                            if n == f * SIDE_TAPS + 1:
                                if f >= 2:
                                    pool.wait_ge(conv_done, f - 1)
                                pool.tensor_tensor(dst, CM[:, (n - 1) % 4, :], CM[:, n % 4, :], ALU.add).then_inc(taps_added, 2)
                            else:
                                pool.wait_ge(taps_added, n)
                                pool.tensor_tensor(dst, dst, CM[:, n % 4, :], ALU.add).then_inc(taps_added, 1)
                if s["kind"] == "pair" and s["mods"]:
                    with pool.Fori(0, s["mods"] // 4) as i:
                        add_mod_terms(MODS_AT_START + s["mods0"], i)
                if s["kind"] == "norm":
                    n = s["n"]
                    src = source(s)
                    pool.wait_ge(rstd_ready, s["rstd0"] + 1)
                    for c in range(DC):
                        if c >= 2:
                            if s["norm"] in ("mod", "ln"):
                                pool.wait_ge(affine, s["affine0"] + c - 1)
                            else:
                                pool.wait_ge(xnew, s["xnew0"] + c - 1)
                        pool.tensor_tensor(SCL[:, c % 2, 0:n], src[:, c, 0:n], RST[:, 0:n], ALU.mult).then_inc(scaled, 1)
                    if s["norm"] == "mod" and s["layer"] == 0 and s["site"] == 1:
                        pool.memset(U[:, :, :, 0:TAPS // 2], 0.0)
                        pool.memset(U[:, :, :, PADW - TAPS // 2:PADW], 0.0).then_inc(margins_set, 1)
                if s["kind"] == "norm" and s["norm"] == "mod" and s["layer"] == 3 and s["site"] == 1:
                    for dst, name in ((SPAR, "s5_par"), (BC, "s5_bc"), (DSK, "s5_skip"), (MASK, "s5_mask"), (SM, "s5_zero")):
                        pool.dma_start(dst[:], io[name]).then_inc(s5_loaded, 16)
                if s["kind"] == "s5":
                    pool.wait_ge(u_copied, DC)
                    pool.dma_start(u_scratch.rearrange("(k p) d -> p k d", p=P), UTOK[:]).then_inc(u_stored, 16)
                    pool.wait_ge(u_stored, 16)
                    half = CHUNKS // 2
                    for rows, at in ((slice(0, half), slice(TOK, T2)), (slice(half, CHUNKS), slice(0, TOK))):
                        pool.dma_start(UCH[rows], u_scratch[at].rearrange("(c t) d -> c t d", t=SUB)).then_inc(uch_loaded, 16)
                    pool.wait_ge(e_ready, 8)
                    pool.wait_ge(w_turned, 32)
                    made = [0]

                    def link(ins):
                        made[0] += 1
                        ins.then_inc(pool_chain, 1)
                        pool.wait_ge(pool_chain, made[0])

                    for e in range(2):
                        for f in range(2):
                            for d in range(2):
                                s5_spread(pool, link, EE[f], range(4 * e, 4 * e + 4), 4 * e, d, 2 * f, f_ready)
                    pool.wait_ge(yc_copied, 16)
                    pool.dma_start(y_scratch.rearrange("(c t) d -> c t d", t=SUB), YC[:]).then_inc(y_stored, 16)
                    pool.wait_ge(y_stored, 16)
                    pool.dma_start(YTOK[:], y_scratch.rearrange("(k p) d -> p k d", p=P)).then_inc(ytok_loaded, 16)
                if s["kind"] == "norm" and s["norm"] == "mod" and s["layer"] == 2 and s["site"] == 1:
                    for dst, name in ((WUQ, "w_uq"), (WUKV, "w_ukv"), (ROT, "rot"), (TURN, "turn"), (BAND, "band")):
                        pool.dma_start(dst[:], io[name]).then_inc(mix_loaded, 16)
                if s["kind"] == "attention" and s["which"] == "na":
                    for u, unit in enumerate(units["na"]):
                        if u < 2:
                            pool.wait_ge(evac, s["acc0"] + BANKS)
                        else:
                            pool.wait_ge(s_moved, u - 1)
                        pool.dma_start(NB[:, u % 2, :], io["na_bias"][unit["h"], unit["qt"]]).then_inc(bias_loaded[u % 2], 16)
                if s["kind"] == "norm" and s["norm"] == "mod" and s["layer"] == 1 and s["site"] == 1:
                    pool.wait_ge(affine, s["affine0"] + DC)
                    pool.dma_start(X[:, :, TOK:T2], io["ctx_2"]).then_inc(ctx2_loaded, 16)
            pool.wait_ge(evac, totals["acc"] + BANKS)
            pool.wait_ge(xnew, totals["xnew"])
            pool.dma_start(out, X[:, :, 0:TOK]).then_inc(stored, 16)
            pool.wait_ge(stored, 16)

        @block.vector
        def _(dve):
            chain = [0]

            def link(ins):
                chain[0] += 1
                ins.then_inc(dve_chain, 1)
                dve.wait_ge(dve_chain, chain[0])

            dve.sem_inc(lo_ready, RAW)
            dve.sem_inc(evac, BANKS)

            def split_lo(t, b, width=TILE):
                if isinstance(t.step, int) and t.count(b) >= totals["tile"]:
                    return
                dve.wait_ge(hi_ready, t.count(b) + 1)
                dve.tensor_tensor(w_lo[:, t.split(b), 0:width], raw[:, t.raw(b), 0:width],
                                  w_hi[:, t.split(b), 0:width].bitcast(F32), ALU.subtract).then_inc(lo_ready, 1)

            dve.wait_ge(vec_loaded, 16)

            def add_mod_tile(base, i, b, blk, block=None):
                dve.wait_ge(modw_loaded[b % 2], 16 * (base // 2 + 2 * i + b // 2 + 1))
                sums = mod_sums(block, 0)
                for h in range(2):
                    rows, by = modw[:, b % 2, h * T2:(h + 1) * T2], mod_factor(blk, 0, 2 * b + h)
                    if b == 0 and h == 0:
                        sums_free(dve, base, i, block)
                        op = dve.tensor_scalar(sums, rows, by, None, ALU.mult)
                    else:
                        dve.wait_ge(mod_terms[0], 2 * (base + 4 * i + b) + h)
                        op = dve.scalar_tensor_tensor(out=sums, in0=rows, scalar=by, in1=sums, op0=ALU.mult, op1=ALU.add)
                    op.then_inc(mod_terms[0], 1)

            def take_mods(j0, n):
                dve.wait_ge(mods_summed, (j0 + n) // 4)
                link(dve.tensor_tensor(MOD[:, 2 * j0:2 * (j0 + n)], acc[:, MOD_BANK, 0:2 * n],
                                       V[:, VEC["mod_b"][0] + 2 * j0:VEC["mod_b"][0] + 2 * (j0 + n)], ALU.add))

            def statistics(s):
                n = s["n"]
                dve.wait_ge(sum_ready, s["sums0"] + (2 if s["norm"] == "ln" else 1))
                eps = LN_EPS if s["norm"] == "ln" else RMS_EPS
                link(dve.tensor_scalar(RST[:, 0:n], acc[:, SUM_BANK, 0:n], 1.0 / D, eps, ALU.mult, ALU.add))
                dve.reciprocal(RST[:, 0:n], RST[:, 0:n]).then_inc(recip_ready, 1)

            dve.wait_ge(silu_c_ready, 1)
            for block in range(MODS_AT_START // 4):
                if block == 2:
                    statistics(plan[0])
                for b in range(4):
                    add_mod_tile(4 * block, 0, b, 0, block)
            take_mods(0, MODS_AT_START)
            split_lo(Tiles(0), 0)

            def convolve(f, half):
                dst = CO[:, f, :].rearrange("p (s t) -> p s t", s=2)
                taps = TAPS - SIDE_TAPS
                for tap in (range(taps // 2), range(taps // 2, taps))[half]:
                    src = U[:, f, :, tap:tap + TOK]
                    w = vec("w_dw", f * TAPS + tap)
                    if tap == 0:
                        link(dve.tensor_scalar(dst, src, w, vec("b_dw", f), ALU.mult, ALU.add))
                    else:
                        link(dve.scalar_tensor_tensor(out=dst, in0=src, scalar=w, in1=dst, op0=ALU.mult, op1=ALU.add))
                if half:
                    dve.wait_ge(taps_added, (f + 1) * SIDE_TAPS)
                    dve.tensor_tensor(CO[:, f, :], CO[:, f, :], CP[:, f % 2, :], ALU.add).then_inc(conv_done, 1)

            def pair_body(s, i, mods=False, blk=0):
                n = s["n"]
                t = Tiles(s["tile0"], i)
                for b in range(4):
                    split_lo(t, b + 1)
                    if mods:
                        add_mod_tile(MODS_AT_START + s["mods0"], i, b, blk)
                    if s["pair"] == "conv":
                        if b % 2 == 0:
                            if 2 * i + b:
                                convolve(2 * i + b // 2 - 1, 1)
                            continue
                    elif b < 2:
                        continue
                    else:
                        b = (1, 3)[b - 2]
                    f = 2 * i + b // 2
                    dve.wait_ge(silu_ready, s["silu0"] + f + 1)
                    dve.wait_ge(tile_done, t.count(b) + 1 + SPLIT)
                    up = acc[:, (s["acc0"] + b) % BANKS, 0:n]
                    part = SCL[:, b // 2, 0:n]
                    if s["pair"] == "ffn":
                        dve.tensor_tensor(AFF[:, b // 2, 0:n], part, up, ALU.mult).then_inc(evac, 2)
                        dve.wait_ge(evac, s["acc0"] + 2 * f + 2 + BANKS)
                        dve.tensor_copy(H_hi[:, f, 0:n], AFF[:, b // 2, 0:n]).then_inc(h_ready, 1)
                        dve.wait_ge(h_ready, 2 * (s["h0"] + f) + 1)
                        dve.tensor_tensor(H_lo[:, f, 0:n], AFF[:, b // 2, 0:n], H_hi[:, f, 0:n].bitcast(F32),
                                          ALU.subtract).then_inc(h_ready, 1)
                    elif s["pair"] == "conv":
                        dve.scalar_tensor_tensor(
                            out=U[:, f, :, TAPS // 2:TAPS // 2 + TOK], in0=up.rearrange("p (s t) -> p s t", s=2),
                            scalar=vec("b_pw1", f), in1=part.rearrange("p (s t) -> p s t", s=2),
                            op0=ALU.add, op1=ALU.mult).then_inc(evac, 2)
                        dve.wait_ge(evac, s["acc0"] + 2 * f + 2 + BANKS)
                        convolve(f, 0)
                    else:
                        dve.tensor_tensor(Y_mix[:, f, 0:n], up, part, ALU.mult).then_inc(evac, 2)

            def add_gated(dst_c, bank, n):
                for half in range(n // TOK):
                    at = slice(half * TOK, half * TOK + TOK)
                    yield dve.scalar_tensor_tensor(out=X[:, dst_c, at], in0=acc[:, bank, at],
                                                   scalar=GATE_col(dst_c, half), in1=X[:, dst_c, at],
                                                   op0=ALU.mult, op1=ALU.add)

            def GATE_col(c, half):
                return GATE[:, bass.ds(2 * c + half, 1)]

            def down_body(s, i):
                n = s["n"]
                for o in range(2):
                    t = Tiles(s["tile0"] + 4 * o, 2 * i)
                    for b in range(4):
                        split_lo(t, b + 1, TILE if b == 3 else DOWN_PARTS[b + 1] * P)
                    c = 2 * i + o
                    dve.wait_ge(tile_done, t.count(3) + 1 + SPLIT)
                    bank = (s["acc0"] + o) % 2
                    if s["post"]:
                        dve.tensor_copy(Y_ffn[:, c, 0:n], acc[:, bank, 0:n]).then_inc(evac, 1)
                    else:
                        *_, last = list(add_gated(c, bank, n))
                        last.then_inc(evac, 1)

            def norm_stage(s):
                n = s["n"]
                dve.wait_ge(evac, s["acc0"] + BANKS)
                if s["xnew0"]:
                    dve.wait_ge(xnew, s["xnew0"])
                if s["norm"] == "mod":
                    base = s["layer"] * MODC * 2 + 3 * s["site"] * 2 * DC
                    g = vec(f"g{s['layer']}{s['site']}", 0, 2 * DC)
                    dve.scalar_tensor_tensor(out=A_scale[:], in0=MOD[:, base + 2 * DC:base + 4 * DC], scalar=1.0,
                                             in1=g, op0=ALU.add, op1=ALU.mult).then_inc(vecs_ready, 1)
                    gate = MOD[:, base + 4 * DC:base + 6 * DC]
                    half = 1.0 if s["site"] == 1 else 0.5
                    if s["layer"] < 2:
                        link(dve.tensor_scalar(GATE[:], gate, half, None, ALU.mult))
                    else:
                        link(dve.scalar_tensor_tensor(out=GATE[:], in0=gate, scalar=half,
                                                      in1=vec(f"gpost{s['layer']}{s['site']}", 0, 2 * DC),
                                                      op0=ALU.mult, op1=ALU.mult))
                if s["norm"] == "ln":
                    dve.wait_ge(sum_ready, s["sums0"] + 1)
                    link(dve.tensor_scalar(MU[:, 0:n], acc[:, SUM_BANK, 0:n], 1.0 / D, None, ALU.mult))
                    for c in range(DC):
                        dve.tensor_tensor(CO[:, c, :], CO[:, c, :], MU[:], ALU.subtract).then_inc(centred, 1)
                if s is not plan[0]:
                    statistics(s)
                for c in range(DC):
                    if s["norm"] in ("mod", "ln"):
                        dve.wait_ge(affine, s["affine0"] + c + 1)
                        link(dve.tensor_copy(A_hi[:, c, 0:n], AFF[:, c % 2, 0:n]))
                        dve.tensor_tensor(A_lo[:, c, 0:n], AFF[:, c % 2, 0:n], A_hi[:, c, 0:n].bitcast(F32),
                                          ALU.subtract).then_inc(operand_ready, 1)
                    elif s["norm"] == "final":
                        dve.wait_ge(scaled, s["scaled0"] + c + 1)
                        dve.tensor_scalar(X[:, c, 0:n], SCL[:, c % 2, 0:n], vec("final_g", c), None,
                                          ALU.mult).then_inc(xnew, 1)
                    else:
                        dve.wait_ge(scaled, s["scaled0"] + c + 1)
                        for half in range(n // TOK):
                            at = slice(half * TOK, half * TOK + TOK)
                            op = dve.scalar_tensor_tensor(out=X[:, c, at], in0=SCL[:, c % 2, at],
                                                          scalar=GATE[:, 2 * c + half:2 * c + half + 1],
                                                          in1=X[:, c, at], op0=ALU.mult, op1=ALU.add)
                        op.then_inc(xnew, 1)

            def dense_body(s, i, outs):
                n = s["n"]
                t = Tiles(s["tile0"], i)
                for b in outs:
                    split_lo(t, b + 1)
                    c = 4 * i + b
                    dve.wait_ge(tile_done, t.count(b) + 1 + SPLIT)
                    bank = (s["acc0"] + b) % BANKS
                    what = s["dense"]
                    if what in ("pw2", "o"):
                        bias = "b_pw2" if what == "pw2" else "b_o"
                        for half in range(n // TOK):
                            at = slice(half * TOK, half * TOK + TOK)
                            op = dve.tensor_scalar(AFF[:, b % 2, at], acc[:, bank, at], vec(bias, c), GATE_col(c, half),
                                                   ALU.add, ALU.mult)
                        op.then_inc(biased, 1)
                        dve.wait_ge(biased, s["biased0"] + 4 * i + b + 1)
                        dve.tensor_tensor(X[:, c, 0:n], X[:, c, 0:n], AFF[:, b % 2, 0:n], ALU.add).then_inc(evac, 1)
                    elif what == "qkv":
                        dst = (Q, K, VT)[i // 2]
                        m = TOK if i // 2 == 0 else T2
                        dve.tensor_scalar(dst[:, c % DC, 0:m], acc[:, bank, 0:m], vec("b_qkv", c), None,
                                          ALU.add).then_inc(evac, 1)
                    elif what == "s5in":
                        dve.tensor_copy(UT[:, c, :], acc[:, bank, :]).then_inc(evac, 1)
                    elif what == "win":
                        dst = (CQ[:, 0, :], CQ[:, 1, :], CKV[:], KP[:], QS[:, 0, :], QS[:, 1, :], QS[:, 2, :],
                               QS[:, 3, :], KS[:], VST[:])[c]
                        dve.tensor_copy(dst, acc[:, bank, :]).then_inc(evac, 1)
                    elif what == "wout":
                        dve.tensor_copy(Y_mix[:, c, 0:n], acc[:, bank, 0:n]).then_inc(evac, 1)

            def mix_norms(s):
                dve.wait_ge(evac, s["acc0"] + BANKS)
                for i, (r, bank, width) in enumerate(((RST[:], SUM_BANK, 2 * P), (AFF[:, 1, :], AUX0, P))):
                    dve.wait_ge(lora_summed, i + 1)
                    link(dve.tensor_scalar(r, acc[:, bank, :], 1.0 / width, RMS_EPS, ALU.mult, ALU.add))
                    dve.reciprocal(r, r).then_inc(lora_recip, 1)
                for i, (dst, g, r) in enumerate(((CQ[:, 0, :], vec("q_norm", 0), RST[:]), (CQ[:, 1, :], vec("q_norm", 1), RST[:]),
                                                 (CKV[:], vec("kv_norm"), AFF[:, 1, :]))):
                    dve.wait_ge(lora_rstd, 1 + i // 2)
                    dve.scalar_tensor_tensor(out=dst, in0=dst, scalar=g, in1=r, op0=ALU.mult, op1=ALU.mult).then_inc(lora_ready, 1)

            def mix_rotations():
                dve.wait_ge(mix_loaded, 16 * 5)
                for j, (x, which, bank, rows) in enumerate(rotations()):
                    dve.wait_ge(rot_ready, j + 1)
                    link(dve.tensor_tensor(AFF[0:rows, 0, 0:TOK], acc[0:rows, bank, 0:TOK], ROT[0:rows, 2 * which + 1, :], ALU.mult))
                    link(dve.tensor_tensor(x, x, ROT[0:rows, 2 * which, :], ALU.mult))
                    dve.tensor_tensor(x, x, AFF[0:rows, 0, 0:TOK], ALU.add).then_inc(rot_done, 1)
                    dve.wait_ge(rot_done, j + 1)

            def product(out_re, out_im, a, b, t1, t2, sign=1.0):
                link(dve.tensor_tensor(t1, a[0], b[0], ALU.mult))
                link(dve.tensor_tensor(t2, a[1], b[1], ALU.mult))
                link(dve.tensor_tensor(out_re, t1, t2, ALU.subtract))
                link(dve.tensor_tensor(t1, a[0], b[1], ALU.mult))
                link(dve.tensor_tensor(t2, a[1], b[0], ALU.mult))
                if sign > 0:
                    link(dve.tensor_tensor(out_im, t1, t2, ALU.add))
                else:
                    link(dve.scalar_tensor_tensor(out=out_im, in0=t1, scalar=-1.0, in1=t2, op0=ALU.mult, op1=ALU.subtract))

            def s5_discretise():
                dve.wait_ge(s5_loaded, 16 * 5)
                dt, lr, x, mag, inv, li, angle, lean, sine, cosine, den, spare = (SM[:, i, :] for i in range(12))
                link(dve.tensor_scalar(lr, SPAR[:, 0, :], -1e-4, None, ALU.min))
                dve.wait_ge(dt_ready, 1)
                dve.tensor_tensor(x, lr, dt, ALU.mult).then_inc(rates_ready, 1)
                li = SPAR[:, 1, :]
                link(dve.tensor_tensor(SM[:, 5, :], li, dt, ALU.mult))

                def reduce(dst, src, shift):
                    if shift:
                        link(dve.tensor_scalar(dst, src, shift, None, ALU.add))
                        src = dst
                    link(dve.tensor_scalar(spare, src, 1 / (2 * np.pi), 1.5 * 2.0 ** 23, ALU.mult, ALU.add))
                    link(dve.tensor_scalar(spare, spare, 1.5 * 2.0 ** 23, None, ALU.subtract))
                    for part in (6.28125, 0.0019350051879882812, 3.0199159819567e-07):
                        link(dve.scalar_tensor_tensor(out=dst, in0=spare, scalar=-part, in1=src, op0=ALU.mult, op1=ALU.add))
                        src = dst

                reduce(angle, SM[:, 5, :], 0.0)
                reduce(lean, angle, float(np.pi / 2))
                dve.tensor_scalar(SM[:, 6:8, :], SM[:, 6:8, :], 3.1415925, -3.1415925, ALU.min, ALU.max).then_inc(angles_ready, 1)
                dve.wait_ge(sines_ready, 1)
                dve.wait_ge(mags_ready, 1)
                link(dve.memset(PW[:, 0:4:2, 0, :], 1.0))
                link(dve.memset(PW[:, 1:4:2, 0, :], 0.0))
                link(dve.tensor_tensor(PW[:, 0, 1, :], mag, cosine, ALU.mult))
                link(dve.tensor_tensor(PW[:, 1, 1, :], mag, sine, ALU.mult))
                link(dve.tensor_tensor(PW[:, 2, 1, :], inv, cosine, ALU.mult))
                link(dve.scalar_tensor_tensor(out=PW[:, 3, 1, :], in0=inv, scalar=-1.0, in1=sine, op0=ALU.mult, op1=ALU.mult))
                t1, t2 = AFF[:].rearrange("p a b -> p (a b)"), SCL[:].rearrange("p a b -> p (a b)")
                for part in (0, 2):
                    for k, n in ((1, 1), (2, 2), (4, 4)):
                        at = slice(k + 1, k + n + 1)
                        one = [PW[:, part + i, 1:n + 1, :] for i in range(2)]
                        two = [PW[:, part + i, k:k + 1, :].broadcast_to([P, n, COLS]) for i in range(2)]
                        v1, v2 = (t[:, 0:n * COLS].rearrange("p (n c) -> p n c", n=n) for t in (t1, t2))
                        product(PW[:, part, at, :], PW[:, part + 1, at, :], one, two, v1, v2)
                link(dve.tensor_copy(A8[:, 0, 0, :], PW[:, 0, 8, :]))
                link(dve.tensor_copy(A8[:, 0, 1, :], PW[:, 0, 8, :]))
                link(dve.tensor_scalar(A8[:, 1, 0, :], PW[:, 1, 8, :], -1.0, None, ALU.mult))
                link(dve.tensor_copy(A8[:, 1, 1, :], PW[:, 1, 8, :]))
                for i in range(4):
                    link(dve.tensor_copy(EP[:, i, 0:32, :], PW[:, i, 7::-1, 0:32].rearrange("p t c -> p c t")))
                    link(dve.tensor_copy(EP[:, i, 32:64, :], PW[:, i, 0:8, 32:64].rearrange("p t c -> p c t")))
                a_re, a_im = PW[:, 0, 1, :], PW[:, 1, 1, :]
                f_re, f_im = SM[:, 6, :], SM[:, 7, :]
                nr, u1, u2 = SM[:, 8, :], SM[:, 9, :], SM[:, 11, :]
                link(dve.tensor_tensor(u1, lr, lr, ALU.mult))
                link(dve.tensor_tensor(u2, li, li, ALU.mult))
                link(dve.tensor_tensor(den, u1, u2, ALU.add))
                link(dve.reciprocal(den, den))
                link(dve.tensor_scalar(nr, a_re, -1.0, None, ALU.add))
                link(dve.tensor_tensor(u1, nr, lr, ALU.mult))
                link(dve.tensor_tensor(u2, a_im, li, ALU.mult))
                link(dve.tensor_tensor(f_re, u1, u2, ALU.add))
                link(dve.tensor_tensor(f_re, f_re, den, ALU.mult))
                link(dve.tensor_tensor(u1, a_im, lr, ALU.mult))
                link(dve.tensor_tensor(u2, nr, li, ALU.mult))
                link(dve.tensor_tensor(f_im, u1, u2, ALU.subtract))
                link(dve.tensor_tensor(f_im, f_im, den, ALU.mult))
                fs = [f.rearrange("p (c o) -> p c o", o=1).broadcast_to([P, COLS, GROUP]) for f in (f_re, f_im)]
                v1, v2 = (t.rearrange("p (c h) -> p c h", c=COLS) for t in (t1, t2))
                v3 = PW[:].rearrange("p a b c -> p (a b c)")[:, 0:COLS * GROUP].rearrange("p (c h) -> p c h", c=COLS)
                b_re, b_im = BC[:, 0], BC[:, 1]
                link(dve.tensor_tensor(v1, b_re, fs[0], ALU.mult))
                link(dve.tensor_tensor(v2, b_im, fs[1], ALU.mult))
                link(dve.tensor_tensor(v3, b_re, fs[1], ALU.mult))
                link(dve.tensor_tensor(b_re, v1, v2, ALU.subtract))
                link(dve.tensor_tensor(v2, b_im, fs[0], ALU.mult))
                link(dve.tensor_tensor(b_im, v3, v2, ALU.add))

            def s5_output_part(e, part):
                if part == 0:
                    dve.wait_ge(y_pair_done, 4 * (e - 1))
                f, d = divmod(part, 2)
                s5_spread(dve, link, EE[f], range(4 * e, 4 * e + 4), 4 * (e % 2), d, 2 * f, f_ready)

            def s5_take_outputs(q):
                dve.wait_ge(y_pair_done, 8 * q + 8)
                at = slice(16 * q, 16 * q + 16)
                skip = DSK[:, at].rearrange("p (g o) -> p g o", o=1).broadcast_to([P, 16, CHUNKS // 2])
                link(dve.tensor_tensor(YS[:, at], UG[:, at, CHUNKS // 2:CHUNKS], skip, ALU.mult))
                for g2 in range(2):
                    at = slice(16 * q + g2, 16 * q + 16, 2)
                    dve.tensor_tensor(YG[:, at], acc[:, 2 + 2 * (q % 2) + g2, 0:TOK].rearrange("p (g c) -> p g c", g=8),
                                      YS[:, at], ALU.add).then_inc(y_taken, 1)

            def s5_stage(s):
                dve.wait_ge(evac, s["acc0"] + BANKS)
                s5_discretise()
                dve.wait_ge(ug_copied, 8)
                for q in range(4):
                    if q >= 2:
                        dve.wait_ge(w_turned, 8 * (q - 1))
                    for d in range(2):
                        s5_spread(dve, link, EE[q % 2], range(8 * q, 8 * q + 8), 0, d, 0, e_ready)
                dve.wait_ge(s_stored, 32)
                M1, M2 = (SM[:, 2 * i:2 * i + 2, :] for i in range(2))

                def scan_step_of(k, at):
                    dve.tensor_tensor(M1, S[:, k - 1], A8[:, 0], ALU.mult).then_inc(scan_step, 1)
                    dve.tensor_tensor(M2[:, 0], S[:, k - 1, 1], A8[:, 1, 0], ALU.mult).then_inc(scan_step, 1)
                    dve.tensor_tensor(M2[:, 1], S[:, k - 1, 0], A8[:, 1, 1], ALU.mult).then_inc(scan_step, 1)
                    dve.wait_ge(scan_step, 5 * k - 2)
                    dve.tensor_tensor(TT[:, at], M1, M2, ALU.add).then_inc(scan_step, 1)
                    dve.wait_ge(scan_step, 5 * k - 1)
                    dve.tensor_tensor(S[:, k], S[:, k], TT[:, at], ALU.add).then_inc(scan_step, 1)
                    dve.wait_ge(scan_step, 5 * k)

                half, run = CHUNKS // 2, 8
                for k in range(1, run):
                    scan_step_of(k, 0)
                with dve.Fori(1, half // run) as i:
                    for x in range(run):
                        scan_step_of(run * i + x, 0)
                with dve.Fori(0, half // run) as i:
                    for x in range(run):
                        scan_step_of(run * i + x + half, run * i + x)
                dve.wait_ge(f_ready, 8)
                for j in range(32):
                    e = j // 4
                    dve.wait_ge(d_summed, j + 1)
                    if j:
                        dve.wait_ge(d_ready, j)
                    link(dve.tensor_tensor(DM.rearrange("p g d m -> p g (d m)"),
                                           acc[:, (0, AUX0)[j % 2]:(0, AUX0)[j % 2] + 2, 0:2 * P],
                                           MASK[:].rearrange("p (o d) m -> p o (d m)", o=1).broadcast_to([P, 2, 2 * P]), ALU.mult))
                    if j >= 2:
                        dve.wait_ge(y_pair_done, j - 1)
                    dve.tensor_tensor(DD[:, j % 2], DM[:, :, 0, :], DM[:, :, 1, :], ALU.add).then_inc(d_ready, 1)
                    if 1 <= e < 7:
                        s5_output_part(e + 1, j % 4)
                    if j % 8 == 1 and j > 1:
                        s5_take_outputs(j // 8 - 1)
                s5_take_outputs(3)
                dve.wait_ge(y_taken, 8)
                link(dve.tensor_tensor(YS[:], YG[:], YG[:], ALU.mult))
                link(dve.tensor_scalar(YS[:], YS[:], 0.044715, 1.0, ALU.mult, ALU.add))
                dve.tensor_tensor(YS[:], YS[:], YG[:], ALU.mult).then_inc(g_inner, 1)
                dve.wait_ge(g_tanh, 1)
                link(dve.tensor_scalar(YS[:], YS[:], 1.0, 0.5, ALU.add, ALU.mult))
                dve.tensor_tensor(YG[:], YG[:], YS[:], ALU.mult).then_inc(g_done, 1)
                for c in range(DC):
                    dve.wait_ge(y_turned, c + 1)
                    src = acc[:, c % 2, 0:TOK]
                    link(dve.tensor_copy(A_hi[:, c, 0:TOK], src))
                    dve.tensor_tensor(A_lo[:, c, 0:TOK], src, A_hi[:, c, 0:TOK].bitcast(F32),
                                      ALU.subtract).then_inc(operand_ready, 1)

            def softmax_stage(s):
                SS, PX, PT, ST = soft[s["which"]]
                todo, u0 = units[s["which"]], s["unit0"]
                per = len(todo) // DC
                for u in range(len(todo) + 1):
                    if u < len(todo):
                        w, r = todo[u], u % 2
                        m = T2 - w["k0"]
                        dve.wait_ge(s_scored, u0 + u + 1)
                        if u >= 2:
                            dve.wait_ge(exp_ready, u0 + u - 1)
                        if w["bias"] is None:
                            op = dve.tensor_scalar(SS[:, r, 0:m], acc[:, r, 0:m], w["scale"], None, ALU.mult)
                        else:
                            if w["bias"] == "loaded":
                                dve.wait_ge(bias_loaded[r], 16 * (u // 2 + 1))
                                bias = NB[:, r, :]
                            else:
                                bias = w["bias"]
                            dve.scalar_tensor_tensor(out=SS[:, r, 0:TOK], in0=acc[:, r, 0:TOK], scalar=w["scale"],
                                                     in1=bias, op0=ALU.mult, op1=ALU.add)
                            op = dve.tensor_scalar(SS[:, r, TOK:T2], acc[:, r, TOK:T2], w["scale"], None, ALU.mult)
                        op.then_inc(s_moved, 1)
                        if w["sink"] is not None:
                            link(dve.tensor_copy(SS[:, r, m:m + 1], vec("sink", w["sink"])))
                            m += 1
                        dve.wait_ge(s_moved, u0 + u + 1)
                        link(dve.tensor_reduce(ST[:, r, 0:1], SS[:, r, 0:m], AX.X, ALU.max))
                        dve.tensor_scalar(ST[:, r, 1:2], ST[:, r, 0:1], -1.0, None, ALU.mult).then_inc(nmax_ready, 1)
                    if u >= 1:
                        v, r = u - 1, (u - 1) % 2
                        m = T2 - todo[v]["k0"]
                        dve.wait_ge(exp_ready, u0 + v + 1)
                        link(dve.reciprocal(ST[:, r, 3:4], ST[:, r, 2:3]))
                        dve.tensor_scalar(PX[:, r, 0:m], PX[:, r, 0:m], ST[:, r, 3:4], None, ALU.mult).then_inc(p_ready, 1)
                        dve.wait_ge(p_ready, u0 + v + 1)
                    if u >= per + 2 and (u - 2) % per == 0 or u == len(todo):
                        pair = (u - per - 2) // per if u < len(todo) else DC - 1
                        n = per // 2 * P
                        dve.wait_ge(o_ready, u0 + per * (pair + 1))
                        src = acc[:, AUX0 + pair % 2, 0:n]
                        link(dve.tensor_copy(A_hi[:, pair, 0:n], src))
                        dve.tensor_tensor(A_lo[:, pair, 0:n], src, A_hi[:, pair, 0:n].bitcast(F32),
                                          ALU.subtract).then_inc(operand_ready, 1)

            for s in plan:
                if s["kind"] == "s5":
                    s5_stage(s)
                if s["kind"] == "norm":
                    norm_stage(s)
                elif s["kind"] == "pair":
                    if s["pair"] == "conv":
                        dve.wait_ge(margins_set, 1)
                        for i in range(s["pairs"] // 2):
                            pair_body(s, i)
                        convolve(DC - 1, 1)
                    else:
                        for i0, i1, mods, blk in pair_runs(s):
                            steps(dve, s, i0, i1, lambda i: pair_body(s, i, mods, blk))
                    if s["mods"]:
                        take_mods(MODS_AT_START + s["mods0"], s["mods"])
                elif s["kind"] == "down":
                    steps(dve, s, 0, DC // 2, lambda i: down_body(s, i))
                elif s["kind"] == "dense":
                    if s["dense"] in ("pw2", "o", "wout"):
                        steps(dve, s, 0, s["outs"] // 4, lambda i: dense_body(s, i, range(4)))
                    else:
                        for i in range(s["outs"] // 4):
                            dense_body(s, i, range(4))
                        if s["outs"] % 4:
                            dense_body(s, s["outs"] // 4, range(s["outs"] % 4))
                elif s["kind"] == "attention":
                    if s["which"] == "mix":
                        mix_norms(s)
                        mix_rotations()
                    softmax_stage(s)

        @block.tensor
        def _(pe):
            pe.sem_inc(tile_done, SPLIT)
            pe.sem_inc(sq_used, 2)

            def add_up_mods(block, i, col, place=None):
                for terms in mod_terms:
                    pe.wait_ge(terms, 8 * (block + i + 1))
                for m in range(4):
                    for stream in range(2):
                        mm = pe.matmul(acc[:, MOD_BANK, bass.ds(col + 2 * m + stream, 1)],
                                       mod_sums(place, stream)[:, m * P:(m + 1) * P], ones[:, 0:1], start=True, stop=True)
                mm.then_inc(mods_summed, 1)

            def products(t, b, hi, lo, n, blocks, bank, first, last, waits=None):
                pe.wait_ge(lo_ready, t.count(b) + 1 + RAW)
                slot = t.split(b)
                for x, k in enumerate(blocks):
                    if waits is not None and waits(k) is not None:
                        pe.wait_ge(*waits(k))
                    wh, wl = (w[:, slot, x * P:(x + 1) * P] for w in (w_hi, w_lo))
                    dst = acc[:, bank, 0:n]
                    pe.matmul(dst, wh, hi[:, k, 0:n], start=(first and x == 0), stop=False)
                    pe.matmul(dst, wh, lo[:, k, 0:n], start=False, stop=False)
                    mm = pe.matmul(dst, wl, hi[:, k, 0:n], start=False, stop=(last and x == len(blocks) - 1))
                mm.then_inc(tile_done, 1)

            def operand_wait(s):
                return lambda k: (operand_ready, s["operand0"] + k + 1 - DC)

            def pair_body(s, i, mods):
                t = Tiles(s["tile0"], i)
                for b in range(4):
                    pe.wait_ge(evac, s["acc0"] + 4 * i + b + 1)
                    products(t, b, A_hi, A_lo, s["n"], range(DC), (s["acc0"] + b) % BANKS, True, True,
                             operand_wait(s) if b == 0 else None)
                if mods:
                    add_up_mods((MODS_AT_START + s["mods0"]) // 4, i, 8 * i)

            def add_square(s, k, slot, first, last):
                pe.wait_ge(sq_ready, k + 1)
                n = s["n"]
                mm = pe.matmul(acc[:, SUM_BANK, 0:n], ones[:], SQ[:, slot, 0:n], start=first, stop=last)
                if last:
                    mm.then_inc(sum_ready, 1)
                else:
                    mm.then_inc(sq_used, 1)

            def down_body(s, i, first):
                for o in range(2):
                    t = Tiles(s["tile0"] + 4 * o, 2 * i)
                    bank = (s["acc0"] + o) % 2
                    pe.wait_ge(evac, s["acc0"] + 2 * i + o + 1 + 2)
                    for b in range(4):
                        h = 2 * s["h0"]

                        def waits(k):
                            return (h_ready, h - 2 * FC + 2 * (k + 1)) if k >= FC - 2 and o == 0 else (
                                (h_ready, h - 4) if k == 0 and o == 0 else None)
                        products(t, b, H_hi, H_lo, s["n"], range(DOWN_AT[b], DOWN_AT[b] + DOWN_PARTS[b]), bank,
                                 b == 0, b == 3, waits)
                        if b == 1 and not (first and o == 0):
                            add_square(s, s["sq0"] + 2 * i + o - 1, (s["sq0"] + o - 1) % 2, first and o == 1, False)

            def dense_body(s, i, outs, first=False):
                t = Tiles(s["tile0"], i)
                for b in outs:
                    pe.wait_ge(evac, s["acc0"] + 4 * i + b + 1)
                    m = s["n"]
                    if s["dense"] == "qkv" and i in (0, 1):
                        m = TOK
                    products(t, b, A_hi, A_lo, m, range(DC), (s["acc0"] + b) % BANKS, True, True,
                             operand_wait(s) if b == 0 else None)
                    if s["dense"] in ("pw2", "o", "wout") and not (first and b == 0):
                        add_square(s, s["sq0"] + 4 * i + b - 1, (s["sq0"] + b - 1) % 2, first and b == 1, False)

            def norm_stage(s):
                src = source(s)
                n = s["n"]
                if s["norm"] == "ln":
                    pe.wait_ge(conv_done, DC)
                    for c in range(DC):
                        mm = pe.matmul(acc[:, SUM_BANK, 0:n], ones[:], src[:, c, 0:n], start=(c == 0), stop=(c == DC - 1))
                    mm.then_inc(sum_ready, 1)
                if s["fused"]:
                    add_square(s, s["sq0"] + DC - 1, (s["sq0"] + DC - 1) % 2, False, True)
                    pe.sem_inc(sq_used, 1)
                else:
                    for c in range(DC):
                        add_square(s, s["sq0"] + c, (s["sq0"] + c) % 2, c == 0, c == DC - 1)
                    pe.sem_inc(sq_used, 1)

            def na_values(s):
                pe.wait_ge(evac, s["acc0"] + BANKS)
                pe.wait_ge(ident_loaded, 16)
                for c in range(DC):
                    if c >= 2:
                        pe.wait_ge(v_copied, c - 1)
                    for k in range(4):
                        mm = pe.transpose(acc[:, AUX0 + c % 2, k * P:(k + 1) * P], VT[:, c, k * P:(k + 1) * P], ident[:])
                    mm.then_inc(vt_ready, 1)
                pe.wait_ge(v_copied, DC)

            def mix_projections(s):
                pe.wait_ge(mix_loaded, 16 * 5)
                for i, (src, bank, first, last) in enumerate(((SCL[:, 0, :], SUM_BANK, True, False),
                                                              (SCL[:, 1, :], SUM_BANK, False, True),
                                                              (AFF[:, 0, :], AUX0, True, True))):
                    pe.wait_ge(lora_squared, i + 1)
                    mm = pe.matmul(acc[:, bank, :], ones[:], src, start=first, stop=last)
                    if last:
                        mm.then_inc(lora_summed, 1)
                for k in range(4):
                    mm = pe.transpose(acc[:, 0, k * P:(k + 1) * P], VST[:, k * P:(k + 1) * P], ident[:])
                mm.then_inc(proj_ready, 1)
                pe.wait_ge(lora_ready, 2)
                for h in range(8):
                    j = 1 + h
                    if j >= 4:
                        pe.wait_ge(proj_moved, j - 3)
                    for k in range(2):
                        mm = pe.matmul(acc[0:96, j % 4, :], WUQ[:, k, h * 96:(h + 1) * 96], CQ[:, k, :],
                                       start=(k == 0), stop=(k == 1))
                    mm.then_inc(proj_ready, 1)
                pe.wait_ge(lora_ready, 3)
                for h in range(8):
                    j = 9 + h
                    pe.wait_ge(proj_moved, j - 3)
                    pe.matmul(acc[0:64, j % 4, :], WUKV[:, h * 64:(h + 1) * 64], CKV[:], start=True,
                              stop=True).then_inc(proj_ready, 1)
                for k in range(4):
                    j = 17 + k
                    pe.wait_ge(proj_moved, j - 3)
                    pe.matmul(acc[:, j % 4, :], CKV[:, k * P:(k + 1) * P], WUKV[:, 512:1024], start=True,
                              stop=True).then_inc(proj_ready, 1)
                pe.wait_ge(proj_moved, 21)
                for j, (x, which, bank, rows) in enumerate(rotations()):
                    if j >= 2:
                        pe.wait_ge(rot_done, j - 1)
                    pe.matmul(acc[0:rows, bank, 0:TOK], TURN[0:rows, which, 0:rows], x, start=True,
                              stop=True).then_inc(rot_ready, 1)
                pe.wait_ge(rot_done, 14)
                pe.wait_ge(kpe_spread, 8)

            def softmax_stage(s):
                SS, PX, PT, ST = soft[s["which"]]
                todo, u0 = units[s["which"]], s["unit0"]
                per = len(todo) // DC
                for u in range(-1, len(todo) + 2):
                    if u + 1 < len(todo):
                        w = todo[u + 1]
                        if u >= 1:
                            pe.wait_ge(s_moved, u0 + u)
                        pe.matmul(acc[:, (u + 1) % 2, 0:T2 - w["k0"]], w["q"], w["k"], start=True,
                                  stop=True).then_inc(s_scored, 1)
                    if 1 <= u <= len(todo):
                        v, r = u - 1, (u - 1) % 2
                        pe.wait_ge(p_ready, u0 + v + 1)
                        if v >= 2:
                            pe.wait_ge(pt_copied, u0 + v - 1)
                        for k in range((T2 - todo[v]["k0"]) // P):
                            mm = pe.transpose(acc[:, 2 + r, k * P:(k + 1) * P], PX[:, r, k * P:(k + 1) * P], ident[:])
                        mm.then_inc(pt_ready, 1)
                    if u >= 2:
                        v, w = u - 2, todo[u - 2]
                        pe.wait_ge(pt_copied, u0 + v + 1)
                        if v % per == 0 and v >= 2 * per:
                            pe.wait_ge(operand_ready, s["operand0"] + w["pair"] - 1)
                        nk = (T2 - w["k0"]) // P
                        for k in range(nk):
                            mm = pe.matmul(acc[w["po"]:w["po"] + 64, AUX0 + w["pair"] % 2, w["qt"] * P:(w["qt"] + 1) * P],
                                           w["v"](w["k0"] // P + k), PT[:, v % 2, k * P:(k + 1) * P],
                                           start=(k == 0), stop=(k == nk - 1))
                        mm.then_inc(o_ready, 1)

            def s5_stage(s):
                pe.wait_ge(evac, s["acc0"] + BANKS)
                half = CHUNKS // 2
                for c in range(DC):
                    if c >= 2:
                        pe.wait_ge(u_copied, c - 1)
                    for k in range(4):
                        mm = pe.transpose(acc[:, AUX0 + c % 2, k * P:(k + 1) * P], UT[:, c, k * P:(k + 1) * P], ident[:])
                    mm.then_inc(u_turned, 1)
                for b in range(8):
                    pe.wait_ge(uch_sorted, b + 1)
                    pe.wait_ge(u_copied, DC)
                    if b >= 2:
                        pe.wait_ge(ug_copied, b - 1)
                    for i in range(8):
                        g = 8 * b + i
                        mm = pe.transpose(acc[:, AUX0 + b % 2, i * CHUNKS:(i + 1) * CHUNKS],
                                          UGT[:, g].rearrange("p t c -> p (t c)"), ident[0:CHUNKS, 0:CHUNKS])
                    mm.then_inc(ug_turned, 1)
                pe.wait_ge(ug_copied, 8)

                def own_states(j):
                    pe.wait_ge(w_copied, j + 1)
                    if j >= 2:
                        pe.wait_ge(s_stored, j - 1)
                    for g2 in range(2):
                        for x in range(4):
                            mm = pe.matmul(acc[64 * g2:64 * g2 + 64, 2 + j % 2, x * CHUNKS:(x + 1) * CHUNKS],
                                           WT[:, j % 2, x, 64 * g2:64 * g2 + 64], UG[:, 2 * j + g2, :],
                                           start=True, stop=True)
                    mm.then_inc(s_summed, 1)

                for j in range(33):
                    if j < 32:
                        q = j // 8
                        pe.wait_ge(e_ready, 2 * q + 2)
                        if j >= 2:
                            pe.wait_ge(w_copied, j - 1)
                        for d in range(2):
                            for part in range(2):
                                x = 2 * d + part
                                mm = pe.transpose(acc[:, j % 2, x * P:(x + 1) * P], EE[q % 2][:, d, part, j % 8, :], ident[:])
                        mm.then_inc(w_turned, 1)
                    if j >= 1:
                        own_states(j - 1)

                def outputs(j):
                    q = j // 8
                    pe.wait_ge(d_ready, j + 1)
                    for g2 in range(2):
                        rows = slice(64 * g2, 64 * g2 + 64)
                        at = j % 8 * half
                        dst = acc[:, 2 + 2 * (q % 2) + g2, at:at + half]
                        pe.matmul(dst, DD[:, j % 2, g2, :], UG[:, 2 * j + g2, half:CHUNKS], start=True, stop=False)
                        for d in range(2):
                            order = slice(None, None, -1) if d else slice(None)
                            for part in range(2):
                                mm = pe.matmul(dst, EE[1][rows, d, part, j % 8, :], TT[rows, order, part, 32 * d + j],
                                               start=False, stop=(d == 1 and part == 1))
                    mm.then_inc(y_pair_done, 1)

                pe.wait_ge(scan_step, 5 * (CHUNKS - 1))
                for j in range(33):
                    if j < 32:
                        pe.wait_ge(f_ready, 4 * (j // 4) + 4)
                        if j >= 2:
                            pe.wait_ge(d_ready, j - 1)
                        for g2 in range(2):
                            rows = slice(64 * g2, 64 * g2 + 64)
                            for d in range(2):
                                for part in range(2):
                                    mm = pe.matmul(acc[:, (0, AUX0)[j % 2] + g2, d * P:(d + 1) * P],
                                                   EE[0][rows, d, part, j % 8, :], EE[1][rows, d, part, j % 8, :],
                                                   start=(part == 0), stop=(part == 1))
                        mm.then_inc(d_summed, 1)
                    if j >= 1:
                        if (j - 1) % 8 == 0 and j > 16:
                            pe.wait_ge(y_taken, 2 * ((j - 1) // 8 - 1))
                        outputs(j - 1)
                pe.wait_ge(g_done, 1)
                for b in range(16):
                    if b >= 2:
                        pe.wait_ge(yc_copied, b - 1)
                    for i in range(4):
                        mm = pe.transpose(acc[0:half, AUX0 + b % 2, i * P:(i + 1) * P], YG[:, 4 * b + i, :], ident[:])
                    mm.then_inc(yc_turned, 1)
                pe.wait_ge(ytok_loaded, 16)
                for c in range(DC):
                    if c >= 2:
                        pe.wait_ge(operand_ready, s["operand0"] + c - 1)
                    for k in range(2):
                        mm = pe.transpose(acc[:, c % 2, k * P:(k + 1) * P], YTOK[:, k, c * P:(c + 1) * P], ident[:])
                    mm.then_inc(y_turned, 1)

            pe.wait_ge(ones_set, 1)
            norm_stage(plan[0])
            for block in range(MODS_AT_START // 4):
                add_up_mods(block, 0, 8 * block, block)
            for s in plan:
                if s["kind"] == "s5":
                    s5_stage(s)
                if s["kind"] == "norm" and s is not plan[0]:
                    norm_stage(s)
                elif s["kind"] == "pair":
                    for i0, i1, mods, _blk in pair_runs(s):
                        with pe.Fori(i0, i1) as i:
                            pair_body(s, i, mods)
                elif s["kind"] == "down":
                    down_body(s, 0, True)
                    with pe.Fori(1, DC // 2) as i:
                        down_body(s, i, False)
                elif s["kind"] == "dense":
                    if s["dense"] in ("pw2", "o", "wout"):
                        dense_body(s, 0, range(4), True)
                        dense_body(s, 1, range(4))
                    else:
                        for i in range(s["outs"] // 4):
                            dense_body(s, i, range(4))
                        if s["outs"] % 4:
                            dense_body(s, s["outs"] // 4, range(s["outs"] % 4))
                elif s["kind"] == "attention":
                    if s["which"] == "na":
                        na_values(s)
                    else:
                        mix_projections(s)
                    softmax_stage(s)



def _tiles(w):
    k, m = w.shape
    return np.ascontiguousarray(
        w.reshape(k // P, P, m // P, P).transpose(2, 1, 0, 3).reshape(m // P, P, k))


def _columns(v):
    return v.reshape(-1, P).T


def _twice(v):
    return np.repeat(_columns(v), 2, axis=1)


def _features(x):
    return x.T.reshape(DC, P, -1).transpose(1, 0, 2)


def _rotation_tables():
    f = np.float32
    pos = np.arange(TOK)
    rot, turn = np.zeros((P, 4, TOK), f), np.zeros((P, 2, P), f)
    rot[:, 0] = 1
    for which, (width, starts) in enumerate(((32, (64,)), (64, (0, 64)))):
        axis = width // 2
        inv = f(10000.0) ** (-np.arange(0, axis, 2, dtype=f) / f(axis))
        angle = np.concatenate([(pos // 64).astype(f)[:, None] * inv, (pos % 64).astype(f)[:, None] * inv], axis=1)
        for at in starts:
            for half in range(2):
                rows = slice(at + half * axis, at + (half + 1) * axis)
                rot[rows, 2 * which], rot[rows, 2 * which + 1] = np.cos(angle).T, np.sin(angle).T
            for i in range(axis):
                turn[at + axis + i, which, at + i] = -1
                turn[at + i, which, at + axis + i] = 1
    band = np.where(np.abs(pos[:, None] - pos[None]) <= 128, f(0), f(-1e30)).reshape(2, P, TOK).transpose(1, 0, 2)
    return rot, turn, band


def _arrays(a):
    a = {k: np.asarray(v) for k, v in a.items()}
    out = {}
    out["x"] = np.concatenate([_features(a["x"][0]), _features(a["ctx"][0])], axis=2)
    out["ctx_2"] = _features(a["ctx_2"][0])
    out["ident"] = np.eye(P, dtype=np.float32)

    vecs = np.zeros((P, NVEC), np.float32)

    def put(name, cols):
        at, width = VEC[name]
        vecs[:, at:at + width] = cols

    put("mod_b", np.concatenate([_twice(a[n][l]) for n in ("mod_b", "mod_b_2") for l in range(2)], axis=1))
    for l in range(LAYERS):
        for s in range(3):
            put(f"g{l}{s}", _twice((a["norm_g"] if l < 2 else a["norm_pre_2"])[l % 2, s]))
            if l >= 2:
                put(f"gpost{l}{s}", _twice(a["norm_post_2"][l % 2, s]))
    put("c", np.stack([np.stack([_columns(a["c"][0]), _columns(a["c_ctx"])], axis=2),
                       np.stack([_columns(a["c_2"][0]), _columns(a["c_ctx_2"])], axis=2)], axis=1).reshape(P, -1))
    put("b_pw1", _columns(a["conv_b_pw1"][0]))
    put("w_dw", a["conv_w_dw"][0].reshape(TAPS, DC, P).transpose(2, 1, 0).reshape(P, -1))
    put("b_dw", _columns(a["conv_b_dw"][0]))
    put("ln_g", _columns(a["conv_ln_g"][0]))
    put("ln_b", _columns(a["conv_ln_b"][0]))
    put("b_pw2", _columns(a["conv_b_pw2"][0]))
    put("b_qkv", _columns(a["na_b_qkv"][0]))
    put("b_o", _columns(a["na_b_o"][0]))
    put("final_g", _columns(a["final_g"]))
    put("q_norm", _columns(a["mla_q_norm_2"][0]))
    put("kv_norm", _columns(a["mla_kv_norm_2"][0]))
    put("sink", np.broadcast_to(a["swa_sink_2"][0], (P, 8)))
    out["vecs"] = vecs

    out["mod_w"] = np.concatenate([a[n][l].reshape(4, 2, P, N_MOD * D // T2, T2).transpose(3, 0, 2, 1, 4).reshape(-1, P, TILE)
                                   for n in ("mod_w", "mod_w_2") for l in range(2)])
    for l in range(LAYERS):
        for h in range(2):
            if l < 2:
                gate, up, down = (a[n][l, h] for n in ("ffn_w_gate", "ffn_w_up", "ffn_w_down"))
            else:
                gate, up = a["ffn_w13_2"][l - 2, h, :, :F], a["ffn_w13_2"][l - 2, h, :, F:]
                down = a["ffn_w2_2"][l - 2, h]
            out[f"ffn_gate_{l}{h}"] = _tiles(gate)
            out[f"ffn_up_{l}{h}"] = _tiles(up)
            out[f"ffn_down_{l}{h}"] = _tiles(down)
    pw1 = a["conv_w_pw1"][0]
    out["pw1_a"], out["pw1_gate"] = _tiles(pw1[:, :D]), _tiles(pw1[:, D:])
    out["pw2"] = _tiles(a["conv_w_pw2"][0])
    out["qkv"] = _tiles(a["na_w_qkv"][0])
    out["o"] = _tiles(a["na_w_o"][0])

    w = a["attn_w_in_2"][0]
    at = np.cumsum([0, 256, 128, 32, 512, 128, 128])
    cq, ckv, kpe, qs, ks, vs = (w[:, at[i]:at[i + 1]] for i in range(6))
    pad = np.zeros((D, 64), np.float32)
    qs = qs.reshape(D, 2, 4, 64).transpose(0, 2, 1, 3).reshape(D, 512)
    out["win"] = _tiles(np.concatenate([cq, ckv, pad, kpe, pad[:, :32], qs, ks, vs], axis=1))
    out["wout"] = _tiles(a["attn_w_out_2"][0])
    out["w_uq"] = a["mla_w_uq_2"][0].reshape(2, P, 768).transpose(1, 0, 2)
    out["w_ukv"] = a["mla_w_ukv_2"][0].reshape(P, 8, 2, 64).transpose(0, 2, 1, 3).reshape(P, 1024)
    out["rot"], out["turn"], out["band"] = _rotation_tables()

    out["s5in"] = _tiles(a["s5_w_in_2"][0])
    glu = a["s5_w_glu_2"][0]
    out["glu_a"], out["glu_gate"] = _tiles(glu[:, :D]), _tiles(glu[:, D:])

    def states(v):
        v = v.reshape((2, GROUPS // 2, 2, 64) + v.shape[3:])
        return np.moveaxis(v, (2, 3), (0, 1)).reshape((P, COLS) + v.shape[4:])

    step = np.broadcast_to(a["s5_log_step_2"][0][:, :, None], (2, GROUPS, 64))
    out["s5_par"] = np.stack([states(a["s5_lambda_re_2"][0]), states(a["s5_lambda_im_2"][0]), states(step)], axis=1)
    out["s5_bc"] = np.stack([states(a["s5_b_re_2"][0]), states(a["s5_b_im_2"][0]),
                             states(a["s5_c_re_2"][0].transpose(0, 1, 3, 2)),
                             states(a["s5_c_im_2"][0].transpose(0, 1, 3, 2))], axis=1)
    out["s5_skip"] = np.tile(a["s5_d_2"][0].reshape(GROUPS, GROUP).T, (SUB, 1))
    token = np.arange(P) // GROUP
    out["s5_mask"] = np.stack([token[:, None] <= token[None], token[:, None] >= token[None]], axis=1).astype(np.float32)
    out["s5_zero"] = np.zeros((P, 12, COLS), np.float32)

    rows, cols, win = TOK // 64, 64, 16
    q, k = np.arange(TOK), np.arange(TOK)
    qr, qc, kr, kc = q[:, None] // cols, q[:, None] % cols, k[None] // cols, k[None] % cols
    start = np.clip(qc - win // 2, 0, cols - win)
    inside = (kc >= start) & (kc < start + win)
    rel = np.clip(kc - qc, -(win - 1), win - 1) + win - 1
    bias = a["na_rpb"][0][:, kr - qr + 7, rel]
    out["na_bias"] = np.where(inside[None], bias, np.float32(-1e30)).astype(np.float32).reshape(16, 2, P, TOK)
    return {k: np.ascontiguousarray(v) for k, v in out.items()}


def kernel(**inputs):
    import concourse.bacc as _bacc
    from concourse.bass_utils import run_bass_kernel_spmd as _run

    nc = _bacc.Bacc("TRN2", target_bir_lowering=False, num_devices=1)
    arrays = _arrays(inputs)
    io = {}
    for name, a in arrays.items():
        io[name] = nc.dram_tensor(f"in_{name}", a.shape, F32, kind="ExternalInput").ap()
    for kind in ("gate", "up", "down"):
        io[f"ffn_{kind}"] = [[io[f"ffn_{kind}_{l}{h}"] for h in range(2)] for l in range(LAYERS)]
    out = nc.dram_tensor("out_x", (P, DC, TOK), F32, kind="ExternalOutput").ap()
    build(nc, io, out)
    r = _run(nc, [{f"in_{k}": v for k, v in arrays.items()}], core_ids=[0])
    got = r.results[0]["out_x"]
    return np.ascontiguousarray(got.transpose(1, 0, 2).reshape(D, TOK).T)[None]
```
